# Optimizing a Trainium2 kernel written in Bass

```python
import jax, jax.numpy as jnp
from jax import lax
import numpy as np
import math

D_MODEL = 1024
BATCH = 1
SEQ = 512
DEPTH = 1

MEM_LEN = 256
MIX_WIDTH = D_MODEL
HGRN_WIDTH = MIX_WIDTH // 2
MLSTM_WIDTH = MIX_WIDTH - HGRN_WIDTH
HGRN_HEADS = 4
HGRN_HEAD_DIM = HGRN_WIDTH // HGRN_HEADS
MLSTM_HEADS = 4
MLSTM_HEAD_DIM = MLSTM_WIDTH // MLSTM_HEADS
CONV_WIDTH = 5
XATTN_HEADS = 4
XATTN_HEAD_DIM = D_MODEL // XATTN_HEADS
D_FF = 4 * D_MODEL
CHUNK = 64
NORM_EPS = 1e-6
MLSTM_FGATE_BIAS = 3.0
IN_SPLITS = (HGRN_WIDTH, HGRN_WIDTH, HGRN_WIDTH, HGRN_WIDTH, HGRN_WIDTH,
             MLSTM_WIDTH, MLSTM_WIDTH, MLSTM_WIDTH, MLSTM_WIDTH,
             MLSTM_HEADS, MLSTM_HEADS, MLSTM_HEADS, MLSTM_HEADS)
D_IN = 5 * HGRN_WIDTH + 4 * MLSTM_WIDTH + 4 * MLSTM_HEADS


def rmsnorm(x, g):
    x32 = x.astype(jnp.float32)
    y = x32 * lax.rsqrt(jnp.mean(x32 * x32, axis=-1, keepdims=True) + NORM_EPS)
    return (y * g.astype(jnp.float32)).astype(x.dtype)

def head_rmsnorm(h, g, n_heads):
    b, s, w = h.shape
    h32 = h.astype(jnp.float32).reshape(b, s, n_heads, w // n_heads)
    h32 = h32 * lax.rsqrt(jnp.mean(h32 * h32, axis=-1, keepdims=True) + NORM_EPS)
    return (h32.reshape(b, s, w) * g.astype(jnp.float32)).astype(h.dtype)

def split_cols(t, sizes):
    idx = np.cumsum(np.array(sizes))[:-1].tolist()
    return jnp.split(t, idx, axis=-1)

def to_heads(t, n_heads):
    b, s, w = t.shape
    return t.reshape(b, s, n_heads, w // n_heads).transpose(0, 2, 1, 3)

def from_heads(t):
    b, h, s, d = t.shape
    return t.transpose(0, 2, 1, 3).reshape(b, s, h * d)

def to_chunks(t):
    b, h, s = t.shape[:3]
    t = t.reshape(b, h, s // CHUNK, CHUNK, *t.shape[3:])
    return jnp.moveaxis(t, 2, 0)

def from_chunks(t):
    t = jnp.moveaxis(t, 0, 2)
    b, h, n, c = t.shape[:4]
    return t.reshape(b, h, n * c, *t.shape[4:])

def flip_seq(t):
    return jnp.flip(t, axis=2)

def hgrn2_scan(q, k, v, log_f):
    b, h, _, dk = q.shape
    dv = v.shape[-1]
    tril = jnp.tril(jnp.ones((CHUNK, CHUNK), dtype=bool))

    def step(state, xs):
        qc, kc, vc, lfc = xs
        cum = jnp.cumsum(lfc, axis=-2)
        o_inter = jnp.einsum('bhtd,bhde->bhte', qc * jnp.exp(cum), state)
        diff = cum[:, :, :, None, :] - cum[:, :, None, :, :]
        decay = jnp.exp(jnp.where(tril[:, :, None], diff, -jnp.inf))
        scores = jnp.einsum('bhtd,bhsd,bhtsd->bhts', qc, kc, decay)
        o_intra = jnp.einsum('bhts,bhse->bhte', scores, vc)
        cum_last = cum[:, :, -1:, :]
        k_dec = kc * jnp.exp(cum_last - cum)
        state = (jnp.exp(cum_last[:, :, 0, :])[..., None] * state
                 + jnp.einsum('bhsd,bhse->bhde', k_dec, vc))
        return state, o_inter + o_intra

    s0 = jnp.zeros((b, h, dk, dv), jnp.float32)
    xs = tuple(to_chunks(t.astype(jnp.float32)) for t in (q, k, v, log_f))
    _, o = lax.scan(step, s0, xs)
    return from_chunks(o)

def mlstm_scan(q, k, v, ig, log_fg):
    b, h, _, d = q.shape
    tril = jnp.tril(jnp.ones((CHUNK, CHUNK), dtype=bool))

    def step(carry, xs):
        c_st, n_st, m = carry
        qc, kc, vc, igc, lfc = xs
        cum = jnp.cumsum(lfc, axis=-1)
        log_d = cum[..., :, None] - cum[..., None, :] + igc[..., None, :]
        log_d = jnp.where(tril, log_d, -jnp.inf)
        log_inter = cum + m[..., None]
        m_t = jnp.maximum(jnp.max(log_d, axis=-1), log_inter)
        d_mat = jnp.exp(log_d - m_t[..., None])
        w_inter = jnp.exp(log_inter - m_t)
        scores = jnp.einsum('bhtd,bhsd->bhts', qc, kc) * d_mat
        num = (jnp.einsum('bhts,bhse->bhte', scores, vc)
               + w_inter[..., None] * jnp.einsum('bhtd,bhde->bhte', qc, c_st))
        den = jnp.sum(scores, axis=-1) + w_inter * jnp.einsum('bhtd,bhd->bht', qc, n_st)
        h_out = num / jnp.maximum(jnp.abs(den), jnp.exp(-m_t))[..., None]
        cum_last = cum[..., -1]
        log_w = cum_last[..., None] - cum + igc
        m_new = jnp.maximum(cum_last + m, jnp.max(log_w, axis=-1))
        carry_w = jnp.exp(cum_last + m - m_new)
        k_w = kc * jnp.exp(log_w - m_new[..., None])[..., None]
        c_st = carry_w[..., None, None] * c_st + jnp.einsum('bhsd,bhse->bhde', k_w, vc)
        n_st = carry_w[..., None] * n_st + jnp.sum(k_w, axis=-2)
        return (c_st, n_st, m_new), h_out

    init = (jnp.zeros((b, h, d, d), jnp.float32),
            jnp.zeros((b, h, d), jnp.float32),
            jnp.zeros((b, h), jnp.float32))
    xs = tuple(to_chunks(t.astype(jnp.float32)) for t in (q, k, v, ig, log_fg))
    _, hs = lax.scan(step, init, xs)
    return from_chunks(hs)

def layer_lower_bounds(logits):
    p = jax.nn.softmax(logits.astype(jnp.float32), axis=1)
    c = jnp.cumsum(p, axis=1)
    return c - c[:, :1]

def lower_bounded_log_forget(z, lb):
    z = z.astype(jnp.float32)
    return jnp.logaddexp(jnp.log(lb), jnp.log1p(-lb) + jax.nn.log_sigmoid(z))

def centred_dwconv(x, w, b):
    y = lax.conv_general_dilated(
        x, w[:, None, :], window_strides=(1,),
        padding=[(CONV_WIDTH // 2, CONV_WIDTH // 2)],
        dimension_numbers=('NWC', 'WIO', 'NWC'),
        feature_group_count=x.shape[-1])
    return y + b

def token_mixer(xn, w_in, b_in, lb_fwd, lb_bwd, conv_w, conv_b, hgrn_g, mlstm_g, w_out):
    proj = xn @ w_in + b_in
    (h_q, h_f_fwd, h_f_bwd, h_i, h_g,
     m_q, m_k, m_v, m_o,
     m_ig_fwd, m_ig_bwd, m_fg_fwd, m_fg_bwd) = split_cols(proj, IN_SPLITS)

    q_h = to_heads(jax.nn.silu(h_q), HGRN_HEADS)
    v_h = to_heads(h_i, HGRN_HEADS)
    lf_fwd = to_heads(lower_bounded_log_forget(h_f_fwd, lb_fwd), HGRN_HEADS)
    lf_bwd = to_heads(lower_bounded_log_forget(h_f_bwd, lb_bwd), HGRN_HEADS)
    k_fwd = -jnp.expm1(lf_fwd)
    k_bwd = -jnp.expm1(lf_bwd)
    o_h = (hgrn2_scan(q_h, k_fwd, v_h, lf_fwd)
           + flip_seq(hgrn2_scan(flip_seq(q_h), flip_seq(k_bwd), flip_seq(v_h), flip_seq(lf_bwd))))
    hgrn_out = head_rmsnorm(from_heads(o_h).astype(xn.dtype), hgrn_g, HGRN_HEADS) * jax.nn.silu(h_g)

    qk = jax.nn.silu(centred_dwconv(jnp.concatenate([m_q, m_k], axis=-1), conv_w, conv_b))
    m_q, m_k = jnp.split(qk, 2, axis=-1)
    q_m = to_heads(m_q, MLSTM_HEADS)
    k_m = to_heads(m_k, MLSTM_HEADS) * (MLSTM_HEAD_DIM ** -0.5)
    v_m = to_heads(m_v, MLSTM_HEADS)
    ig_fwd = jnp.swapaxes(m_ig_fwd, 1, 2).astype(jnp.float32)
    ig_bwd = jnp.swapaxes(m_ig_bwd, 1, 2).astype(jnp.float32)
    lfg_fwd = jax.nn.log_sigmoid(jnp.swapaxes(m_fg_fwd, 1, 2).astype(jnp.float32))
    lfg_bwd = jax.nn.log_sigmoid(jnp.swapaxes(m_fg_bwd, 1, 2).astype(jnp.float32))
    h_m = (mlstm_scan(q_m, k_m, v_m, ig_fwd, lfg_fwd)
           + flip_seq(mlstm_scan(flip_seq(q_m), flip_seq(k_m), flip_seq(v_m),
                                 flip_seq(ig_bwd), flip_seq(lfg_bwd))))
    mlstm_out = head_rmsnorm(from_heads(h_m).astype(xn.dtype), mlstm_g, MLSTM_HEADS) * jax.nn.sigmoid(m_o)

    return jnp.concatenate([hgrn_out, mlstm_out], axis=-1) @ w_out

def cross_attention(xn, memn, w_q, w_kv, w_o):
    b, s, _ = xn.shape
    q = (xn @ w_q).reshape(b, s, XATTN_HEADS, XATTN_HEAD_DIM)
    k, v = jnp.split(memn @ w_kv, 2, axis=-1)
    k = k.reshape(b, -1, XATTN_HEADS, XATTN_HEAD_DIM)
    v = v.reshape(b, -1, XATTN_HEADS, XATTN_HEAD_DIM)
    scores = jnp.einsum('bqhd,bkhd->bhqk', q, k).astype(jnp.float32) * (XATTN_HEAD_DIM ** -0.5)
    p = jax.nn.softmax(scores, axis=-1).astype(v.dtype)
    o = jnp.einsum('bhqk,bkhd->bqhd', p, v).reshape(b, s, D_MODEL)
    return o @ w_o

def squared_relu_mlp(xn, w_up, w_down):
    return jnp.square(jax.nn.relu(xn @ w_up)) @ w_down

def first_inputs(seed: int = 0) -> dict:
    key = jax.random.key(seed)
    ks = jax.random.split(key, 20)

    def nrm(k, shape, scale):
        return jax.random.normal(k, shape, jnp.float32) * scale

    def gain(k, shape):
        return 1.0 + 0.05 * jax.random.normal(k, shape, jnp.float32)

    fgate_offset = jnp.concatenate([jnp.zeros((D_IN - 2 * MLSTM_HEADS,), jnp.float32),
                                    jnp.full((2 * MLSTM_HEADS,), MLSTM_FGATE_BIAS, jnp.float32)])
    return {
        "x": nrm(ks[0], (BATCH, SEQ, D_MODEL), 1.0),
        "mem": nrm(ks[1], (BATCH, MEM_LEN, D_MODEL), 1.0),
        "norm_mix": gain(ks[2], (DEPTH, D_MODEL)),
        "norm_xattn": gain(ks[3], (DEPTH, D_MODEL)),
        "norm_mem": gain(ks[4], (DEPTH, D_MODEL)),
        "norm_mlp": gain(ks[5], (DEPTH, D_MODEL)),
        "norm_final": gain(ks[6], (D_MODEL,)),
        "w_in": nrm(ks[7], (DEPTH, D_MODEL, D_IN), D_MODEL ** -0.5),
        "b_in": nrm(ks[8], (DEPTH, D_IN), 0.02) + fgate_offset,
        "hgrn_lb_logits": nrm(ks[9], (2, DEPTH, HGRN_WIDTH), 0.5),
        "hgrn_norm": gain(ks[10], (DEPTH, HGRN_WIDTH)),
        "mlstm_conv_w": nrm(ks[11], (DEPTH, CONV_WIDTH, 2 * MLSTM_WIDTH), CONV_WIDTH ** -0.5),
        "mlstm_conv_b": nrm(ks[12], (DEPTH, 2 * MLSTM_WIDTH), 0.02),
        "mlstm_norm": gain(ks[13], (DEPTH, MLSTM_WIDTH)),
        "w_out": nrm(ks[14], (DEPTH, MIX_WIDTH, D_MODEL), MIX_WIDTH ** -0.5),
        "w_xq": nrm(ks[15], (DEPTH, D_MODEL, D_MODEL), D_MODEL ** -0.5),
        "w_xkv": nrm(ks[16], (DEPTH, D_MODEL, 2 * D_MODEL), D_MODEL ** -0.5),
        "w_xo": nrm(ks[17], (DEPTH, D_MODEL, D_MODEL), D_MODEL ** -0.5),
        "w_up": nrm(ks[18], (DEPTH, D_MODEL, D_FF), D_MODEL ** -0.5),
        "w_down": nrm(ks[19], (DEPTH, D_FF, D_MODEL), D_FF ** -0.5),
    }

def first_block(x, mem, norm_mix, norm_xattn, norm_mem, norm_mlp, norm_final, w_in, b_in,
              hgrn_lb_logits, hgrn_norm, mlstm_conv_w, mlstm_conv_b, mlstm_norm, w_out,
              w_xq, w_xkv, w_xo, w_up, w_down):
    lb = layer_lower_bounds(hgrn_lb_logits)
    for l in range(DEPTH):
        x = x + token_mixer(rmsnorm(x, norm_mix[l]), w_in[l], b_in[l], lb[0, l], lb[1, l],
                            mlstm_conv_w[l], mlstm_conv_b[l], hgrn_norm[l], mlstm_norm[l], w_out[l])
        x = x + cross_attention(rmsnorm(x, norm_xattn[l]), rmsnorm(mem, norm_mem[l]),
                                w_xq[l], w_xkv[l], w_xo[l])
        x = x + squared_relu_mlp(rmsnorm(x, norm_mlp[l]), w_up[l], w_down[l])
    return rmsnorm(x, norm_final)


ATT_HEADS = 8
ATT_KV_HEADS = 2
ATT_HEAD_DIM = 64
ATT_GROUP = ATT_HEADS // ATT_KV_HEADS
ATT_Q_DIM = ATT_HEADS * ATT_HEAD_DIM
ATT_KV_DIM = ATT_KV_HEADS * ATT_HEAD_DIM
WINDOW = 128
ATT_BLOCK = 128
ROPE_DIM = ATT_HEAD_DIM // 4
ROPE_THETA = 500000.0

GLA_HEADS = 4
GLA_KEY_DIM = D_MODEL // 2
GLA_VAL_DIM = D_MODEL
GLA_DK = GLA_KEY_DIM // GLA_HEADS
GLA_DV = GLA_VAL_DIM // GLA_HEADS
GLA_GATE_RANK = 16
GLA_GATE_NORM = 16.0
GLA_CHUNK = 64

N_EXPERTS = 16
EXPERT_FF = D_MODEL
CAPACITY_FACTOR = 2

PLE_DIM = 256

EPS = 1e-6

IN_SIZES = (ATT_Q_DIM, ATT_KV_DIM, ATT_KV_DIM,
            GLA_KEY_DIM, GLA_KEY_DIM, GLA_VAL_DIM, GLA_VAL_DIM,
            GLA_GATE_RANK, GLA_GATE_RANK, D_MODEL, D_MODEL)
IN_DIM = ATT_Q_DIM + 2 * ATT_KV_DIM + 2 * GLA_KEY_DIM + 2 * GLA_VAL_DIM + 2 * GLA_GATE_RANK + 2 * D_MODEL


def rmsnorm_2(x, g):
    xf = x.astype(jnp.float32)
    y = xf * lax.rsqrt(jnp.mean(xf * xf, axis=-1, keepdims=True) + EPS)
    return (y * g.astype(jnp.float32)).astype(x.dtype)

def split_columns(proj):
    parts, start = [], 0
    for size in IN_SIZES:
        parts.append(proj[..., start:start + size])
        start += size
    return parts

def partial_rope(t, positions):
    half = ROPE_DIM // 2
    inv_freq = ROPE_THETA ** (-jnp.arange(0, ROPE_DIM, 2, dtype=jnp.float32) / ROPE_DIM)
    ang = positions.astype(jnp.float32)[..., None] * inv_freq
    cos = jnp.cos(ang)[:, :, None, :].astype(t.dtype)
    sin = jnp.sin(ang)[:, :, None, :].astype(t.dtype)
    t1 = t[..., :half]
    t2 = t[..., half:ROPE_DIM]
    rot = jnp.concatenate([t1 * cos - t2 * sin, t2 * cos + t1 * sin], axis=-1)
    return jnp.concatenate([rot, t[..., ROPE_DIM:]], axis=-1)

def windowed_gqa(q, k, v, sink):
    B, S = q.shape[0], q.shape[1]
    nb = S // ATT_BLOCK
    qb = q.reshape(B, nb, ATT_BLOCK, ATT_KV_HEADS, ATT_GROUP, ATT_HEAD_DIM)

    def band(t):
        tp = jnp.pad(t, ((0, 0), (ATT_BLOCK, ATT_BLOCK), (0, 0), (0, 0)))
        tp = tp.reshape(B, nb + 2, ATT_BLOCK, ATT_KV_HEADS, ATT_HEAD_DIM)
        return jnp.concatenate([tp[:, :-2], tp[:, 1:-1], tp[:, 2:]], axis=2)

    kb, vb = band(k), band(v)
    scores = jnp.einsum('bnqhgd,bnkhd->bnhgqk', qb, kb).astype(jnp.float32) * (ATT_HEAD_DIM ** -0.5)
    blk = jnp.arange(nb)[:, None, None]
    qi = blk * ATT_BLOCK + jnp.arange(ATT_BLOCK)[None, :, None]
    kj = (blk - 1) * ATT_BLOCK + jnp.arange(3 * ATT_BLOCK)[None, None, :]
    valid = (jnp.abs(qi - kj) <= WINDOW) & (kj >= 0) & (kj < S)
    scores = jnp.where(valid[None, :, None, None], scores, -jnp.inf)
    sink_b = sink.astype(jnp.float32).reshape(1, 1, ATT_KV_HEADS, ATT_GROUP, 1, 1)
    m = jnp.maximum(jnp.max(scores, axis=-1, keepdims=True), sink_b)
    e = jnp.exp(scores - m)
    probs = e / (jnp.sum(e, axis=-1, keepdims=True) + jnp.exp(sink_b - m))
    out = jnp.einsum('bnhgqk,bnkhd->bnqhgd', probs.astype(v.dtype), vb)
    return out.reshape(B, S, ATT_Q_DIM)

def gla_chunked(q, k, v, log_a, strict):
    B, S, H, dk = q.shape
    dv = v.shape[-1]
    nc = S // GLA_CHUNK

    def chunk(t):
        return t.reshape(B, nc, GLA_CHUNK, H, t.shape[-1])

    qc, kc, vc, ac = chunk(q), chunk(k), chunk(v), chunk(log_a)
    b = jnp.cumsum(ac, axis=2)
    g = b[:, :, -1]
    q_t = qc * jnp.exp(b)
    k_t = kc * jnp.exp(-b)
    k_end = kc * jnp.exp(g[:, :, None] - b)
    attn = jnp.einsum('bclhd,bcmhd->bchlm', q_t, k_t)
    mask = jnp.tril(jnp.ones((GLA_CHUNK, GLA_CHUNK), dtype=bool), -1 if strict else 0)
    attn = jnp.where(mask, attn, 0.0)
    o_intra = jnp.einsum('bchlm,bcmhe->bclhe', attn, vc)
    kv = jnp.einsum('bclhd,bclhe->bchde', k_end, vc)
    decay = jnp.exp(g)

    def step(state, xs):
        dec, kv_c = xs
        return dec[..., None] * state + kv_c, state

    s0 = jnp.zeros((B, H, dk, dv), dtype=jnp.float32)
    _, s_prev = lax.scan(step, s0, (jnp.moveaxis(decay, 1, 0), jnp.moveaxis(kv, 1, 0)))
    s_prev = jnp.moveaxis(s_prev, 0, 1)
    o_inter = jnp.einsum('bclhd,bchde->bclhe', q_t, s_prev)
    return (o_intra + o_inter).reshape(B, S, H, dv)

def gla_branch(gq, gk, gv, gr, z_f, z_b, up_f, bias_f, up_b, bias_b, norm_gain):
    B, S = gq.shape[0], gq.shape[1]
    f32 = jnp.float32
    q = gq.astype(f32).reshape(B, S, GLA_HEADS, GLA_DK) * (GLA_DK ** -0.5)
    k = gk.astype(f32).reshape(B, S, GLA_HEADS, GLA_DK)
    v = gv.astype(f32).reshape(B, S, GLA_HEADS, GLA_DV)
    la_f = (jax.nn.log_sigmoid(z_f.astype(f32) @ up_f.astype(f32) + bias_f.astype(f32)) / GLA_GATE_NORM).reshape(B, S, GLA_HEADS, GLA_DK)
    la_b = (jax.nn.log_sigmoid(z_b.astype(f32) @ up_b.astype(f32) + bias_b.astype(f32)) / GLA_GATE_NORM).reshape(B, S, GLA_HEADS, GLA_DK)
    o_f = gla_chunked(q, k, v, la_f, strict=False)
    flip = lambda t: jnp.flip(t, axis=1)
    o_b = flip(gla_chunked(flip(q), flip(k), flip(v), flip(la_b), strict=True))
    o = o_f + o_b
    o = o * lax.rsqrt(jnp.mean(o * o, axis=-1, keepdims=True) + EPS) * norm_gain.astype(f32).reshape(GLA_HEADS, GLA_DV)
    o = o.reshape(B, S, GLA_VAL_DIM) * jax.nn.silu(gr.astype(f32))
    return o.astype(gq.dtype)

def expert_choice_ffn(xn, w_router, w_gate, w_up, w_down):
    B, S, D = xn.shape
    cap = CAPACITY_FACTOR * S // N_EXPERTS
    aff = jax.nn.softmax(jnp.einsum('bsd,de->bse', xn, w_router).astype(jnp.float32), axis=-1)
    top_aff, top_idx = lax.top_k(jnp.swapaxes(aff, 1, 2), cap)
    bidx = jnp.arange(B)[:, None, None]
    xg = xn[bidx, top_idx]
    hid = jax.nn.silu(jnp.einsum('becd,edf->becf', xg, w_gate)) * jnp.einsum('becd,edf->becf', xg, w_up)
    y = jnp.einsum('becf,efd->becd', hid, w_down) * top_aff[..., None].astype(xn.dtype)
    return jnp.zeros((B, S, D), dtype=y.dtype).at[bidx, top_idx].add(y)

def second_inputs(seed: int = 0) -> dict:
    key = jax.random.key(seed)
    ks = jax.random.split(key, 32)
    f32 = jnp.float32
    L, D = DEPTH, D_MODEL

    def w(k, shape, fan_in):
        return jax.random.normal(k, shape, f32) * (fan_in ** -0.5)

    def gain(k, shape):
        return 1.0 + 0.1 * jax.random.normal(k, shape, f32)

    x = jax.random.normal(ks[0], (BATCH, SEQ, D), f32)
    p = jax.random.normal(ks[1], (L, BATCH, SEQ, PLE_DIM), f32)
    offsets = jax.random.randint(ks[2], (BATCH, 1), 0, 1024, dtype=jnp.int32)
    positions = jnp.arange(SEQ, dtype=jnp.int32)[None, :] + offsets
    return {
        "x": x,
        "p": p,
        "positions": positions,
        "norm_mix": gain(ks[3], (L, D)),
        "w_in": w(ks[4], (L, D, IN_DIM), D),
        "gla_gate_up_fwd": w(ks[5], (L, GLA_GATE_RANK, GLA_KEY_DIM), GLA_GATE_RANK),
        "gla_gate_bias_fwd": 1.0 + 0.5 * jax.random.normal(ks[6], (L, GLA_KEY_DIM), f32),
        "gla_gate_up_bwd": w(ks[7], (L, GLA_GATE_RANK, GLA_KEY_DIM), GLA_GATE_RANK),
        "gla_gate_bias_bwd": 1.0 + 0.5 * jax.random.normal(ks[8], (L, GLA_KEY_DIM), f32),
        "attn_sink": 0.5 * jax.random.normal(ks[9], (L, ATT_HEADS), f32),
        "gla_norm": gain(ks[10], (L, GLA_VAL_DIM)),
        "w_branch_attn": w(ks[11], (L, ATT_Q_DIM, D), ATT_Q_DIM),
        "w_branch_gla": w(ks[12], (L, GLA_VAL_DIM, D), GLA_VAL_DIM),
        "w_out": w(ks[13], (L, D, D), D),
        "norm_ffn": gain(ks[14], (L, D)),
        "w_router": w(ks[15], (L, D, N_EXPERTS), D),
        "w_exp_gate": w(ks[16], (L, N_EXPERTS, D, EXPERT_FF), D),
        "w_exp_up": w(ks[17], (L, N_EXPERTS, D, EXPERT_FF), D),
        "w_exp_down": w(ks[18], (L, N_EXPERTS, EXPERT_FF, D), EXPERT_FF),
        "norm_ple": gain(ks[19], (L, D)),
        "w_ple_gate": w(ks[20], (L, D, D), D),
        "w_ple": w(ks[21], (L, PLE_DIM, D), PLE_DIM),
        "norm_final": gain(ks[22], (D,)),
    }

def second_block(x, p, positions, norm_mix, w_in, gla_gate_up_fwd, gla_gate_bias_fwd,
              gla_gate_up_bwd, gla_gate_bias_bwd, attn_sink, gla_norm, w_branch_attn,
              w_branch_gla, w_out, norm_ffn, w_router, w_exp_gate, w_exp_up, w_exp_down,
              norm_ple, w_ple_gate, w_ple, norm_final):
    B, S, _ = x.shape
    h = x
    for l in range(DEPTH):
        a = rmsnorm_2(h, norm_mix[l])
        proj = a @ w_in[l]
        aq, ak, av, gq, gk, gv, gr, z_f, z_b, g_att, g_gla = split_columns(proj)
        aq = partial_rope(aq.reshape(B, S, ATT_HEADS, ATT_HEAD_DIM), positions)
        ak = partial_rope(ak.reshape(B, S, ATT_KV_HEADS, ATT_HEAD_DIM), positions)
        av = av.reshape(B, S, ATT_KV_HEADS, ATT_HEAD_DIM)
        y_att = windowed_gqa(aq, ak, av, attn_sink[l]) @ w_branch_attn[l]
        y_gla = gla_branch(gq, gk, gv, gr, z_f, z_b,
                           gla_gate_up_fwd[l], gla_gate_bias_fwd[l],
                           gla_gate_up_bwd[l], gla_gate_bias_bwd[l], gla_norm[l]) @ w_branch_gla[l]
        merged = jax.nn.sigmoid(g_att) * y_att + jax.nn.sigmoid(g_gla) * y_gla
        h = h + merged @ w_out[l]
        h = h + expert_choice_ffn(rmsnorm_2(h, norm_ffn[l]), w_router[l],
                                  w_exp_gate[l], w_exp_up[l], w_exp_down[l])
        ple_gate = jax.nn.sigmoid(rmsnorm_2(h, norm_ple[l]) @ w_ple_gate[l])
        h = h + ple_gate * (p[l] @ w_ple[l])
    return rmsnorm_2(h, norm_final)


def setup_inputs(seed=0):
    out = dict(first_inputs(seed))
    for name, value in second_inputs(seed + 1).items():
        if name != "x":
            out[name + "_2"] = value
    return out


def reference(
    x, mem, norm_mix, norm_xattn, norm_mem, norm_mlp, norm_final, w_in, b_in, hgrn_lb_logits,
    hgrn_norm, mlstm_conv_w, mlstm_conv_b, mlstm_norm, w_out, w_xq, w_xkv, w_xo, w_up, w_down,
    p_2, positions_2, norm_mix_2, w_in_2, gla_gate_up_fwd_2, gla_gate_bias_fwd_2,
    gla_gate_up_bwd_2, gla_gate_bias_bwd_2, attn_sink_2, gla_norm_2, w_branch_attn_2,
    w_branch_gla_2, w_out_2, norm_ffn_2, w_router_2, w_exp_gate_2, w_exp_up_2, w_exp_down_2,
    norm_ple_2, w_ple_gate_2, w_ple_2, norm_final_2,
):
    x = first_block(
        x, mem, norm_mix, norm_xattn, norm_mem, norm_mlp, norm_final, w_in, b_in,
        hgrn_lb_logits, hgrn_norm, mlstm_conv_w, mlstm_conv_b, mlstm_norm, w_out, w_xq, w_xkv,
        w_xo, w_up, w_down,
    )
    return second_block(
        x, p_2, positions_2, norm_mix_2, w_in_2, gla_gate_up_fwd_2, gla_gate_bias_fwd_2,
        gla_gate_up_bwd_2, gla_gate_bias_bwd_2, attn_sink_2, gla_norm_2, w_branch_attn_2,
        w_branch_gla_2, w_out_2, norm_ffn_2, w_router_2, w_exp_gate_2, w_exp_up_2, w_exp_down_2,
        norm_ple_2, w_ple_gate_2, w_ple_2, norm_final_2,
    )


_drawn_inputs = setup_inputs


def setup_inputs(seed=0):
    import zlib

    import numpy as np

    out = dict(_drawn_inputs(seed))
    spreads = {}
    factors = {'norm_xattn': 7.923,
     'norm_mem': 4.104,
     'mlstm_conv_b': 5.558,
     'attn_sink_2': 57.519,
     'norm_ple_2': 3.007}
    for name, (base, spread) in spreads.items():
        noise = np.random.default_rng([zlib.crc32(name.encode()), seed]).standard_normal(out[name].shape)
        drawn = base * np.exp(spread * noise) if base else spread * noise
        out[name] = __import__('jax').numpy.asarray(drawn.astype(out[name].dtype))
    for name, factor in factors.items():
        out[name] = (out[name] * factor).astype(out[name].dtype)
    return out
```

```python
import numpy as np

import concourse.bass as bass
from concourse import mybir

ACT = mybir.ActivationFunctionType
ALU = mybir.AluOpType
AX = mybir.AxisListType
F32 = mybir.dt.float32
F32R = mybir.dt.float32r
I32 = mybir.dt.int32

P = 128
S = 512
KT = 8
BASE = 16512
TOP = 229344
SLOT = 2048
NRAW = 3
NSPL = 3
BIG = 1.0e30
EPS = 1e-6
TWO_PI = (6.28125, 0.0019350051879882812, float(2 * np.pi - 6.28125 - 0.0019350051879882812))



def _cols(start, n=128):
    return list(range(start, start + n))


def unit_plan():
    plan = []
    q, ff, fb, hi, hg, mq, mk, mv, mo, gt = 0, 512, 1024, 1536, 2048, 2560, 3072, 3584, 4096, 4608
    head = lambda o, h: ("f", "w_in", 0, _cols(o + 128 * h))
    tm = lambda w, c: [("t", w, 2 * u, _cols(c, 512)) for u in range(4)]
    g = [-1] * 128
    for i in range(4):
        g[i], g[64 + i], g[32 + i], g[96 + i] = gt + i, gt + 4 + i, gt + 8 + i, gt + 12 + i
    hin = lambda h: [head(q, h), head(ff, h), head(fb, h)]
    plan += hin(0) + tm("w_in", hi) + hin(1) + [head(hg, 0), ("f", "w_in", 0, g), head(hg, 1)]
    plan += hin(2) + [head(hg, 2), head(mo, 0), head(mo, 1)] + hin(3) + [head(hg, 3), head(mo, 2), head(mo, 3)]
    plan += tm("w_in", mv)
    for h in range(4):
        plan += [head(mq, h), head(mk, h)]
    fm = lambda w, c, k0=0: ("f", w, k0, _cols(128 * c))
    plan += [fm("w_xkv", c) for c in range(8)]
    for c in (1024, 1536):
        plan += tm("w_xkv", c)
    plan += [fm("w_out", c) for c in range(8)]
    plan += [fm("w_xq", c) for c in range(8)]
    plan += [fm("w_xo", c) for c in range(8)]
    for r in range(4):
        plan += [fm("w_up", 8 * r + c) for c in range(8)]
        plan += [fm("w_down", c, 8 * r) for c in range(8)]
    gla_gates = list(range(3840, 3856)) + [-1] * 16 + list(range(3856, 3872)) + [-1] * 80
    plan += [("f", "w_in_2", 0, gla_gates)]
    f2 = lambda o, n: [("f", "w_in_2", 0, _cols(o + 128 * i)) for i in range(n)]
    gin = lambda h: f2(768 + 128 * h, 1) + f2(1280 + 128 * h, 1)
    gr = lambda h: f2(2816 + 256 * h, 2)
    plan += gin(0) + tm("w_in_2", 1792) + gr(0) + gin(1) + gr(1) + tm("w_in_2", 2304) + gin(2) + gr(2) + gin(3) + gr(3)
    plan += f2(512, 1)
    plan += [("f", "w_in_2", 0, _cols(64 * j, 64) + _cols(64 * (4 + j), 64)) for j in range(4)]
    plan += f2(640, 1) + f2(3872, 8) + f2(4896, 8)
    plan += [("h", "w_branch_attn_2", 0, _cols(256 * c, 256)) for c in range(4)]
    plan += [fm("w_branch_gla_2", c) for c in range(8)]
    plan += [fm("w_out_2", c) for c in range(8)]
    plan += [("w", "w_ple_2", 0, _cols(512 * c, 512)) for c in range(2)]
    plan += [fm("w_ple_gate_2", c) for c in range(8)]
    return plan


TAIL = 10


def const_columns():
    p, c = np.arange(P)[:, None], np.arange(P)[None, :]
    f = lambda m: m.astype(np.float32)
    parts = {"ident": f(p == c), "ones": np.ones((P, P), np.float32)}
    for lv in range(7):
        parts[f"lev{lv}"] = f(((p >> lv) ^ (c >> lv)) == 1)
    parts["hi"] = f(p > c) * np.float32(BIG)
    parts["none"] = np.zeros((P, P), np.float32)
    parts["lo"] = f(p < c) * np.float32(BIG)
    parts["le"] = f(p <= c)
    parts["ge"] = f(p >= c)
    cf = f(p <= c) - f(p <= 63)
    cf[:, 63] = np.arange(P) <= 63
    cb = f(p >= c) - f(p >= 64)
    cb[:, 64] = np.arange(P) >= 64
    parts["cf"], parts["cb"] = cf / np.float32(16), cb / np.float32(16)
    rot = np.zeros((P, P), np.float32)
    for o in (0, 64):
        for i in range(8):
            rot[o + i + 8, o + i], rot[o + i, o + i + 8] = -1, 1
    parts["rot"] = rot
    parts["slots"] = np.broadcast_to(np.arange(1, 65, dtype=np.float32), (P, 64))
    return parts


def const_index():
    at, n = {}, 0
    for k, v in const_columns().items():
        at[k] = n
        n += v.shape[1]
    return at, n


VECS = [("norm_mix", 8), ("norm_xattn", 8), ("norm_mem", 8), ("norm_mlp", 8), ("norm_final", 8),
        ("b_q", 4), ("b_ff", 4), ("b_fb", 4), ("b_hg", 4), ("b_mq", 4), ("b_mk", 4), ("b_mo", 4), ("b_gt", 1),
        ("lb", 8), ("hgrn_norm", 4), ("conv_w", 40), ("conv_b", 8), ("mlstm_norm", 4), ("eps", 1),
        ("norm_mix_2", 8), ("gla_norm_2", 8), ("norm_ffn_2", 8), ("norm_ple_2", 8), ("norm_final_2", 8), ("sink", 8),
        ("freq", 1), ("halfpi", 1), ("slot", 1)]


def vec_index():
    at, n = {}, 0
    for k, w in VECS:
        at[k] = n
        n += w
    return at, n



def flat(x):
    if x is None:
        return []
    if isinstance(x, tuple) and len(x) == 2 and isinstance(x[1], int):
        return [x]
    return [t for y in x for t in flat(y)]


class Lane:

    def __init__(self, nc, name):
        self.nc, self.name, self.ops, self.n, self.k, self.sem = nc, name, [], 0, 0, None

    def do(self, fn, *waits):
        if self.sem is None or self.n == 4000:
            self.sem, self.n, self.k = self.nc.alloc_semaphore(f"{self.name}{self.k}"), 0, self.k + 1
        self.n += 1
        self.ops.append((fn, flat(waits), self.sem, 1))
        return (self.sem, self.n)

    def quiet(self, fn, *waits):
        self.ops.append((fn, flat(waits), None, 0))

    def dma(self, ch, fn, *waits):
        ch.n += 16
        self.ops.append((fn, flat(waits), ch.sem, 16))
        return (ch.sem, ch.n)

    def wait(self, *waits):
        self.ops.append((None, flat(waits), None, 0))

    def play(self, e):
        seen = {}
        for fn, waits, sem, inc in self.ops:
            for s, v in waits:
                if v > seen.get(s.num, 0):
                    e.wait_ge(s, v)
                    seen[s.num] = v
            if fn is not None:
                ins = fn(e)
                if sem is not None:
                    ins.then_inc(sem, inc)


class Channel:

    def __init__(self, nc, name):
        self.sem, self.n = nc.alloc_semaphore(name), 0


def weave(*gens):
    live = [list(x) for x in gens]
    while live:
        for item in list(live):
            for _ in range(item[1]):
                try:
                    next(item[0])
                except StopIteration:
                    live.remove(item)
                    break


def drain(g):
    for _ in g:
        pass



TILES = {
    "y_h": [(24 + 2 * h, 25 + 2 * h) for h in range(4)],
    "v_h": [32, 33, 34, 35], "hg": [36, 37, 38, 39], "mo": [40, 41, 42, 43],
    "hin": [[48, 49, 50, 51, 52], [53, 54, 55, 56, 57]],
    "qf": 58, "kc": 59, "qc": 60, "t2": [61, 62], "diag": 63, "yh": 64,
    "gates": [44, 45, 46, 47, 65],
    "q": [48, 50, 53, 55], "k": [49, 51, 54, 56], "conv": [62, 63],
    "mb": [32, 33], "md": [34, 35], "pt": [36, 37, 38, 39, 58], "hn": 59, "junk": 60, "ym": 61,
    "y_m": [(48, 49), (50, 51), (53, 54), (55, 56)],
    "mem": [16, 17, 18, 19], "memn": [8, 9, 10, 11, 12, 13, 14, 15], "kx": [44, 45, 52, 57], "vx": [64, 65, 62, 63],
    "qx": [32, 33, 34, 35, 36, 37, 38, 39], "pp": [40, 41, 42, 43], "pts": [58, 59, 60, 61],
    "xo": [(24, 25), (26, 27), (28, 29), (30, 31), (48, 49), (50, 51), (53, 54), (55, 56)],
    "hid": [(24 + 2 * i, 25 + 2 * i) for i in range(8)],
    "la": [[40, 41, 42, 43], [44, 45, 46, 47]], "gq": [24, 25, 26, 27], "gk": [28, 29, 30, 31],
    "gr": [32, 33, 34, 35, 36, 37, 38, 39], "gv": [48, 49, 50, 51, 52, 53, 54, 55],
    "e1": [56, 66], "e2": [57, 67], "ks": [58, 68], "qs": [59, 69], "near": 60, "far": [61, 62], "gdiag": 63, "yg": 64,
    "zt": 63, "upa": 64, "pos": 65,
    "sin": 40, "cos": 41, "rot": [42, 43], "ak": 44, "aq": [45, 46, 47, 48], "av": 49,
    "sc": [50, 51, 52, 53, 54, 55, 56, 57], "apt": [58, 59], "yatt": [60, 61, 62, 63],
    "y_att": [(50, 51), (52, 53), (54, 55), (56, 57)],
    "g_att": [75, 76, 77, 78, 64, 65, 66, 67], "g_gla": [40, 41, 42, 43, 44, 45, 46, 47],
    "hn_f": [8, 9, 10, 11, 12, 13, 14, 15], "hn_t": [(16, 17), (18, 19), (20, 21), (22, 23)],
    "rank": 58, "aff": 59, "rank_t": 60, "wr": 61, "pick": [62, 63],
    "xg": [(8, 9), (10, 11)], "ht": (12, 13), "eh": (14, 15), "put": [64, 65], "ey": [(75, 76), (77, 78)],
    "p": [24, 25], "pp2": [(26, 27), (28, 29)], "pw": [30, 31, 32, 33, 34, 35, 36, 37],
    "out": [56, 57],
}
XIN = [(8 + 2 * i, 9 + 2 * i) for i in range(8)]
XPLE = [(38 + 2 * i, 39 + 2 * i) for i in range(8)]
RSTD, RSTD1 = 74, 73
BANKS = {"dense": [0, 1, 2, 3], "mix": [4, 5], "out": [6, 7], "gate": [0, 1], "up": [2, 3], "down": [4, 5]}
RINGS = {"z": [70, 71, 72], "sq": [68, 69]}
EX_TILES = [50, 52, 54, 56, 48] + list(range(24, 40, 2)) + [40, 42, 44, 46] + [66, 68, 70, 72]
EX_TILES_EARLY = 17


def encoder_decoder_kernel(nc, io, outs):
    T, V, A, G, D = (Lane(nc, n) for n in ("pe", "dve", "act", "pool", "sp"))
    cat, ncc = const_index()
    vat, nvc = vec_index()
    W = lambda i, n=P: slice(n * i, n * i + n)

    top = BASE
    def region(name, cols, dt=F32):
        nonlocal top
        t = nc.alloc_sbuf_tensor_at(name, [P, cols], dt, offset=top)
        top += -(-cols * 4 // 32) * 32
        return t

    cst = region("cst", ncc)
    vec = region("vec", nvc)
    sm = region("sm", 512)
    wide_at = top
    wide = region("wide", 4 * 4 * 129)
    raw_at = top
    raws = [region(f"raw{i}", 1024) for i in range(NRAW)]
    his = [region(f"whi{i}", 1024, F32R) for i in range(NSPL)]
    los = [region(f"wlo{i}", 1024, F32R) for i in range(NSPL)]
    tile_at = [top + SLOT * i for i in range(75)] + [wide_at + SLOT * i for i in range(4)]
    assert tile_at[74] + SLOT <= TOP
    F = [nc.alloc_sbuf_tensor_at(f"t{i}", [P, S], F32, offset=a) for i, a in enumerate(tile_at)]
    R = [nc.alloc_sbuf_tensor_at(f"t{i}r", [P, S], F32R, offset=a) for i, a in enumerate(tile_at)]
    bank = [nc.alloc_psum_tensor(f"bank{i}", [P, S], F32) for i in range(8)]

    C = lambda k, n=P: cst[:, cat[k]:cat[k] + n]
    vcol = lambda k, i=0: vec[:, vat[k] + i:vat[k] + i + 1]
    ident, ones, one, eps = C("ident"), C("ones"), C("ones", 1), vcol("eps")

    end, left = {}, {}

    uses = dict.fromkeys(list(BANKS) + list(RINGS), 0)
    first = {}
    def use(ring):
        uses[ring] += 1
        return uses[ring] - 1

    def gone(ring, k):
        n = len(BANKS.get(ring) or RINGS[ring])
        return left[ring, k - n] if k >= n else first.get(ring)

    def B(ring, k):
        return bank[BANKS[ring][k % len(BANKS[ring])]]

    def RT(ring, k):
        return F[RINGS[ring][k % len(RINGS[ring])]]

    channels = {}
    def channel(name):
        if name not in channels:
            channels[name] = Channel(nc, name)
        return channels[name]

    def load(name, dst, src, *waits):
        return D.dma(channel(name), lambda e: e.dma_start(dst, src), *waits)

    def act(out, in_, fn, *waits, bias=None, scale=None, acc=None):
        kw = {k: v for k, v in (("bias", bias), ("scale", scale), ("accum_out", acc)) if v is not None}
        return A.do(lambda e: e.activation(out, in_, fn, **kw), *waits)

    def tt(out, a, b, op, *waits, on=V):
        return on.do(lambda e: e.tensor_tensor(out, a, b, op), *waits)

    def ts(out, a, s1, s2, o0, o1, *waits, on=V):
        if o1 is None:
            return on.do(lambda e: e.tensor_scalar(out, a, s1, None, o0), *waits)
        return on.do(lambda e: e.tensor_scalar(out, a, s1, s2, o0, o1), *waits)

    def stt(out, a, s, b, o0, o1, *waits):
        return V.do(lambda e: e.scalar_tensor_tensor(out=out, in0=a, scalar=s, in1=b, op0=o0, op1=o1), *waits)

    def mm(out, lhsT, rhs, start, stop, *waits):
        return T.do(lambda e: e.matmul(out, lhsT, rhs, start=start, stop=stop), *waits)

    def mmq(out, lhsT, rhs, start, stop, *waits):
        T.quiet(lambda e: e.matmul(out, lhsT, rhs, start=start, stop=stop), *waits)

    def tr(out, in_, *waits):
        n = in_.shape[0]
        return T.do(lambda e: e.transpose(out, in_, ident[0:n, 0:n]), *waits)

    def recip(x, *waits):
        return V.do(lambda e: e.reciprocal(x, x), *waits)

    def reduce(out, in_, op, *waits):
        return V.do(lambda e: e.tensor_reduce(out, in_, AX.X, op), *waits)

    def copy(out, in_, *waits, on=V):
        if on is A:
            return act(out, in_, ACT.Copy, *waits)
        return on.do(lambda e: e.tensor_copy(out, in_), *waits)

    def fill(out, x, *waits):
        return V.do(lambda e: e.memset(out, x), *waits)

    def put_where(dst, mask, src, *waits):
        m = mask.bitcast(I32).unsqueeze(1).to_broadcast([P, 4, P])
        d, s = (x.rearrange("p (c t) -> p c t", c=4) for x in (dst, src))
        return V.do(lambda e: e.copy_predicated(d, m, s), *waits)

    plan = unit_plan()
    nunit = len(plan) - TAIL
    limit = [nunit]

    def load_unit(u, *waits):
        if u < limit[0]:
            r = raws[u % NRAW]
            end["raw", u] = load(f"raw{u % NRAW}", r[:], io["units"][u], left.get(("raw", u - NRAW)), waits)

    def split_unit(u, *waits):
        if u < limit[0]:
            r, h, l = raws[u % NRAW], his[u % NSPL], los[u % NSPL]
            a = act(h[:], r[:], ACT.Copy, end["raw", u], left.get(("unit", u - NSPL)), waits)
            b = tt(l[:], r[:], h[:].bitcast(F32), ALU.subtract, a)
            end["unit", u] = left["raw", u] = (a, b)
            load_unit(u + NRAW)

    cur = [0]
    def next_unit(kind, weight, first_col):
        u = cur[0]
        k = plan[u]
        assert k[0] == kind and k[1] == weight and (first_col is None or k[3][0] == first_col), (u, k[:3], k[3][0])
        cur[0] += 1
        return u

    def done_unit(u, tok):
        left["unit", u] = tok
        split_unit(u + NSPL - 1)

    def fm(weight, col, ins, n=S):
        u = next_unit("f", weight, col)
        k = use("dense")
        wh, wl, o = his[u % NSPL], los[u % NSPL], B("dense", k)[:, 0:n]
        for d, (hi, lo, name) in enumerate(ins):
            mmq(o, wh[:, W(d)], hi, d == 0, False, gone("dense", k), end["unit", u], end[name])
            mmq(o, wh[:, W(d)], lo, False, False)
            (mmq if d < KT - 1 else mm)(o, wl[:, W(d)], hi, False, d == KT - 1)
        end["dense", k] = (T.sem, T.n)
        done_unit(u, end["dense", k])
        return k

    def fm_half(weight, col, ins):
        u = next_unit("h", weight, col)
        wh, wl, ks = his[u % NSPL], los[u % NSPL], []
        for c in range(2):
            k = use("dense")
            o = B("dense", k)[:]
            for d, (hi, lo, name) in enumerate(ins):
                w = slice(256 * d + P * c, 256 * d + P * c + P)
                mmq(o, wh[:, w], hi, d == 0, False, gone("dense", k), end["unit", u], end[name])
                mmq(o, wh[:, w], lo, False, False)
                (mmq if d < 3 else mm)(o, wl[:, w], hi, False, d == 3)
            end["dense", k] = (T.sem, T.n)
            ks.append(k)
        done_unit(u, end["dense", k])
        return ks

    def tm(weight, col, ins, nt=4):
        ks = [use("dense") for _ in range(nt)]
        for g in range(4):
            u = next_unit("t", weight, col)
            wh, wl = his[u % NSPL], los[u % NSPL]
            for i, k in enumerate(ks):
                o = B("dense", k)[:]
                for kk in range(2):
                    d = 2 * g + kk
                    hi, lo, name = ins[d]
                    mmq(o, hi[:, W(i)], wh[:, W(kk, S)], d == 0, False, gone("dense", k), end["unit", u], end[name])
                    mmq(o, lo[:, W(i)], wh[:, W(kk, S)], False, False)
                    end["dense", k] = mm(o, hi[:, W(i)], wl[:, W(kk, S)], False, d == KT - 1)
            done_unit(u, end["dense", ks[-1]])
            yield
        return ks

    def split(name, src, gain, places, *waits):
        h, l = R[places[0]][:, 0:src.shape[1]], R[places[1]][:, 0:src.shape[1]]
        if gain is None:
            a = act(h, src, ACT.Copy, waits)
            b = tt(l, src, h.bitcast(F32), ALU.subtract, a, waits)
        else:
            a = act(h, src, ACT.Identity, waits, scale=gain)
            b = stt(l, src, gain, h.bitcast(F32), ALU.mult, ALU.subtract, a, waits)
        end[name] = (a, b)
        return (h, l, name)

    def add_square(acc, i, src, n, *waits, scale=None):
        if i == 0:
            end["acc", acc] = act(F[acc][:, 0:n], src, ACT.Square, left.get(("acc", acc)), waits, scale=scale)
            return end["acc", acc]
        k = use("sq")
        sq = RT("sq", k)[:, 0:n]
        a = act(sq, src, ACT.Square, gone("sq", k), waits, scale=scale)
        end["acc", acc] = left["sq", k] = tt(F[acc][:, 0:n], F[acc][:, 0:n], sq, ALU.add, a, end["acc", acc], on=G)
        return a

    def sum_rows(acc, n):
        k = use("mix")
        end["mix", k] = left["acc", acc] = mm(B("mix", k)[:, 0:n], ones, F[acc][:, 0:n], True, True, gone("mix", k), end["acc", acc], end["cst"])
        return k

    def sum_columns(acc, n):
        k = use("mix")
        for i in range(n // P):
            t = mm(B("mix", k)[:, i:i + 1], F[acc][:, W(i)], one, True, True, gone("mix", k), end["acc", acc], end["cst"])
        end["mix", k] = left["acc", acc] = t
        return k

    def rsqrt(out, sums, width, *waits):
        a = act(out, sums, ACT.Ln, waits, scale=1.0 / width, bias=eps)
        return a, act(out, out, ACT.Exp, a, scale=-0.5)

    def rstd_row(tile, acc, n=S):
        k = sum_rows(acc, n)
        left["mix", k], end["rstd", tile] = rsqrt(F[tile][:, 0:n], B("mix", k)[:, 0:n], 1024, end["mix", k], left.get(("rstd", tile)))

    def rstd_column(out, name, acc, n=S):
        k = sum_columns(acc, n)
        left["mix", k], end[name] = rsqrt(out, B("mix", k)[:, 0:n // P], 1024, end["mix", k])

    end["vec"] = load("vec", vec[:], io["vecs"])
    xt = io["xT"]
    for i in range(KT):
        end["x", i] = load(f"x{i}", F[i][:], xt[W(i)])
        if i in (0, 3, 7):
            load_unit((0, 3, 7).index(i))
    end["cst"] = load("cst", cst[:], io["consts"])
    def bias_rows(name, tile, start):
        src = bass.AP(io["b_in"].tensor, io["b_in"].offset + start, [[0, P], [1, S]])
        end[name] = load(name, F[tile][:], src)
    bias_rows("b_hi", 46, 1536)
    bias_rows("b_mv", 67, 3584)

    xs = []
    for i in range(KT):
        if i == 0:
            split_unit(0)
        xs.append(split(("xs", i), F[i][:], vcol("norm_mix", i), XIN[i], end["x", i], end["vec"]))
        if i == 1:
            split_unit(1)
        add_square(66, i, F[i][:], S, end["x", i])

    nb, e0, lb, oml = sm[:, 0:8], sm[:, 8:16], sm[:, 16:24], sm[:, 24:32]
    end["nb"] = ts(nb, vec[:, vat["b_ff"]:vat["b_ff"] + 8], -1.0, None, ALU.mult, None, end["vec"])
    lbv = vec[:, vat["lb"]:vat["lb"] + 8]
    t = tt(e0, lbv, lbv, ALU.subtract, end["vec"])
    t = act(e0, e0, ACT.Exp, t)
    t = copy(lb, e0, t)
    t = recip(lb, t)
    t = tt(e0, e0, lb, ALU.mult, t)
    t = tt(lb, e0, e0, ALU.subtract, t)
    end["lb"] = ts(oml, lb, -1.0, 1.0, ALU.mult, ALU.add, t)

    rcol = sm[:, 32:36]
    rstd_row(RSTD, 66)
    rstd_column(rcol, "rcol", 66)
    rbc = F[RSTD]

    def z_of(kd):
        k = use("z")
        end["z", k] = left["dense", kd] = tt(RT("z", k)[:], B("dense", kd)[:], rbc[:], ALU.mult, end["dense", kd], gone("z", k), end["rstd", RSTD])
        return k

    def silu_of(name, k, bias, tile, *waits):
        a = act(F[tile][:], RT("z", k)[:], ACT.Sigmoid, end["z", k], waits, bias=bias)
        end[name] = left["z", k] = stt(F[tile][:], RT("z", k)[:], bias, F[tile][:], ALU.add, ALU.mult, a)

    def hgrn_in(h):
        tq, tf, tg, tkf, tkb = TILES["hin"][h % 2]
        silu_of(("q", h), z_of(fm("w_in", 128 * h, xs)), vcol("b_q", h), tq, left.get(("hin", h - 2)))
        yield
        for d, (name, col, ti, tk, f, kf) in enumerate((("b_ff", 512, tf, tkf, "f", "kf"), ("b_fb", 1024, tg, tkb, "g", "kb"))):
            k = z_of(fm("w_in", col + 128 * h, xs))
            j = 4 * d + h
            a = act(F[ti][:], RT("z", k)[:], ACT.Sigmoid, end["z", k], left.get(("hin", h - 2)), bias=vcol(name, h))
            b = left["z", k] = act(F[tk][:], RT("z", k)[:], ACT.Sigmoid, end["nb"], bias=nb[:, j:j + 1], scale=-1.0)
            end[f, h] = ts(F[ti][:], F[ti][:], oml[:, j:j + 1], lb[:, j:j + 1], ALU.mult, ALU.add, a, end["lb"])
            end[kf, h] = ts(F[tk][:], F[tk][:], oml[:, j:j + 1], None, ALU.mult, None, b)
            yield

    def v_in():
        ks = yield from tm("w_in", 1536, xs)
        for i, k in enumerate(ks):
            end["v_h", i] = left["dense", k] = stt(F[TILES["v_h"][i]][:], B("dense", k)[:], rcol[:, i:i + 1], F[46][:],
                                                   ALU.mult, ALU.add, end["dense", k], end["b_hi"], end["rcol"])
        left["b_hi"] = end["v_h", 3]
        yield

    vw = wide[:].rearrange("p (i h e) -> p i h e", i=4, h=4)
    end["vw ones"] = fill(vw[:, :, :, 128:129], 1.0)
    def vm_in():
        ks = yield from tm("w_in", 3584, xs)
        for i, k in enumerate(ks):
            end["v_m", i] = left["dense", k] = stt(
                vw[:, i, :, 0:128], B("dense", k)[:].rearrange("p (h e) -> p h e", h=4), rcol[:, i:i + 1],
                F[67][:].rearrange("p (h e) -> p h e", h=4), ALU.mult, ALU.add, end["dense", k], end["b_mv"], end["vw ones"])
        left["b_mv"] = end["v_m", 3]
        yield

    def blocks(ap, size):
        v = ap.rearrange("p (b two l) -> p b two l", two=2, l=size)
        return v[:, :, 0, :], v[:, :, 1, :]

    def scores(k, K, Q, *waits):
        for c in range(4):
            end["mix", k] = mm(B("mix", k)[:, W(c)], K[:, W(c)], Q[:, W(c)], True, True, gone("mix", k), waits)

    def hgrn_head(h):
        tq, tf, tg, tkf, tkb = TILES["hin"][h % 2]
        q, f, g, kf, kb = (F[i] for i in (tq, tf, tg, tkf, tkb))
        qf, kc, qc, dg = (F[TILES[n]] for n in ("qf", "kc", "qc", "diag"))
        qb = q
        free_work = left.get(("hgrn work", h - 1))
        t = tt(kc[:], kf[:], kb[:], ALU.add, end["kf", h], end["kb", h], free_work)
        k = use("mix")
        scores(k, kc, q, t, end["q", h])
        end["diag"] = left["mix", k] = copy(dg[:], B("mix", k)[:], end["mix", k], free_work, on=A)
        combined_read = end["mix", k]
        yield
        s_qf = tt(qf[:], q[:], f[:], ALU.mult, end["q", h], end["f", h], free_work)
        s_qb = tt(q[:], q[:], g[:], ALU.mult, end["g", h], s_qf, end["mix", k])
        s_kf, s_kb = end["kf", h], end["kb", h]
        df, db, s_df, s_db = f[:], g[:], end["f", h], end["g", h]
        size = 1
        while size < P:
            (qfe, qfo), (qbe, qbo), (kfe, kfo), (kbe, kbo) = (blocks(x[:], size) for x in (qf, qb, kf, kb))
            (qce, qco), (kce, kco) = (blocks(x[:], size) for x in (qc, kc))
            c_qf = act(qco, qfo, ACT.Copy, s_qf, combined_read, free_work)
            c_kf = act(kce, kfe, ACT.Copy, s_kf)
            c_qb = act(qce, qbe, ACT.Copy, s_qb)
            c_kb = act(kco, kbo, ACT.Copy, s_kb)
            k = use("mix")
            scores(k, kc, qc, c_kb)
            combined_read = end["mix", k]
            yield
            n = S // (2 * size)
            lv = size.bit_length() - 1
            t2 = F[TILES["t2"][lv % 2]]
            (dfe, dfo), (dbe, dbo) = blocks(df, 1), blocks(db, 1)
            line = lambda x: x.rearrange("p b l -> p (b l)")
            over = lambda x: x.to_broadcast([P, n, size])
            n_df = tt(t2[:, 0:n], line(dfe), line(dfo), ALU.mult, s_df, s_kb, free_work)
            n_db = tt(t2[:, 256:256 + n], line(dbe), line(dbo), ALU.mult, s_db)
            s_qf = tt(qfo, qfo, over(dfe), ALU.mult, s_qf, s_df, c_qf)
            s_kf = tt(kfe, kfe, over(dfo), ALU.mult, s_kf, c_kf)
            s_qb = tt(qbe, qbe, over(dbo), ALU.mult, s_qb, s_db, c_qb)
            s_kb = tt(kbo, kbo, over(dbe), ALU.mult, s_kb, c_kb)
            end["diag"] = left["mix", k] = put_where(dg[:], C(f"lev{lv}"), B("mix", k)[:], end["mix", k], end["diag"])
            df, db, s_df, s_db = t2[:, 0:n], t2[:, 256:256 + n], n_df, n_db
            size *= 2
            yield
        place = {}
        near = ((0, 1, kf, qf), (2, 3, kf, qf), (1, 0, kb, qb), (3, 2, kb, qb))
        k = use("mix")
        for n, (ks, qt, K, Q) in enumerate(near):
            end["mix", k] = mm(B("mix", k)[:, W(n)], K[:, W(ks)], Q[:, W(qt)], True, True, s_qf, s_qb, s_kf, s_kb, gone("mix", k))
            place[ks, qt] = (F[TILES["t2"][1]], n)
        end["near"] = left["mix", k] = copy(F[TILES["t2"][1]][:], B("mix", k)[:], end["mix", k], s_qf, s_kf, s_qb, s_kb, on=A)
        yield
        u = [tt(qf[:, W(3)], qf[:, W(3)], df[:, 2:3].to_broadcast([P, P]), ALU.mult, end["mix", k], s_df),
             tt(kf[:, W(0)], kf[:, W(0)], df[:, 1:2].to_broadcast([P, P]), ALU.mult),
             tt(qb[:, W(0)], qb[:, W(0)], db[:, 1:2].to_broadcast([P, P]), ALU.mult, s_db),
             tt(kb[:, W(3)], kb[:, W(3)], db[:, 2:3].to_broadcast([P, P]), ALU.mult)]
        for m, (K, Q, s0, t0, dst) in enumerate(((kf, qf, 0, 2, kc), (kb, qb, 2, 0, qc))):
            k = use("mix")
            for j in range(2):
                end["mix", k] = mm(B("mix", k)[:, W(j, 256)], K[:, W(s0 + j)], Q[:, P * t0:P * t0 + 256], True, True, u, gone("mix", k))
                for i in range(2):
                    place[s0 + j, t0 + i] = (dst, 2 * j + i)
            end["far", m] = left["mix", k] = copy(dst[:], B("mix", k)[:], end["mix", k], combined_read, on=A)
            yield
        left["hin", h] = end["mix", k]
        for i in range(4):
            place[i, i] = (dg, i)
        o = use("out")
        for i in range(4):
            for j in range(4):
                src, n = place[j, i]
                end["out", o] = mm(B("out", o)[:, W(i)], F[TILES["v_h"][j]][:, W(h)], src[:, W(n)], j == 0, j == 3,
                                   end["v_h", j], end["diag"], end["near"], end["far", 0], end["far", 1], gone("out", o))
            yield
        left["hgrn work", h] = left["v_h"] = end["out", o]
        yield from head_out(("y_h", h), o, vcol("hgrn_norm", h), F[TILES["hg"][h]], end["hg", h], TILES["yh"], TILES["y_h"][h],
                            left.get(("yh", h - 1)))
        left["yh", h] = end["y_h", h]
        left["hg", h] = end["y", h]

    def head_out(name, o, gain, gate, gate_ok, tile, places, *waits):
        k, m = use("sq"), use("mix")
        a = act(RT("sq", k)[:], B("out", o)[:], ACT.Square, end["out", o], gone("sq", k))
        end["mix", m] = mm(B("mix", m)[:], ones, RT("sq", k)[:], True, True, a, gone("mix", m))
        yield
        rb = RT("sq", k)
        left["mix", m], t = rsqrt(rb[:], B("mix", m)[:], P, end["mix", m])
        y = F[tile]
        t = left["out", o] = left["sq", k] = stt(y[:], B("out", o)[:], gain, rb[:], ALU.mult, ALU.mult, t, waits)
        yield
        t = end["y", name[1]] = tt(y[:], y[:], gate[:], ALU.mult, t, gate_ok)
        y_mix[name] = split(name, y[:], None, places, t)
        yield

    y_mix = {}

    def gates():
        g0, g1, g2, g3, g4 = (F[i] for i in TILES["gates"])
        k = z_of(fm("w_in", 4608, xs))
        z_ok = left["z", k] = act(g0[:], RT("z", k)[:], ACT.Identity, end["z", k], bias=vcol("b_gt"))
        a = act(g1[:], g0[:], ACT.Abs, z_ok)
        a = act(g1[:], g1[:], ACT.Exp, a, scale=-1.0)
        a = act(g1[:], g1[:], ACT.Ln, a, bias=one)
        t = stt(g1[:], g0[:], 0.0, g1[:], ALU.min, ALU.subtract, a)
        yield
        k = use("mix")
        for i in range(4):
            end["mix", k] = tr(B("mix", k)[:, W(i)], g1[:, W(i)], t, gone("mix", k))
        turned = end["mix", k]
        t = left["mix", k] = copy(g2[:], B("mix", k)[:], turned, left["b_hi"], on=A)
        yield
        k = use("mix")
        b = B("mix", k)
        for i in range(4):
            for j in range(i + 1):
                mmq(b[0:64, W(i)], g2[:, P * j + 32:P * j + 96], C("le") if j == i else ones, j == 0, j == i, t, gone("mix", k))
            for j in range(i, 4):
                end["mix", k] = mm(b[64:96, W(i)], g2[:, P * j + 96:P * j + 128], C("ge") if j == i else ones, j == i, j == 3)
        f_ok = left["mix", k] = copy(g4[0:96, :], b[0:96, :], end["mix", k], on=A)
        summed = end["mix", k]
        yield
        x0 = fill(g1[96:128, :], 0.0, turned)
        x1 = tt(g1[0:96, :], g0[0:96, :], g4[0:96, :], ALU.subtract, f_ok, z_ok, turned)
        m_f = m_b = ts(g3[0:96, :], g1[0:96, :], 0.0, None, ALU.max, None, x1)
        yield
        for lv in range(9):
            size = 1 << lv
            e, o = blocks(g3[:], size)
            n = S // (2 * size)
            m_f = tt(o[0:4], o[0:4], e[0:4, :, size - 1:size].to_broadcast([4, n, size]), ALU.max, m_f)
            m_b = tt(e[64:68], e[64:68], o[64:68, :, 0:1].to_broadcast([4, n, size]), ALU.max, m_b)
            if lv % 2:
                yield
        end["M"] = (m_f, m_b)
        t = tt(g0[0:96, :], g3[0:96, :], g4[0:96, :], ALU.add, m_f, m_b, x1)
        left["F"] = t
        t = ts(g0[0:96, :], g0[0:96, :], -88.0, None, ALU.max, None, t)
        yield
        a = act(g1[32:36, :], g0[0:4, :], ACT.Exp, t, x1, scale=-1.0)
        a = act(g1[96:100, :], g0[64:68, :], ACT.Exp, x0, scale=-1.0)
        k = use("mix")
        for i in range(4):
            end["mix", k] = tr(B("mix", k)[:, W(i)], g1[:, W(i)], a, gone("mix", k))
        end["gate columns"] = left["mix", k] = copy(g2[:], B("mix", k)[:], end["mix", k], summed, on=A)
        left["gate temps"] = end["mix", k]
        yield

    def conv_in(name, h, col, ct, scale):
        tile = TILES[name][h]
        kz = z_of(fm("w_in", col, xs))
        x = RT("z", kz)
        x_ok = act(x[:], x[:], ACT.Identity, end["z", kz], bias=vcol("b_m" + name, h))
        w = lambda j: vcol("conv_w", 8 * j + ct)
        y, g = F[tile], F[TILES["conv"][ct // 4]]
        t = act(y[:], x[:], ACT.Identity, x_ok, left["hin", 2 if tile < 53 else 3], scale=w(2), bias=vcol("conv_b", ct))
        for j in (0, 1, 3, 4):
            o, i = (slice(2 - j, S), slice(0, S - 2 + j)) if j < 2 else (slice(0, S + 2 - j), slice(j - 2, S))
            t = stt(y[:, o], x[:, i], w(j), y[:, o], ALU.mult, ALU.add, t, x_ok)
        left["z", kz] = t
        a = act(g[:], y[:], ACT.Sigmoid, t, left["hgrn work", 3], left.get(("conv", ct // 4)))
        end[name, h] = left["conv", ct // 4] = stt(y[:], y[:], scale, g[:], ALU.mult, ALU.mult, a)
        yield

    def conv_all():
        for h in range(4):
            yield from conv_in("q", h, 2560 + 128 * h, h, 1.0)
            yield from conv_in("k", h, 3072 + 128 * h, 4 + h, P ** -0.5)

    def mlstm_head(h):
        q, kk = F[TILES["q"][h]], F[TILES["k"][h]]
        M, col = F[TILES["gates"][3]], F[TILES["gates"][2]]
        mb, md = [F[i] for i in TILES["mb"]], [F[i] for i in TILES["md"]]
        pt = [F[i] for i in TILES["pt"]]
        hn, junk, y = F[TILES["hn"]], F[TILES["junk"]], F[TILES["ym"]]
        for d, (r0, mask) in enumerate(((0, "hi"), (64, "lo"))):
            k = use("mix")
            end["mix", k] = mm(B("mix", k)[:], ident[r0:r0 + 4, r0 + h:r0 + h + 1].to_broadcast([4, P]), M[r0:r0 + 4, :], True, True,
                               end["M"], gone("mix", k))
            end["mb", d] = left["mix", k] = copy(mb[d][:], B("mix", k)[:], end["mix", k], left["v_h"], left.get(("mlstm exp", h - 1)), on=A)
            end["md", d] = tt(md[d][:].rearrange("p (c t) -> p c t", c=4), mb[d][:].rearrange("p (c t) -> p c t", c=4),
                              C(mask).unsqueeze(1).to_broadcast([P, 4, P]), ALU.add, end["mb", d])
        yield
        for j in range(4):
            k = use("mix")
            b = B("mix", k)
            end["mix", k] = mm(b[:], kk[:, W(j)], q[:], True, True, end["q", h], end["k", h], gone("mix", k))
            e, g = pt[j], pt[j + 1]
            c0, c1 = col[:, P * j + h:P * j + h + 1], col[:, P * j + 64 + h:P * j + 64 + h + 1]
            free = (left["hg", 3], left.get(("pt", h - 1)), left["hgrn work", 3])
            a = act(e[:, W(j)], md[0][:, W(j)], ACT.Exp, end["md", 0], end["gate columns"], free, scale=-1.0, bias=c0)
            if j < 3:
                a = act(e[:, P * j + P:], mb[0][:, P * j + P:], ACT.Exp, end["mb", 0], scale=-1.0, bias=c0)
            end["p fwd", j] = tt(e[:, P * j:], e[:, P * j:], b[:, P * j:], ALU.mult, a, end["mix", k])
            a = act(g[:, W(j)], md[1][:, W(j)], ACT.Exp, end["md", 1], scale=-1.0, bias=c1)
            if j > 0:
                a = act(g[:, 0:P * j], mb[1][:, 0:P * j], ACT.Exp, end["mb", 1], scale=-1.0, bias=c1)
            end["p bwd", j] = left["mix", k] = tt(g[:, 0:P * j + P], g[:, 0:P * j + P], b[:, 0:P * j + P], ALU.mult, a, end["mix", k])
            yield
        left["mlstm exp", h] = (a, end["md", 1])
        left["qk", h] = end["mix", k]
        o0 = 40 + 16 * h
        ss, rs = sm[:, o0 + 8:o0 + 12], sm[:, o0 + 12:o0 + 16]
        for i in range(4):
            o = use("out")
            b = B("out", o)
            for j in range(i + 1):
                mmq(b[:, 0:129], pt[j][:, W(i)], vw[:, j, h, :], j == 0, j == i, end["p fwd", j], end["v_m", j], gone("out", o))
            for j in range(i, 4):
                end["out", o] = mm(b[:, 129:258], pt[j + 1][:, W(i)], vw[:, j, h, :], j == i, j == 3, end["p bwd", j])
            den = sm[:, o0 + 2 * i:o0 + 2 * i + 2]
            c = P * i + 32 + h
            t = act(den, b[:, 128:258:129], ACT.Abs, end["out", o])
            t = tt(den, den, col[:, c:c + 65:64], ALU.max, t, end["gate columns"])
            t = recip(den, t)
            a = act(hn[:, W(i)], b[:, 0:128], ACT.Identity, t, left.get(("hn", h - 1)), left["hgrn work", 3], scale=den[:, 0:1])
            t = left["out", o] = stt(hn[:, W(i)], b[:, 129:257], den[:, 1:2], hn[:, W(i)], ALU.mult, ALU.add, a)
            s_ = act(junk[:, W(i)], hn[:, W(i)], ACT.Square, t, acc=ss[:, i:i + 1])
            yield
        left["pt", h] = end["out", o]
        a = act(rs, ss, ACT.Ln, s_, scale=1.0 / P, bias=eps)
        a = act(rs, rs, ACT.Exp, a, scale=-0.5)
        k = use("mix")
        for i in range(4):
            t = ts(hn[:, W(i)], hn[:, W(i)], rs[:, i:i + 1], None, ALU.mult, None, a)
            end["mix", k] = tr(B("mix", k)[:, W(i)], hn[:, W(i)], t, gone("mix", k))
        left["hn", h] = end["mix", k]
        yield
        t = left["mix", k] = stt(y[:], B("mix", k)[:], vcol("mlstm_norm", h), F[TILES["mo"][h]][:], ALU.mult, ALU.mult,
                                 end["mix", k], end["mo", h], left.get(("ym", h - 1)))
        y_mix["y_m", h] = split(("y_m", h), y[:], None, TILES["y_m"][h], t, left["qk", h])
        left["ym", h] = end["y_m", h]
        yield

    def hg_in(h):
        silu_of(("hg", h), z_of(fm("w_in", 2048 + 128 * h, xs)), vcol("b_hg", h), TILES["hg"][h])
        yield

    def mo_in(h):
        k = z_of(fm("w_in", 4096 + 128 * h, xs))
        end["mo", h] = left["z", k] = act(F[TILES["mo"][h]][:], RT("z", k)[:], ACT.Sigmoid, end["z", k], bias=vcol("b_mo", h))
        yield

    def hgrn_dense():
        yield from hgrn_in(1)
        yield from hg_in(0)
        yield from gates()
        yield from hg_in(1)
        while ("hin", 0) not in left:
            yield
        yield from hgrn_in(2)
        yield from hg_in(2)
        yield from mo_in(0)
        yield from mo_in(1)
        while ("hin", 1) not in left:
            yield
        yield from hgrn_in(3)
        yield from hg_in(3)
        yield from mo_in(2)
        yield from mo_in(3)
        yield from vm_in()

    def hgrn_all():
        for h in range(4):
            while ("kb", h) not in end or ("hg", h) not in end:
                yield
            yield from hgrn_head(h)

    drain(hgrn_in(0))
    drain(v_in())
    weave((hgrn_all(), 3), (hgrn_dense(), 1))

    def xkv():
        n = S // 2
        mem = [F[i] for i in TILES["mem"]]
        ms = []
        for i, x in enumerate(mem):
            end["mem", i] = load(f"x{i}", x[:].rearrange("p (k t) -> p k t", k=2),
                                 io["memT"][W(i, 256)].rearrange("(k p) t -> p k t", k=2), left["xs"])
        for i, x in enumerate(mem):
            th, tl = TILES["memn"][2 * i:2 * i + 2]
            for j in range(2):
                c, d = W(j, n), 2 * i + j
                g = vcol("norm_mem", d)
                a = act(R[th][:, c], x[:, c], ACT.Identity, end["mem", i], left["xs"], scale=g)
                b = stt(R[tl][:, c], x[:, c], g, R[th][:, c].bitcast(F32), ALU.mult, ALU.subtract, a)
                end["memn", d] = (a, b)
                ms.append((R[th][:, c], R[tl][:, c], ("memn", d)))
                add_square(66, d, x[:, c], n, end["mem", i])
            yield
        rstd_row(RSTD1, 66, n)
        rc = sm[:, 36:38]
        rstd_column(rc, "rcol mem", 66, n)
        for i in range(8):
            k = fm("w_xkv", 128 * i, ms, n)
            end["kx", i] = left["dense", k] = tt(F[TILES["kx"][i // 2]][:, W(i % 2, n)], B("dense", k)[:, 0:n], F[RSTD1][:, 0:n], ALU.mult,
                                                 end["dense", k], end["rstd", RSTD1], left["gate temps"], left["hin", 3])
            yield
        left["rstd", RSTD1] = end["kx", 7]
        for g, c in enumerate((1024, 1536)):
            ks = yield from tm("w_xkv", c, ms, 2)
            for i, k in enumerate(ks):
                end["vx", 2 * g + i] = left["dense", k] = act(
                    F[TILES["vx"][2 * g + i]][:], B("dense", k)[:], ACT.Identity, end["dense", k], end["rcol mem"],
                    left["yh", 3], left["F"], left["conv", 0], left["conv", 1], scale=rc[:, i:i + 1])
        left["memn"] = end["dense", k]
        yield

    def conv_then_memory():
        yield from conv_all()
        left["xs"] = end["dense", uses["dense"] - 1]
        yield from xkv()

    def mlstm_all():
        for h in range(4):
            while ("k", h) not in end:
                yield
            yield from mlstm_head(h)

    weave((conv_then_memory(), 1), (mlstm_all(), 2))

    left_x = {}
    for i in range(KT):
        left_x[i] = left["xs"]

    def add_to(i, ring, k):
        end["x", i] = left[ring, k] = tt(F[i][:], F[i][:], B(ring, k)[:], ALU.add, end[ring, k], end["x", i], left_x[i])

    def sublayer(weight, ins, gain, name, *waits):
        nxt = []
        for i in range(KT):
            add_to(i, "dense", fm(weight, 128 * i, ins))
            nxt.append(split((name, i), F[i][:], vcol(gain, i), XIN[i], end["x", i], waits))
            a = add_square(66, i, F[i][:], S, end["x", i])
            left_x[i] = (end[name, i], a)
        left[weight] = end["dense", uses["dense"] - 1]
        rstd_row(RSTD, 66)
        return nxt

    left["rstd", RSTD] = left["z", uses["z"] - 1]
    y_in = [y_mix["y_h", h] for h in range(4)] + [y_mix["y_m", h] for h in range(4)]
    xs = sublayer("w_out", y_in, "norm_xattn", "xs1", left["memn"])

    def xattn_head(h):
        kx = F[TILES["kx"][h]]
        q = [F[TILES["qx"][2 * h]], F[TILES["qx"][2 * h + 1]]]
        o = 104 + 16 * h
        nm, su = sm[:, o:o + 4], sm[:, o + 4:o + 8]
        two = TILES["pp"][2 * (h % 2):2 * (h % 2) + 2]
        for g in range(2):
            k = use("mix")
            b, p = B("mix", k), F[two[g]]
            for i in (2 * g, 2 * g + 1):
                for d in range(2):
                    end["mix", k] = mm(b[:, W(i % 2, 256)], q[d][:, W(i)], kx[:, W(d, 256)], d == 0, d == 1,
                                       end["qx", 2 * h + d], end["kx", 2 * h + d], gone("mix", k))
            t = reduce(nm[:, W(g, 2)], b[:].rearrange("p (i s) -> p i s", i=2), ALU.max, end["mix", k])
            t = ts(nm[:, W(g, 2)], nm[:, W(g, 2)], -1.0 / 16, None, ALU.mult, None, t)
            for i in range(2):
                c = 2 * g + i
                a = act(p[:, W(i, 256)], b[:, W(i, 256)], ACT.Exp, t, left["mo"], left.get(("pp", h - 2)), scale=1.0 / 16,
                        bias=nm[:, c:c + 1], acc=su[:, c:c + 1])
            left["mix", k] = a
            t = recip(su[:, W(g, 2)], a)
            for i in range(2):
                c = 2 * g + i
                end["pp", g] = ts(p[:, W(i, 256)], p[:, W(i, 256)], su[:, c:c + 1], None, ALU.mult, None, t)
            yield
        pts = [F[i] for i in TILES["pts"][2 * (h % 2):2 * (h % 2) + 2]]
        for j in range(2):
            k = use("mix")
            for i in range(4):
                c = 256 * (i % 2) + P * j
                end["mix", k] = tr(B("mix", k)[:, W(i)], F[two[i // 2]][:, c:c + P], end["pp", i // 2], gone("mix", k))
            end["pts", j] = left["mix", k] = copy(pts[j][:], B("mix", k)[:], end["mix", k], left.get(("pts", h - 2)), left["hn", 3], left["pt", 3],
                                                  left["ym", 3], on=V if j else A)
        left["pp", h] = end["mix", k]
        yield
        for d in range(2):
            k = use("out")
            for j in range(2):
                v = F[TILES["vx"][2 * (h // 2) + j]]
                c = 256 * (h % 2) + P * d
                end["out", k] = mm(B("out", k)[:], v[:, c:c + P], pts[j][:], j == 0, j == 1, end["vx", 2 * (h // 2) + j], end["pts", j],
                                   gone("out", k))
            n = 2 * h + d
            xo_in.append(split(("xo", n), B("out", k)[:], None, TILES["xo"][n], end["out", k], left["w_out"]))
            left["out", k] = end["xo", n]
            yield
        left["pts", h] = end["out", k]

    xo_in = []
    left["mo"] = left["mix", uses["mix"] - 1]
    def xq_all():
        for i in range(KT):
            k = fm("w_xq", 128 * i, xs)
            end["qx", i] = left["dense", k] = tt(F[TILES["qx"][i]][:], B("dense", k)[:], F[RSTD][:], ALU.mult, end["dense", k], end["rstd", RSTD],
                                                 left["pt", 3], left["mlstm exp", 3])
            yield
        left["w_xq"] = end["dense", k]
        left["rstd", RSTD] = end["qx", 7]

    def xattn_all():
        for h in range(4):
            while ("qx", 2 * h + 1) not in end:
                yield
            yield from xattn_head(h)

    weave((xq_all(), 1), (xattn_all(), 2))
    xs = sublayer("w_xo", xo_in, "norm_mlp", "xs2", left["w_xq"])

    gg = sm[:, 168:176]
    end["gg"] = tt(gg, vec[:, vat["norm_final"]:vat["norm_final"] + 8], vec[:, vat["norm_mix_2"]:vat["norm_mix_2"] + 8], ALU.mult)
    nxt = []
    for r in range(4):
        hid = []
        for c in range(8):
            kd = fm("w_up", 128 * (8 * r + c), xs)
            k = use("z")
            z = RT("z", k)
            t = left["dense", kd] = tt(z[:], B("dense", kd)[:], F[RSTD][:], ALU.mult, end["dense", kd], gone("z", k), end["rstd", RSTD])
            t = stt(z[:], z[:], 0.0, z[:], ALU.max, ALU.mult, t)
            hid.append(split(("hid", c), z[:], None, TILES["hid"][c], t, left["w_xo"] if r == 0 else left["w_down", r - 1]))
            left["z", k] = end["hid", c]
        left["w_up"] = end["dense", kd]
        for i in range(KT):
            add_to(i, "dense", fm("w_down", 128 * i, hid))
            if r == 3:
                nxt.append(split(("xs3", i), F[i][:], gg[:, i:i + 1], XIN[i], end["x", i], end["gg"], left["w_up"]))
                a1 = add_square(66, i, F[i][:], S, end["x", i])
                a2 = add_square(67, i, F[i][:], S, end["x", i], scale=vcol("norm_final", i))
                left_x[i] = (end["xs3", i], a1, a2)
        left["w_down", r] = end["dense", uses["dense"] - 1]
    left["rstd", RSTD] = t

    xs = nxt
    def both(k1, k2, n, t1, t2, *waits):
        left["mix", k1], t = rsqrt(t1, B("mix", k1)[:, 0:n], 1024, end["mix", k1], waits)
        q = tt(t2, t1, t1, ALU.mult, t, waits)
        q = left["mix", k2] = tt(t2, t2, B("mix", k2)[:, 0:n], ALU.mult, q, end["mix", k2])
        q = act(t2, t2, ACT.Ln, q, scale=1.0 / 1024, bias=eps)
        q = act(t2, t2, ACT.Exp, q, scale=-0.5)
        return t, tt(t2, t2, t1, ALU.mult, q)
    end["rstd", RSTD1], end["rstd", RSTD] = both(sum_rows(66, S), sum_rows(67, S), S, F[RSTD1][:], F[RSTD][:],
                                                 left["rstd", RSTD], left["rstd", RSTD1])
    rcol = sm[:, 180:184]
    _, end["rcol"] = both(sum_columns(66, S), sum_columns(67, S), 4, sm[:, 176:180], rcol)
    def rescale():
        for i in range(KT):
            end["x", i] = stt(F[i][:], F[i][:], vcol("norm_final", i), F[RSTD1][:], ALU.mult, ALU.mult, end["rstd", RSTD1], left_x[i])
            left_x[i] = None
            yield

    end["pos"] = load("pos", F[TILES["pos"]][:].bitcast(I32), bass.AP(io["pos"].tensor, io["pos"].offset, [[0, P], [1, S]]), left["pts", 3])
    end["upa"] = load("upa", F[TILES["upa"]][:], io["gla_up"], left["pts", 3])
    def decays():
        k = fm("w_in_2", 3840, xs)
        z, upa = F[TILES["zt"]], F[TILES["upa"]]
        t = fill(z[0:64, :], 1.0, left["pts", 3])
        for o in (0, 32):
            t = tt(z[o:o + 16, :], B("dense", k)[o:o + 16, :], F[RSTD][o:o + 16, :], ALU.mult, end["dense", k], end["rstd", RSTD], t)
        left["dense", k] = t
        yield
        for i in range(4):
            for d, o in ((0, 0), (1, 32)):
                k = use("mix")
                b, x = B("mix", k), F[TILES["la"][d][i]]
                end["mix", k] = left["zt"] = mm(b[:], z[o:o + 17, W(i)], upa[o:o + 17, :], True, True, t, end["upa"], gone("mix", k))
                a = act(x[:], b[:], ACT.Abs, end["mix", k], left["pp", 3], left["w_xo"])
                a = act(x[:], x[:], ACT.Exp, a, scale=-1.0)
                a = act(x[:], x[:], ACT.Ln, a, bias=one)
                end["la", d, i] = left["mix", k] = stt(x[:], b[:], 0.0, x[:], ALU.min, ALU.subtract, a)
                yield

    def gqk_in(h):
        for name, col, sc in (("gq", 768, P ** -0.5), ("gk", 1280, 1.0)):
            k = fm("w_in_2", col + 128 * h, xs)
            end[name, h] = left["dense", k] = stt(F[TILES[name][h]][:], B("dense", k)[:], sc, F[RSTD][:], ALU.mult, ALU.mult,
                                                  end["dense", k], end["rstd", RSTD], left["w_down", 3])
            yield

    def gv_in(g):
        ks = yield from tm("w_in_2", 1792 + 512 * g, xs)
        for i, k in enumerate(ks):
            n = 4 * g + i
            end["gv", n] = left["dense", k] = act(F[TILES["gv"][n]][:], B("dense", k)[:], ACT.Identity, end["dense", k], end["rcol"],
                                                  left["w_xo"], scale=rcol[:, i:i + 1])
        yield

    def z2_of(kd):
        k = use("z")
        end["z", k] = left["dense", kd] = tt(RT("z", k)[:], B("dense", kd)[:], F[RSTD][:], ALU.mult, end["dense", kd], gone("z", k), end["rstd", RSTD])
        return k

    def gr_in(h):
        for i in (2 * h, 2 * h + 1):
            k = z2_of(fm("w_in_2", 2816 + 128 * i, xs))
            x = F[TILES["gr"][i]]
            a = act(x[:], RT("z", k)[:], ACT.Sigmoid, end["z", k], left["w_down", 3])
            end["gr", i] = left["z", k] = tt(x[:], RT("z", k)[:], x[:], ALU.mult, a)
            yield

    def gla_head(h):
        q, kk = F[TILES["gq"][h]], F[TILES["gk"][h]]
        dg, nr = F[TILES["gdiag"]], F[TILES["near"]]
        busy = (left.get(("gla work", h - 1)), left["zt"], left["acc", 66], left["acc", 67])
        place = {}
        for d, (cm, mid, last) in enumerate((("cf", 63, 127), ("cb", 64, 0))):
            e1, e2, ks, qs, fr = (F[TILES[n][d]] for n in ("e1", "e2", "ks", "qs", "far"))
            k = use("mix")
            for i in range(4):
                end["mix", k] = left["la"] = mm(B("mix", k)[:, W(i)], F[TILES["la"][d][i]][:, W(h)], C(cm), True, True, end["la", d, i], gone("mix", k))
            a1 = act(e1[:], B("mix", k)[:], ACT.Exp, end["mix", k], busy)
            a2 = left["mix", k] = act(e2[:], B("mix", k)[:], ACT.Exp, busy, scale=-1.0)
            yield
            o = 192 + 40 * h + 20 * d
            h0, h1, w, aa, cc = sm[:, o:o + 4], sm[:, o + 4:o + 8], sm[:, o + 8:o + 10], sm[:, o + 10:o + 11], sm[:, o + 11:o + 12]
            t1 = copy(h0, e1[:, mid::P], a1)
            t2 = copy(h1, e1[:, last::P], a1)
            f1 = fill(e1[:, mid::P], 1.0, t1)
            f2 = fill(e2[:, mid::P], 1.0, a2)
            if d == 0:
                t = tt(w, h1[:, 0:4:2], h0[:, 1:4:2], ALU.mult, t1, t2)
                ta = tt(aa, w[:, 0:1], h1[:, 1:2], ALU.mult, t)
                tc = tt(cc, w[:, 1:2], h0[:, 2:3], ALU.mult, t)
                near, far_k, far_q = ((0, 1, w[:, 0:1]), (2, 3, w[:, 1:2])), ((0, aa), (1, h1[:, 1:2])), ((2, h0[:, 2:3]), (3, cc))
            else:
                t = tt(w, h1[:, 1:4:2], h0[:, 0:4:2], ALU.mult, t1, t2)
                ta = tt(aa, w[:, 1:2], h1[:, 2:3], ALU.mult, t)
                tc = tt(cc, w[:, 0:1], h0[:, 1:2], ALU.mult, t)
                near, far_k, far_q = ((1, 0, w[:, 0:1]), (3, 2, w[:, 1:2])), ((2, h1[:, 2:3]), (3, aa)), ((0, cc), (1, h0[:, 1:2]))
            tq = tt(e1[:], e1[:], q[:], ALU.mult, f1, end["gq", h])
            tk = tt(e2[:], e2[:], kk[:], ALU.mult, f2, end["gk", h])
            yield
            k = use("mix")
            scores(k, e2, e1, tk, tq)
            if d == 0:
                end["gdiag"] = left["mix", k] = copy(dg[:], B("mix", k)[:], end["mix", k], busy, on=A)
            else:
                end["gdiag"] = left["mix", k] = put_where(dg[:], C("hi"), B("mix", k)[:], end["mix", k], end["gdiag"])
            yield
            for n, (i, _, c) in enumerate(near):
                t = ts(ks[:, W(n)], e2[:, W(i)], c, None, ALU.mult, None, tk, ta, tc, busy, gone("sq", uses["sq"]), gone("sq", uses["sq"] + 1))
            for n, (i, c) in enumerate(far_k):
                t = ts(ks[:, W(2 + n)], e2[:, W(i)], c, None, ALU.mult, None)
            for n, (i, c) in enumerate(far_q):
                t = ts(qs[:, W(n)], e1[:, W(i)], c, None, ALU.mult, None, tq)
            yield
            k = use("mix")
            for n, (i, j, _) in enumerate(near):
                end["mix", k] = mm(B("mix", k)[:, W(n)], ks[:, W(n)], e1[:, W(j)], True, True, t, gone("mix", k))
                place[i, j] = (nr, 2 * d + n)
            end["gnear", d] = left["mix", k] = copy(nr[:, W(d, 256)], B("mix", k)[:, 0:256], end["mix", k], busy)
            k = use("mix")
            for n, (i, _) in enumerate(far_k):
                end["mix", k] = mm(B("mix", k)[:, W(n, 256)], ks[:, W(2 + n)], qs[:, 0:256], True, True, gone("mix", k))
                for m, (j, _) in enumerate(far_q):
                    place[i, j] = (fr, 2 * n + m)
            end["gfar", d] = left["mix", k] = copy(fr[:], B("mix", k)[:], end["mix", k], busy, on=A)
            yield
        left["gqk", h] = (tq, tk)
        for i in range(4):
            place[i, i] = (dg, i)
        two = [use("out"), use("out")]
        for v, o in enumerate(two):
            for i in range(4):
                for j in range(4):
                    src, n = place[j, i]
                    m = 4 * (h // 2) + j
                    c = 256 * (h % 2) + P * v
                    end["out", o] = mm(B("out", o)[:, W(i)], F[TILES["gv"][m]][:, c:c + P], src[:, W(n)], j == 0, j == 3, end["gv", m],
                                       end["gdiag"], end["gnear", 0], end["gnear", 1], end["gfar", 0], end["gfar", 1], gone("out", o))
                if i % 2:
                    yield
        left["gla work", h] = left["gv"] = end["out", o]
        m = use("mix")
        for v, o in enumerate(two):
            x = F[TILES["ks"][v]]
            a = act(x[:], B("out", o)[:], ACT.Square, end["out", o], left["gla work", h])
            end["mix", m] = mm(B("mix", m)[:], ones, x[:], v == 0, v == 1, a, gone("mix", m))
        yield
        rb = F[TILES["qs"][0]]
        left["mix", m], t3 = rsqrt(rb[:], B("mix", m)[:], 256, end["mix", m])
        left["gla work", h] = end["mix", m]
        for v, o in enumerate(two):
            i = 2 * h + v
            y, g = F[TILES["yg"]], F[TILES["gr"][i]]
            t = left["out", o] = stt(y[:], B("out", o)[:], vcol("gla_norm_2", i), rb[:], ALU.mult, ALU.mult, t3, left.get("yg"))
            t = tt(y[:], y[:], g[:], ALU.mult, t, end["gr", i])
            y_gla.append(split(("y_gla", i), y[:], None, (TILES[("gq", "gk")[v]][h], TILES["gr"][i]), t, left["gqk", h]))
            left["yg"] = end["y_gla", i]
            yield
        left["gla work", h] = (left["gla work", h], left["out", o])

    y_gla = []
    def gla_dense():
        yield from gr_in(0)
        yield from gqk_in(1)
        yield from gr_in(1)
        yield from gv_in(1)
        yield from gqk_in(2)
        yield from gr_in(2)
        yield from gqk_in(3)
        yield from gr_in(3)

    def gla_all():
        for h in range(4):
            while ("gk", h) not in end or (h >= 2 and ("gv", 7) not in end) or ("gr", 2 * h + 1) not in end:
                yield
            yield from gla_head(h)

    def first_dense():
        yield from gqk_in(0)
        yield from gv_in(0)

    dec = decays()
    next(dec)
    weave((dec, 1), (rescale(), 1), (first_dense(), 1))
    left["yg"] = left["zt"]
    weave((gla_all(), 2), (gla_dense(), 1))

    sin, cos = F[TILES["sin"]], F[TILES["cos"]]
    def rope_tables():
        ang, n = F[TILES["pos"]], sin
        t = copy(n[:], ang[:].bitcast(I32), end["pos"], left["la"])
        t = ts(ang[:], n[:], vcol("freq"), None, ALU.mult, None, t)
        magic = 12582912.0
        t = ts(n[:], ang[:], float(np.float32(0.5 / np.pi)), magic, ALU.mult, ALU.add, t)
        t = ts(n[:], n[:], -magic, None, ALU.add, None, t)
        for c in TWO_PI:
            t = stt(ang[:], n[:], -c, ang[:], ALU.mult, ALU.add, t)
        t = ts(ang[:], ang[:], 3.1415925, -3.1415925, ALU.min, ALU.max, t)
        b = act(cos[:], ang[:], ACT.Abs, t, left["la"])
        end["sin"] = act(sin[:], ang[:], ACT.Sin, t)
        end["cos"] = act(cos[:], cos[:], ACT.Sin, b, scale=-1.0, bias=vcol("halfpi"))
        left["pos"] = end["sin"]
        yield

    def rotated(name, kd, tile, n):
        x, y = F[tile], F[TILES["rot"][n % 2]]
        t = left["dense", kd] = tt(x[:], B("dense", kd)[:], F[RSTD][:], ALU.mult, end["dense", kd], end["rstd", RSTD], left["la"], left["gv"])
        k = use("mix")
        end["mix", k] = mm(B("mix", k)[:], C("rot"), x[:], True, True, t, gone("mix", k))
        u = left["mix", k] = tt(y[:], B("mix", k)[:], sin[:], ALU.mult, end["mix", k], end["sin"], left.get(("rot", n - 2)))
        t = tt(x[:], x[:], cos[:], ALU.mult, end["mix", k], end["cos"], on=G)
        end[name] = left["rot", n] = tt(x[:], x[:], y[:], ALU.add, t, u, on=G)

    def att_in():
        yield from rope_tables()
        rotated("ak", fm("w_in_2", 512, xs), TILES["ak"], 0)
        yield
        for j in range(4):
            rotated(("aq", j), fm("w_in_2", 64 * j, xs), TILES["aq"][j], j + 1)
            yield
        kz = z2_of(fm("w_in_2", 640, xs))
        k = use("mix")
        for i in range(4):
            end["mix", k] = left["z", kz] = tr(B("mix", k)[:, W(i)], RT("z", kz)[:, W(i)], end["z", kz], gone("mix", k))
        end["av"] = left["mix", k] = copy(F[TILES["av"]][:], B("mix", k)[:], end["mix", k], left["gv"], on=A)
        yield

    def gate2_in(name, col):
        for i in range(8):
            k = z2_of(fm("w_in_2", col + 128 * i, xs))
            end[name, i] = left["z", k] = act(F[TILES[name][i]][:], RT("z", k)[:], ACT.Sigmoid, end["z", k], left["v_m"], left["pos"], left["yg"],
                                              left["gla work", 3], left["ak"] if name == "g_gla" else None)
            yield

    def attention():
        sinks = vec[:, vat["sink"]:vat["sink"] + 8]
        ak, av = F[TILES["ak"]], F[TILES["av"]]
        aq = [F[i] for i in TILES["aq"]]
        for n in range(4):
            k0, k1 = max(0, n - 1), min(3, n + 1)
            nk = k1 - k0 + 1
            o = 352 + 32 * n
            mx, nm, es, su = (sm[:, o + 8 * i:o + 8 * i + 8] for i in range(4))
            m0 = cat["hi"] + P * (k0 - n + 1)
            for j in range(4):
                ks = [use("mix"), use("mix")]
                for g, k in enumerate(ks):
                    r = W(g, 64)
                    end["mix", k] = mm(B("mix", k)[:, 0:P * nk], aq[j][r, W(n)], ak[r, P * k0:P * k1 + P], True, True,
                                       end["aq", j], end["ak"], gone("mix", k))
                for g, k in enumerate(ks):
                    hd = 4 * g + j
                    x = F[TILES["sc"][hd]]
                    t = left["mix", k] = stt(x[:, 0:P * nk], B("mix", k)[:, 0:P * nk], 0.125, cst[:, m0:m0 + P * nk], ALU.mult, ALU.subtract,
                                             end["mix", k], left.get(("sc", n - 1)), left["gv"], left["gla work", 3])
                    end["max", hd] = reduce(mx[:, hd:hd + 1], x[:, 0:P * nk], ALU.max, t)
                yield
            t = tt(mx, mx, sinks, ALU.max, end["max", 7])
            t1 = ts(nm, mx, -1.0, None, ALU.mult, None, t)
            t2 = tt(es, sinks, mx, ALU.subtract, t)
            for hd in range(8):
                x = F[TILES["sc"][hd]]
                a = act(x[:, 0:P * nk], x[:, 0:P * nk], ACT.Exp, t1, bias=nm[:, hd:hd + 1], acc=su[:, hd:hd + 1])
                if hd == 3:
                    yield
            a = act(es, es, ACT.Exp, t2)
            t = tt(su, su, es, ALU.add, a)
            t = recip(su, t)
            for hd in range(8):
                x = F[TILES["sc"][hd]]
                end["probs", hd] = ts(x[:, 0:P * nk], x[:, 0:P * nk], su[:, hd:hd + 1], None, ALU.mult, None, t)
            yield
            ob = use("out")
            for kk in range(nk):
                for g in range(2):
                    k = use("mix")
                    for j in range(4):
                        end["mix", k] = tr(B("mix", k)[:, W(j)], F[TILES["sc"][4 * g + j]][:, W(kk)], end["probs", 4 * g + j], gone("mix", k))
                    y = F[TILES["apt"][g]]
                    t = left["mix", k] = copy(y[:], B("mix", k)[:], end["mix", k], left.get(("apt", g)), left["gla work", 3], on=A if g else V)
                    c = P * (k0 + kk) + 64 * g
                    end["out", ob] = left["apt", g] = mm(B("out", ob)[W(g, 64), :], av[:, c:c + 64], y[:], kk == 0, kk == nk - 1,
                                                         t, end["av"], gone("out", ob))
                yield
            left["sc", n] = end["mix", k]
            for j in range(4):
                a = act(F[TILES["yatt"][j]][:, W(n)], B("out", ob)[:, W(j)], ACT.Copy, end["out", ob], left["gla work", 3])
            end["yatt", n] = left["out", ob] = a
            yield
        left["ak"] = (end["mix", k], end["out", ob])
        for j in range(4):
            y_att.append(split(("y_att", j), F[TILES["yatt"][j]][:], None, TILES["y_att"][j], end["yatt", 3], left["sc", 3]))

    y_att = []
    left["v_m"] = left["pt", 3]
    drain(att_in())
    weave((attention(), 2), (gate2_in("g_att", 3872), 1))
    drain(gate2_in("g_gla", 4896))
    left["xs3"] = end["dense", uses["dense"] - 1]
    left["rstd", RSTD] = end["z", uses["z"] - 1]

    pieces = []
    for p in range(8):
        for d in range(KT):
            pieces += [(w, e, d) for w in ("w_gate", "w_upx") for e in (2 * p, 2 * p + 1)]
        for d in range(KT):
            pieces += [("w_dn", e, d) for e in (2 * p, 2 * p + 1)]
    at = [tile_at[i] for i in EX_TILES[:EX_TILES_EARLY]] + [raw_at + 4096 * i for i in range(NRAW + 2 * NSPL)] \
        + [tile_at[i] for i in EX_TILES[EX_TILES_EARLY:]]
    NEX = len(at)
    ex = [nc.alloc_sbuf_tensor_at(f"ex{i}", [P, 1024], F32, offset=a) for i, a in enumerate(at)]
    sent = [0]
    def send_piece(*waits):
        n = sent[0]
        if n < len(pieces):
            w, e, d = pieces[n]
            t = ex[n % NEX]
            end["piece", n] = load(f"ex{n % NEX}", t[:], io[w][e, W(d), :], left.get(("piece", n - NEX)), waits)
            sent[0] += 1

    for c in range(4):
        for v, k in enumerate(fm_half("w_branch_attn_2", 256 * c, y_att)):
            i = 2 * c + v
            x = F[TILES["g_att"][i]]
            end["g_att", i] = left["dense", k] = tt(x[:], x[:], B("dense", k)[:], ALU.mult, end["dense", k], end["g_att", i])
    left["y_att"] = end["dense", k]
    merged = []
    for i in range(8):
        if i < 5:
            send_piece(left["y_att"], left["gv"], left["ak"])
        k = fm("w_branch_gla_2", 128 * i, y_gla)
        x, y = F[TILES["g_gla"][i]], F[TILES["g_att"][i]]
        t = left["dense", k] = tt(x[:], x[:], B("dense", k)[:], ALU.mult, end["dense", k], end["g_gla", i])
        left["g_att", i] = t = tt(x[:], x[:], y[:], ALU.add, t, end["g_att", i])
        merged.append(split(("merged", i), x[:], None, XIN[i], t, left["xs3"]))
    left["y_gla"] = end["dense", k]

    wr = F[TILES["wr"]]
    end["wr"] = load("wr", wr[:, 0:P], io["w_router"], end["y_att", 3])
    left["acc", 66] = left["g_att", 7]
    for i in range(KT):
        add_to(i, "dense", fm("w_out_2", 128 * i, merged))
        left_x[i] = add_square(66, i, F[i][:], S, end["x", i])
        if i < 6:
            send_piece(left["y_gla"])
            send_piece(left["y_gla"] if i < 2 else end["merged", 7])
    left["merged"] = end["dense", uses["dense"] - 1]
    for i in range(NRAW):
        send_piece(left["raw", nunit - NRAW + (i - nunit) % NRAW])
    for i in range(2 * NSPL):
        send_piece(left["merged"])
    rstd_row(RSTD, 66)
    hn, lgk = [F[i] for i in TILES["hn_f"]], use("out")
    for i in range(KT):
        end["hn", i] = stt(hn[i][:], F[i][:], vcol("norm_ffn_2", i), F[RSTD][:], ALU.mult, ALU.mult, end["rstd", RSTD], end["x", i], left["merged"])
        end["out", lgk] = mm(B("out", lgk)[0:16, :], wr[:, W(i, 16)], hn[i][:], i == 0, i == KT - 1, end["hn", i], end["wr"], gone("out", lgk))
        left_x[i] = (left_x[i], end["hn", i])
    left["rstd", RSTD] = end["hn", 7]
    for _ in range(NEX - sent[0]):
        send_piece(left["acc", 66], end["x", 7], left_x[7], left["z", uses["z"] - 1], end["rstd", RSTD], end["hn", 7])
    rank, aff, rank_t = (F[TILES[n]] for n in ("rank", "aff", "rank_t"))
    t = left["out", lgk] = copy(rank[0:16, :], B("out", lgk)[0:16, :], end["out", lgk], left["apt", 0], left["apt", 1])
    k = use("mix")
    for i in range(4):
        end["mix", k] = tr(B("mix", k)[:, W(i, 16)], rank[0:16, W(i)], t, gone("mix", k))
    def turn(i, v):
        o = use("out")
        for d in range(4):
            end["out", o] = tr(B("out", o)[:, W(d)], hn[4 * v + d][:, W(i)], end["hn", 4 * v + d], gone("out", o))
        end["hn_t", i, v] = left["out", o] = copy(F[TILES["hn_t"][i][v]][:], B("out", o)[:], end["out", o], left["merged"], on=A)
    for i, v in ((0, 0), (0, 1), (1, 0), (1, 1)):
        turn(i, v)
    a3, b3 = (x[:, 0:64].rearrange("p (i e) -> p i e", i=4) for x in (aff, B("mix", k)))
    m4, s4 = sm[:, 480:484], sm[:, 484:488]
    t = reduce(m4, b3, ALU.max, end["mix", k])
    t = left["mix", k] = tt(a3, b3, m4.unsqueeze(2).to_broadcast([P, 4, 16]), ALU.subtract, t, left["apt", 0], left["apt", 1])
    t = act(aff[:, 0:64], aff[:, 0:64], ACT.Exp, t)
    t = reduce(s4, a3, ALU.add, t)
    t = recip(s4, t)
    end["aff"] = tt(a3, a3, s4.unsqueeze(2).to_broadcast([P, 4, 16]), ALU.mult, t)
    k = use("mix")
    for i in range(4):
        end["mix", k] = tr(B("mix", k)[0:16, W(i)], aff[:, W(i, 16)], end["aff"], gone("mix", k))
    t = left["mix", k] = copy(rank[0:16, :], B("mix", k)[0:16, :], end["mix", k])
    for i, v in ((2, 0), (2, 1), (3, 0), (3, 1)):
        turn(i, v)
    left["hn"] = end["out", uses["out"] - 1]
    t8 = sm[0:16, 488:496]
    for r in range(8):
        t = V.do(lambda e: e.max(t8, rank[0:16, :]), t)
        t = V.do(lambda e: e.match_replace(rank[0:16, :], t8, rank[0:16, :], -1.0), t)
    t = ts(rank[0:16, :], rank[0:16, :], -0.5, None, ALU.is_lt, None, t)
    k = use("mix")
    for i in range(4):
        end["mix", k] = tr(B("mix", k)[:, W(i, 16)], rank[0:16, W(i)], t, gone("mix", k))
    t2 = left["mix", k] = copy(rank_t[:, 0:64], B("mix", k)[:, 0:64], end["mix", k], end["y_att", 0])
    k1, k2 = use("mix"), use("mix")
    for i in range(4):
        for j in range(i + 1):
            tri = C("le") if j == i else ones
            end["mix", k1] = mm(B("mix", k1)[:, W(i, 16)], tri, rank_t[:, W(j, 16)], j == 0, j == i, t2, gone("mix", k1))
            end["mix", k2] = mm(B("mix", k2)[0:16, W(i)], rank_t[:, W(j, 16)], tri, j == 0, j == i, gone("mix", k2))
    end["rank"] = left["mix", k2] = tt(rank[0:16, :], rank[0:16, :], B("mix", k2)[0:16, :], ALU.mult, end["mix", k2])
    end["rank_t"] = left["mix", k1] = tt(rank_t[:, 0:64], rank_t[:, 0:64], B("mix", k1)[:, 0:64], ALU.mult, end["mix", k1], end["mix", k2])

    first["gate"] = first["up"] = left["dense", uses["dense"] - 1]
    first["down"] = (left["mix", k1], left["mix", k2])
    def choose(p):
        pick, put = F[TILES["pick"][p % 2]], F[TILES["put"][p % 2]]
        out = pick[:].rearrange("p (i e s) -> p i e s", i=4, e=2)
        no = C("slots", 64).unsqueeze(1).unsqueeze(1).to_broadcast([P, 4, 2, 64])
        rk = rank_t[:, 0:64].rearrange("p (i e) -> p i e", i=4)[:, :, 2 * p:2 * p + 2].unsqueeze(3).to_broadcast([P, 4, 2, 64])
        end["pick", p] = tt(out, no, rk, ALU.is_equal, end["rank_t"], left.get(("pick", p - 2)), end["y_att", 3])
        for v in range(2):
            o = use("out")
            for d in range(4):
                for i in range(4):
                    end["out", o] = mm(B("out", o)[:, W(d)], F[TILES["hn_t"][i][v]][:, W(d)], pick[:, W(i)], i == 0, i == 3,
                                       end["hn_t", i, v], end["pick", p], gone("out", o))
            end["xg", p, v] = left["out", o] = copy(F[TILES["xg"][p % 2][v]][:], B("out", o)[:], end["out", o], left["hn"],
                                                    left.get(("xg", p - 2)), on=A if v else V)
        o = use("out")
        for i in range(4):
            end["out", o] = mm(B("out", o)[:, 0:2], pick[:, W(i)], aff[:, 16 * i + 2 * p:16 * i + 2 * p + 2], i == 0, i == 3, end["aff"], gone("out", o))
        left["pick", p] = end["out", o]
        ac = sm[:, 496 + p:497 + p]
        t = copy(ac[0:64], B("out", o)[0:64, 0:1], end["out", o])
        end["ac", p] = left["out", o] = copy(ac[64:128], B("out", o)[64:128, 1:2], t)
        o = use("out")
        for v in range(2):
            end["out", o] = mm(B("out", o)[W(v, 64), :], ident[0:16, 2 * p + v:2 * p + v + 1].to_broadcast([16, 64]), rank[0:16, :],
                               True, True, end["rank"], gone("out", o))
        end["put", p] = left["out", o] = ts(put[:], B("out", o)[:], vcol("slot"), None, ALU.is_equal, None, end["out", o],
                                            left.get(("put", p - 2)), left["g_att", 5])

    taken = [0]
    def expert_mm(ring, ks, lhs, w, e, d, *waits):
        n = taken[0]
        assert pieces[n] == (w, e, d)
        taken[0] += 1
        half = W(e % 2, 64)
        for f, k in enumerate(ks):
            end[ring, k] = left["piece", n] = mm(B(ring, k)[half, :], lhs[:, half], ex[n % NEX][:, W(f, S)], d == 0, d == KT - 1,
                                                 end["piece", n], gone(ring, k), waits)
        send_piece()

    def scatter(p):
        y = [F[i] for i in TILES["ey"][p % 2]]
        for d in range(KT):
            o = use("out")
            end["out", o] = mm(B("out", o)[:], y[d // 4][:, W(d % 4)], F[TILES["put"][p % 2]][:], True, True, end["ey", p], end["put", p], gone("out", o))
            add_to(d, "out", o)
            left_x[d] = None
            yield
        left["put", p] = left["ey", p] = end["out", o]

    choose(0)
    for p in range(8):
        kg, ku = [use("gate"), use("gate")], [use("up"), use("up")]
        for d in range(KT):
            xg = F[TILES["xg"][p % 2][d // 4]]
            for w, ring, ks in (("w_gate", "gate", kg), ("w_upx", "up", ku)):
                for e in (2 * p, 2 * p + 1):
                    expert_mm(ring, ks, xg[:, W(d % 4)], w, e, d, end["xg", p, d // 4])
        left["xg", p] = end["up", ku[1]]
        for f in range(2):
            x = F[TILES["eh"][f]]
            a = act(x[:], B("gate", kg[f])[:], ACT.Sigmoid, end["gate", kg[f]], left.get(("eh", p - 1)), left["hn"])
            t = left["gate", kg[f]] = tt(x[:], x[:], B("gate", kg[f])[:], ALU.mult, a)
            end["eh", f] = left["up", ku[f]] = tt(x[:], x[:], B("up", ku[f])[:], ALU.mult, t, end["up", ku[f]])
        if p > 0:
            drain(scatter(p - 1))
        if p < 7:
            choose(p + 1)
        for f in range(2):
            o = use("out")
            for c in range(4):
                end["out", o] = tr(B("out", o)[:, W(c)], F[TILES["eh"][f]][:, W(c)], end["eh", f], gone("out", o))
            end["ht", f] = left["out", o] = copy(F[TILES["ht"][f]][:], B("out", o)[:], end["out", o], left["hn"], left.get(("ht", p - 1)), on=A if f else V)
        left["eh", p] = end["out", o]
        kd = [use("down"), use("down")]
        for d in range(KT):
            ht = F[TILES["ht"][d // 4]]
            for e in (2 * p, 2 * p + 1):
                expert_mm("down", kd, ht[:, W(d % 4)], "w_dn", e, d, end["ht", d // 4])
        left["ht", p] = end["down", kd[1]]
        for f in range(2):
            end["ey", p] = left["down", kd[f]] = act(F[TILES["ey"][p % 2][f]][:], B("down", kd[f])[:], ACT.Identity, end["down", kd[f]], end["ac", p],
                                                     left.get(("ey", p - 2)), left["g_att", 3], scale=sm[:, 496 + p:497 + p])

    def piece_left(address):
        i = at.index(address)
        return left["piece", max(n for n in range(len(pieces)) if n % NEX == i)]
    def tile_left(i):
        return piece_left(tile_at[i - i % 2])
    first["dense"], uses["dense"] = (left["gate", kg[1]], left["up", ku[1]]), 0
    limit[0] = len(plan)
    for i in range(2):
        end["p", i] = load(f"x{i}", F[TILES["p"][i]][:], io["pT"][W(i)], tile_left(TILES["p"][i]))
    for u in range(nunit, nunit + NRAW):
        load_unit(u, piece_left(raw_at + 4096 * (u % NRAW)))
    for u in range(nunit, nunit + NSPL - 1):
        split_unit(u, *[piece_left(raw_at + 4096 * (NRAW + o + u % NSPL)) for o in (0, NSPL)])
    ps = [split(("ps", i), F[TILES["p"][i]][:], None, TILES["pp2"][i], end["p", i], [tile_left(t) for t in TILES["pp2"][i]]) for i in range(2)]
    for g in range(2):
        u = next_unit("w", "w_ple_2", S * g)
        for c in range(4):
            k = use("dense")
            for d, (hi, lo, name) in enumerate(ps):
                w = slice(S * d + P * c, S * d + P * c + P)
                mmq(B("dense", k)[:], his[u % NSPL][:, w], hi, d == 0, False, end["unit", u], end[name], gone("dense", k))
                mmq(B("dense", k)[:], his[u % NSPL][:, w], lo, False, False)
                (mmq if d == 0 else mm)(B("dense", k)[:], los[u % NSPL][:, w], hi, False, d == 1)
            end["dense", k] = (T.sem, T.n)
            i = 4 * g + c
            end["pw", i] = left["dense", k] = copy(F[TILES["pw"][i]][:], B("dense", k)[:], end["dense", k], tile_left(TILES["pw"][i]), on=A)
        left["unit", u] = end["dense", k]
        split_unit(u + NSPL - 1, *([piece_left(raw_at + 4096 * (NRAW + o + (u + NSPL - 1) % NSPL)) for o in (0, NSPL)] if g == 0 else []))
    sc = scatter(7)
    nxt = []
    first_acc = [tile_left(66), tile_left(68), tile_left(72)]
    for i in range(KT):
        next(sc)
        nxt.append(split(("xs4", i), F[i][:], vcol("norm_ple_2", i), XPLE[i], end["x", i], [tile_left(t) for t in XPLE[i]]))
        a = add_square(66, i, F[i][:], S, end["x", i], first_acc)
        left_x[i] = (end["xs4", i], a)
    drain(sc)
    first["mix"], uses["mix"] = end["ey", 7], 0
    rstd_row(RSTD, 66)
    for i in range(KT):
        kd = fm("w_ple_gate_2", 128 * i, nxt)
        k = use("z")
        z = RT("z", k)
        q = left["dense", kd] = tt(z[:], B("dense", kd)[:], F[RSTD][:], ALU.mult, end["dense", kd], end["rstd", RSTD], gone("z", k), tile_left(70), tile_left(72))
        a = act(z[:], z[:], ACT.Sigmoid, q)
        q = tt(z[:], z[:], F[TILES["pw"][i]][:], ALU.mult, a, end["pw", i])
        end["x", i] = left["z", k] = tt(F[i][:], F[i][:], z[:], ALU.add, q, end["x", i], left_x[i])
        add_square(67, i, F[i][:], S, end["x", i])
    rstd_row(RSTD1, 67)
    for i in range(KT):
        y = F[TILES["out"][i % 2]]
        q = stt(y[:], F[i][:], vcol("norm_final_2", i), F[RSTD1][:], ALU.mult, ALU.mult, end["rstd", RSTD1], end["x", i], left.get(("sent", i - 2)), tile_left(56))
        left["sent", i] = D.dma(channel(f"sent{i % 2}"), lambda e, y=y, i=i: e.dma_start(outs[W(i)], y[:]), q)
    D.wait(left["sent", 6], left["sent", 7])
    with nc.Block() as block:
        block.sync(lambda e: D.play(e))
        block.vector(lambda e: V.play(e))
        block.scalar(lambda e: A.play(e))
        block.gpsimd(lambda e: G.play(e))
        block.tensor(lambda e: T.play(e))



def pack(inputs):
    g = {k: np.asarray(v) for k, v in inputs.items()}
    f32 = np.float32
    w = {n: g[n][0] for n in ("w_in", "w_xkv", "w_out", "w_xq", "w_xo", "w_up", "w_down", "w_in_2", "w_branch_attn_2",
                                "w_branch_gla_2", "w_out_2", "w_ple_2", "w_ple_gate_2")}
    rows = np.concatenate([np.r_[64 * j:64 * j + 64, 256 + 64 * j:320 + 64 * j] for j in range(4)])
    w["w_branch_attn_2"] = w["w_branch_attn_2"][rows]
    plan = unit_plan()
    units = np.zeros((len(plan), P, 1024), f32)
    for u, (kind, name, k0, cols) in enumerate(plan):
        m = w[name]
        nk, nc_ = {"f": (8, 128), "t": (2, 512), "h": (4, 256), "w": (2, 512)}[kind]
        dst = units[u].reshape(P, nk, nc_)
        src = m[128 * k0:128 * (k0 + nk)].reshape(nk, P, m.shape[1])
        cols = np.asarray(cols)
        have = cols >= 0
        dst[:, :, have] = src[:, :, cols[have]].transpose(1, 0, 2)
    vat, nvc = vec_index()
    vec = np.zeros((P, nvc), f32)
    def put(name, a, off=0):
        a = np.asarray(a, dtype=f32).reshape(-1, P).T
        vec[:, vat[name] + off:vat[name] + off + a.shape[1]] = a
    for n in ("norm_mix", "norm_xattn", "norm_mem", "norm_mlp"):
        put(n, g[n][0])
    put("norm_final", g["norm_final"])
    b = g["b_in"][0]
    for n, o in (("b_q", 0), ("b_ff", 512), ("b_fb", 1024), ("b_hg", 2048), ("b_mq", 2560), ("b_mk", 3072), ("b_mo", 4096)):
        put(n, b[o:o + 512])
    for i in range(4):
        for r, o in ((i, 4608), (64 + i, 4612), (32 + i, 4616), (96 + i, 4620)):
            vec[r, vat["b_gt"]] = b[o + i]
    put("lb", g["hgrn_lb_logits"][0, 0])
    put("lb", g["hgrn_lb_logits"][1, 0], 4)
    put("hgrn_norm", g["hgrn_norm"][0])
    for j in range(5):
        put("conv_w", g["mlstm_conv_w"][0, j], 8 * j)
    put("conv_b", g["mlstm_conv_b"][0])
    put("mlstm_norm", g["mlstm_norm"][0])
    vec[:, vat["eps"]] = EPS
    for n in ("norm_mix_2", "gla_norm_2", "norm_ffn_2", "norm_ple_2"):
        put(n, g[n][0])
    put("norm_final_2", g["norm_final_2"])
    vec[:, vat["sink"]:vat["sink"] + 8] = g["attn_sink_2"][0]
    i = np.arange(P) % 64
    freq = f32(500000.0) ** (-(2 * (i % 8)).astype(f32) / f32(16))
    vec[:, vat["freq"]] = np.where(i < 16, freq, 0)
    vec[:, vat["halfpi"]] = np.pi / 2
    vec[:, vat["slot"]] = np.arange(P) % 64 + 1
    up = np.zeros((P, S), f32)
    for o, d in ((0, "fwd"), (32, "bwd")):
        up[o:o + 16] = g[f"gla_gate_up_{d}_2"][0]
        up[o + 16] = g[f"gla_gate_bias_{d}_2"][0]
    return {
        "units": units, "consts": np.concatenate(list(const_columns().values()), axis=1), "vecs": vec,
        "w_gate": g["w_exp_gate_2"][0], "w_upx": g["w_exp_up_2"][0], "w_dn": g["w_exp_down_2"][0],
        "w_router": np.ascontiguousarray(g["w_router_2"][0].reshape(8, P, 16).transpose(1, 0, 2).reshape(P, 128)),
        "pT": np.ascontiguousarray(g["p_2"][0, 0].T),
        "gla_up": up, "pos": g["positions_2"],
        "xT": np.ascontiguousarray(g["x"][0].T), "memT": np.ascontiguousarray(g["mem"][0].T), "b_in": b,
    }


def kernel(**inputs):
    import concourse.bacc as bacc
    from concourse.bass_utils import run_bass_kernel_spmd

    nc = bacc.Bacc("TRN2", target_bir_lowering=False, num_devices=1)
    arrays = pack(inputs)
    io = {k: nc.dram_tensor(k, a.shape, mybir.dt.from_np(a.dtype), kind="ExternalInput").ap() for k, a in arrays.items()}
    out = nc.dram_tensor("outT", (1024, S), F32, kind="ExternalOutput").ap()
    encoder_decoder_kernel(nc, io, out)
    r = run_bass_kernel_spmd(nc, [arrays], core_ids=[0])
    return np.ascontiguousarray(r.results[0]["outT"].T)[None]
```

```python
import numpy as np

import concourse.bass as bass
from concourse import mybir

ACT = mybir.ActivationFunctionType
ALU = mybir.AluOpType
AX = mybir.AxisListType
F32 = mybir.dt.float32
F32R = mybir.dt.float32r
I32 = mybir.dt.int32

P = 128
S = 512
KT = 8
BASE = 16512
TOP = 229344
SLOT = 2048
NRAW = 3
NSPL = 3
BIG = 1.0e30
EPS = 1e-6
TWO_PI = (6.28125, 0.0019350051879882812, float(2 * np.pi - 6.28125 - 0.0019350051879882812))



def _cols(start, n=128):
    return list(range(start, start + n))


def unit_plan():
    plan = []
    q, ff, fb, hi, hg, mq, mk, mv, mo, gt = 0, 512, 1024, 1536, 2048, 2560, 3072, 3584, 4096, 4608
    head = lambda o, h: ("f", "w_in", 0, _cols(o + 128 * h))
    tm = lambda w, c: [("t", w, 2 * u, _cols(c, 512)) for u in range(4)]
    g = [-1] * 128
    for i in range(4):
        g[i], g[64 + i], g[32 + i], g[96 + i] = gt + i, gt + 4 + i, gt + 8 + i, gt + 12 + i
    hin = lambda h: [head(q, h), head(ff, h), head(fb, h)]
    plan += hin(0) + tm("w_in", hi) + hin(1) + [head(hg, 0), ("f", "w_in", 0, g), head(hg, 1)]
    plan += hin(2) + [head(hg, 2), head(mo, 0), head(mo, 1)] + hin(3) + [head(hg, 3), head(mo, 2), head(mo, 3)]
    plan += tm("w_in", mv)
    for h in range(4):
        plan += [head(mq, h), head(mk, h)]
    fm = lambda w, c, k0=0: ("f", w, k0, _cols(128 * c))
    plan += [fm("w_xkv", c) for c in range(8)]
    for c in (1024, 1536):
        plan += tm("w_xkv", c)
    plan += [fm("w_out", c) for c in range(8)]
    plan += [fm("w_xq", c) for c in range(8)]
    plan += [fm("w_xo", c) for c in range(8)]
    for r in range(4):
        plan += [fm("w_up", 8 * r + c) for c in range(8)]
        plan += [fm("w_down", c, 8 * r) for c in range(8)]
    gla_gates = list(range(3840, 3856)) + [-1] * 16 + list(range(3856, 3872)) + [-1] * 80
    plan += [("f", "w_in_2", 0, gla_gates)]
    f2 = lambda o, n: [("f", "w_in_2", 0, _cols(o + 128 * i)) for i in range(n)]
    gin = lambda h: f2(768 + 128 * h, 1) + f2(1280 + 128 * h, 1)
    gr = lambda h: f2(2816 + 256 * h, 2)
    plan += gin(0) + tm("w_in_2", 1792) + gr(0) + gin(1) + gr(1) + tm("w_in_2", 2304) + gin(2) + gr(2) + gin(3) + gr(3)
    plan += f2(4896, 4) + f2(512, 1)
    plan += [("f", "w_in_2", 0, _cols(64 * j, 64) + _cols(64 * (4 + j), 64)) for j in range(4)]
    plan += f2(640, 1) + f2(5408, 4) + [fm("w_branch_gla_2", c) for c in range(8)] + f2(3872, 8)
    plan += [("h", "w_branch_attn_2", 0, _cols(256 * c, 256)) for c in range(4)]
    plan += [fm("w_out_2", c) for c in range(8)]
    plan += [("w", "w_ple_2", 0, _cols(512 * c, 512)) for c in range(2)]
    plan += tm("w_ple_gate_2", 0) + [fm("w_ple_gate_2", c) for c in range(4, 8)]
    return plan


TAIL = 10


def const_columns():
    p, c = np.arange(P)[:, None], np.arange(P)[None, :]
    f = lambda m: m.astype(np.float32)
    parts = {"ident": f(p == c), "ones": np.ones((P, P), np.float32)}
    parts["le"] = f(p <= c)
    parts["slots"] = np.broadcast_to(np.arange(1, 65, dtype=np.float32), (P, 64))
    for lv in range(7):
        parts[f"lev{lv}"] = f(((p >> lv) ^ (c >> lv)) == 1)
    parts["hi"] = f(p > c) * np.float32(BIG)
    parts["none"] = np.zeros((P, P), np.float32)
    parts["lo"] = f(p < c) * np.float32(BIG)
    parts["ge"] = f(p >= c)
    cf = f(p <= c) - f(p <= 63)
    cf[:, 63] = np.arange(P) <= 63
    cb = f(p >= c) - f(p >= 64)
    cb[:, 64] = np.arange(P) >= 64
    parts["cf"], parts["cb"] = cf / np.float32(16), cb / np.float32(16)
    rot = np.zeros((P, P), np.float32)
    for o in (0, 64):
        for i in range(8):
            rot[o + i + 8, o + i], rot[o + i, o + i + 8] = -1, 1
    parts["rot"] = rot
    return parts


def const_index():
    at, n = {}, 0
    for k, v in const_columns().items():
        at[k] = n
        n += v.shape[1]
    return at, n


VECS = [("norm_mix", 8), ("norm_xattn", 8), ("norm_mem", 8), ("norm_mlp", 8), ("norm_final", 8),
        ("b_q", 4), ("b_ff", 4), ("b_fb", 4), ("b_hg", 4), ("b_mq", 4), ("b_mk", 4), ("b_mo", 4), ("b_gt", 1),
        ("lb", 8), ("hgrn_norm", 4), ("conv_w", 40), ("conv_b", 8), ("mlstm_norm", 4), ("eps", 1),
        ("norm_mix_2", 8), ("gla_norm_2", 8), ("norm_ffn_2", 8), ("norm_ple_2", 8), ("norm_final_2", 8), ("sink", 8),
        ("freq", 1), ("halfpi", 1), ("slot", 1)]


def vec_index():
    at, n = {}, 0
    for k, w in VECS:
        at[k] = n
        n += w
    return at, n



def flat(x):
    if x is None:
        return []
    if isinstance(x, tuple) and len(x) == 2 and isinstance(x[1], int):
        return [x]
    return [t for y in x for t in flat(y)]


class Lane:

    def __init__(self, nc, name):
        self.nc, self.name, self.ops, self.n, self.k, self.sem = nc, name, [], 0, 0, None
        self.clock = 0.0
        self.table = None

    def pace(self, waits, cost):
        self.clock = max([self.clock] + [ENDS.get((s.num, v), 0.0) + 60 for s, v in flat(waits)]) + cost
        return self.clock

    def do(self, fn, *waits, cost=200):
        if self.sem is None or self.n == 4000:
            self.sem, self.n, self.k = self.nc.alloc_semaphore(f"{self.name}{self.k}"), 0, self.k + 1
        self.n += 1
        self.ops.append((fn, flat(waits), self.sem, 1))
        ENDS[self.sem.num, self.n] = self.pace(waits, cost)
        return (self.sem, self.n)

    def quiet(self, fn, *waits, cost=200):
        self.ops.append((fn, flat(waits), None, 0))
        self.pace(waits, cost)

    def dma(self, ch, fn, *waits, cost=1450):
        ch.n += 16
        self.ops.append((fn, flat(waits), ch.sem, 16))
        ENDS[ch.sem.num, ch.n] = self.pace(waits, cost) + 2000
        return (ch.sem, ch.n)

    def wait(self, *waits):
        self.ops.append((None, flat(waits), None, 0))

    def play(self, e):
        seen = {}
        for fn, waits, sem, inc in self.ops:
            for s, v in waits:
                if v > seen.get(s.num, 0):
                    e.wait_ge(s, v)
                    seen[s.num] = v
            if fn is not None:
                ins = fn(e)
                if sem is not None:
                    ins.then_inc(sem, inc)


class Table:

    def __init__(self, lane, ids):
        self.lane, self.ids = lane, ids

    @property
    def clock(self):
        return self.lane.clock + (0 if self.lane.table in self.ids else 1300)


class Channel:

    def __init__(self, nc, name):
        self.sem, self.n = nc.alloc_semaphore(name), 0


ENDS = {}


class Jobs:

    def __init__(self):
        self.jobs = []

    def step(self, job):
        job[2] = next(job[1], "end")
        if job[2] == "end":
            self.jobs.remove(job)

    def add(self, rank, g):
        job = [rank, g, None]
        self.jobs.append(job)
        self.jobs.sort(key=lambda x: x[0])
        self.step(job)
        return job

    def start(self, job):
        lane, *waits = job[2]
        return max([lane.clock] + [ENDS[s.num, v] + 60 for s, v in flat(waits)])

    def run(self, *gens):
        mine = [self.add(2 + i, g) for i, g in enumerate(gens)] or None
        while any(x in self.jobs for x in mine) if mine else self.jobs:
            for x in [x for x in self.jobs if x[2] is False]:
                self.step(x)
            ready = [x for x in self.jobs if x[2] is not False]
            assert ready or not self.jobs, "each waits for another"
            if ready:
                self.step(min(ready, key=self.start))



TILES = {
    "y_h": [(24 + 2 * h, 25 + 2 * h) for h in range(4)],
    "v_h": [32, 33, 34, 35], "hg": [36, 37, 38, 39], "mo": [40, 41, 42, 43],
    "hin": [[48, 49, 50, 51, 52], [53, 54, 55, 56, 57]],
    "qf": 58, "kc": 59, "qc": 60, "t2": [61, 62], "diag": 63, "yh": 64,
    "gates": [44, 45, 46, 47, 65],
    "q": [48, 50, 53, 55], "k": [49, 51, 54, 56], "conv": [66, 67],
    "mb": [32, 33], "md": [34, 35], "pt": [36, 37, 38, 39, 58], "hn": 59, "junk": 60, "ym": 61,
    "y_m": [(48, 49), (50, 51), (53, 54), (55, 56)],
    "mem": [62, 63, 64, 65], "memn": [8, 9, 10, 11, 12, 13, 14, 15], "kx": [44, 45, 52, 57], "vx": [64, 65, 62, 63],
    "qx": [32, 33, 34, 35, 36, 37, 38, 39], "pp": [40, 41, 42, 43], "pts": [58, 59, 60, 61],
    "xo": [(24, 25), (26, 27), (28, 29), (30, 31), (48, 49), (50, 51), (53, 54), (55, 56)],
    "hid": [(24 + 2 * i, 25 + 2 * i) for i in range(8)],
    "la": [[40, 41, 42, 43], [44, 45, 46, 47]], "gq": [24, 25, 26, 27], "gk": [28, 29, 30, 31],
    "gr": [32, 33, 34, 35, 36, 37, 38, 39], "gv": [48, 49, 50, 51, 52, 53, 54, 55],
    "e1": [56, 66], "e2": [57, 67], "ks": [58, 68], "qs": [59, 69], "near": 60, "far": [61, 62], "gdiag": 63, "yg": 64,
    "dt": [56, 57, 58, 59, 60, 61, 62, 75], "zt": 63, "upa": 64, "pos": 65,
    "sin": 40, "cos": 41, "rot": [42, 43], "ak": 44, "aq": [45, 46, 47, 48], "av": 49,
    "sc": [50, 51, 52, 53, 54, 55, 56, 57], "apt": [58, 59], "y_att": (60, 40),
    "g_gla": [75, 76, 77, 78, 64, 65, 66, 67], "g_att": [32, 33, 34, 35, 36, 37, 38, 39],
    "hn_f": [8, 9, 10, 11, 12, 13, 14, 15], "hn_t": [(16, 17), (18, 19), (20, 21), (22, 23)],
    "rank": 74, "pick": 60,
    "xg": [(8, 9), (10, 11)], "ht": (12, 13), "eh": (14, 15), "put": 61, "ey": (62, 63),
    "p": [24, 25], "ps": [(26, 27), (28, 29)], "pw": [30, 31, 44, 45, 46, 47, 48, 49],
    "xs4": [(24, 25), (26, 27), (28, 29), (32, 33), (34, 35), (36, 37), (38, 39), (40, 41)],
    "out": [50, 51, 52, 53, 54, 55, 56, 57],
}
XIN = [(8 + 2 * i, 9 + 2 * i) for i in range(8)]
RSTD, RSTD1 = 74, 73
BANKS = {"dense": [0, 1, 2, 3], "mix": [4, 5], "out": [6, 7], "gate": [0, 1], "up": [2, 3], "down": [4, 5]}
RINGS = {"z": [70, 71, 72], "sq": [68, 69]}
EX_EARLY = [24, 26, 28, 30] + list(range(44, 60, 2)) + ["cst", 40, 42, 32, 34, 36, 38, 64, 75, 77]
EX_LATE = [66, 68, 70, 72]
EX_FIRST = EX_EARLY + [("w", i) for i in range(NRAW + 2 * NSPL)] + EX_LATE
EX_SWITCH, EX_END = 312, 352
EX_LAST = [42, 32, 34, 36, 38, 66, 68, 70, 72, 50, 52, 54, 56, 40, 58, "cst", 64, 75, 77]
EX_NEW = [16, 18, 20, 22]
EX_FINAL = [42, 50, 52, 54, 56, 58, "cst", 64, 75, 77] + EX_NEW


def encoder_decoder_kernel(nc, io, outs):
    T, V, A, G, D = (Lane(nc, n) for n in ("pe", "dve", "act", "pool", "sp"))
    SIG, EXP, LN, SIN = (Table(A, x) for x in ((2,), (6,), (5,), (9,)))
    TABLES = {ACT.Sigmoid: SIG, ACT.Exp: EXP, ACT.Ln: EXP, ACT.Sin: SIN}
    cat, ncc = const_index()
    vat, nvc = vec_index()
    W = lambda i, n=P: slice(n * i, n * i + n)

    top = BASE
    def region(name, cols, dt=F32):
        nonlocal top
        t = nc.alloc_sbuf_tensor_at(name, [P, cols], dt, offset=top)
        top += -(-cols * 4 // 32) * 32
        return t

    cst_at = top
    cst = region("cst", ncc)
    vec = region("vec", nvc)
    sm = region("sm", 528)
    wide_at = top
    wide = region("wide", 4 * 4 * 129)
    raw_at = top
    raws = [region(f"raw{i}", 1024) for i in range(NRAW)]
    his = [region(f"whi{i}", 1024, F32R) for i in range(NSPL)]
    los = [region(f"wlo{i}", 1024, F32R) for i in range(NSPL)]
    tile_at = [top + SLOT * i for i in range(75)] + [wide_at + SLOT * i for i in range(4)]
    assert tile_at[74] + SLOT <= TOP
    F = [nc.alloc_sbuf_tensor_at(f"t{i}", [P, S], F32, offset=a) for i, a in enumerate(tile_at)]
    R = [nc.alloc_sbuf_tensor_at(f"t{i}r", [P, S], F32R, offset=a) for i, a in enumerate(tile_at)]
    bank = [nc.alloc_psum_tensor(f"bank{i}", [P, S], F32) for i in range(8)]

    C = lambda k, n=P: cst[:, cat[k]:cat[k] + n]
    vcol = lambda k, i=0: vec[:, vat[k] + i:vat[k] + i + 1]
    ident, ones, one, eps = C("ident"), C("ones"), C("ones", 1), vcol("eps")

    end, left = {}, {}

    uses = dict.fromkeys(list(BANKS) + list(RINGS), 0)
    first = {}
    def use(ring):
        uses[ring] += 1
        return uses[ring] - 1

    def gone(ring, k):
        n = len(BANKS.get(ring) or RINGS[ring])
        return left[ring, k - n] if k >= n else first.get(ring)

    jobs = Jobs()
    def spawn(g, rank=0):
        jobs.add(rank, g)

    def freed(*names):
        while any(n not in left for n in names):
            yield False

    def known(*names):
        while any(n not in end for n in names):
            yield False

    def turn(ring, *waits, lane=T, n=None):
        size, c = len(BANKS.get(ring) or RINGS[ring]), n or 1
        while True:
            k = uses[ring]
            if any(x >= size and (ring, x - size) not in left for x in range(k, k + c)):
                yield False
                continue
            yield lane, [gone(ring, x) for x in range(k, k + c)], waits
            if uses[ring] == k:
                ks = [use(ring) for _ in range(c)]
                return ks if n else ks[0]

    def B(ring, k):
        return bank[BANKS[ring][k % len(BANKS[ring])]]

    def RT(ring, k):
        return F[RINGS[ring][k % len(RINGS[ring])]]

    channels = {}
    def channel(name):
        if name not in channels:
            channels[name] = Channel(nc, name)
        return channels[name]

    def load(name, dst, src, *waits):
        return D.dma(channel(name), lambda e: e.dma_start(dst, src), *waits, cost=100 + 1.32 * size(dst))

    def size(ap):
        return int(np.prod(ap.shape[1:]))

    def mm_cost(out, rhs):
        return 0.42 * size(rhs) if rhs.dtype == F32R else max(220, 1.67 * size(rhs)) / (2 if out.shape[0] <= 64 else 1)

    def use_table(table):
        if table and A.table not in table.ids:
            A.table = table.ids[0]
            A.quiet(lambda e, t=A.table: e.add_instruction(mybir.InstLoadActFuncSet(
                name=nc.get_next_instruction_name(), engine=e.engine, act_func_set_id=t, ins=[], outs=[])), cost=1300)

    def act(out, in_, fn, *waits, bias=None, scale=None, acc=None, table=None):
        use_table(table or TABLES.get(fn))
        kw = {k: v for k, v in (("bias", bias), ("scale", scale), ("accum_out", acc)) if v is not None}
        return A.do(lambda e: e.activation(out, in_, fn, **kw), *waits, cost=100 + 0.83 * size(out))

    def tt(out, a, b, op, *waits, on=V):
        return on.do(lambda e: e.tensor_tensor(out, a, b, op), *waits, cost=70 + (1.04 if on is V else 2.2) * size(out))

    def ts(out, a, s1, s2, o0, o1, *waits, on=V):
        if o1 is None:
            return on.do(lambda e: e.tensor_scalar(out, a, s1, None, o0), *waits, cost=70 + 0.52 * size(out))
        return on.do(lambda e: e.tensor_scalar(out, a, s1, s2, o0, o1), *waits, cost=70 + 0.52 * size(out))

    def stt(out, a, s, b, o0, o1, *waits):
        return V.do(lambda e: e.scalar_tensor_tensor(out=out, in0=a, scalar=s, in1=b, op0=o0, op1=o1), *waits, cost=130 + 1.04 * size(out))

    def mm(out, lhsT, rhs, start, stop, *waits):
        return T.do(lambda e: e.matmul(out, lhsT, rhs, start=start, stop=stop), *waits, cost=mm_cost(out, rhs))

    def mmq(out, lhsT, rhs, start, stop, *waits):
        T.quiet(lambda e: e.matmul(out, lhsT, rhs, start=start, stop=stop), *waits, cost=mm_cost(out, rhs))

    def tr(out, in_, *waits):
        n = in_.shape[0]
        return T.do(lambda e: e.transpose(out, in_, ident[0:n, 0:n]), *waits)

    def recip(x, *waits):
        return V.do(lambda e: e.reciprocal(x, x), *waits)

    def reduce(out, in_, op, *waits):
        return V.do(lambda e: e.tensor_reduce(out, in_, AX.X, op), *waits, cost=70 + 1.04 * size(in_))

    def copy(out, in_, *waits, on=V):
        if on is A:
            return act(out, in_, ACT.Copy, *waits)
        return on.do(lambda e: e.tensor_copy(out, in_), *waits, cost=70 + 1.04 * size(out))

    def put(out, x, *waits):
        return V.do(lambda e: e.memset(out, x), *waits)

    def put_where(dst, mask, src, *waits):
        m = mask.bitcast(I32).unsqueeze(1).to_broadcast([P, 4, P])
        d, s = (x.rearrange("p (c t) -> p c t", c=4) for x in (dst, src))
        return V.do(lambda e: e.copy_predicated(d, m, s), *waits, cost=600)

    plan = unit_plan()
    nunit = len(plan) - TAIL

    def load_unit(u, *waits):
        r = raws[u % NRAW]
        end["raw", u] = load(f"raw{u % NRAW}", r[:], io["units"][u], left.get(("raw", u - NRAW)), waits)

    def split_unit(u, *waits):
        r, h, l = raws[u % NRAW], his[u % NSPL], los[u % NSPL]
        yield A, end["raw", u], left.get(("unit", u - NSPL)), waits
        a = act(h[:], r[:], ACT.Copy, end["raw", u], left.get(("unit", u - NSPL)), waits)
        yield V, a
        b = tt(l[:], r[:], h[:].bitcast(F32), ALU.subtract, a)
        end["unit", u] = left["raw", u] = (a, b)
        if u < nunit - NRAW or nunit <= u < len(plan) - NRAW:
            spawn(load_next(u + NRAW))

    def load_next(u):
        while u >= len(plan) - 2 and sent[0] < len(pieces):
            yield False
        load_unit(u)

    def split_units():
        for u in range(nunit):
            while u >= NSPL and ("unit", u - NSPL) not in left:
                yield False
            yield from split_unit(u)

    cur = [0]
    def next_unit(kind, weight, first_col):
        u = cur[0]
        k = plan[u]
        assert k[0] == kind and k[1] == weight and (first_col is None or k[3][0] == first_col), (u, k[:3], k[3][0])
        cur[0] += 1
        return u

    def fm(weight, col, ins, n=S):
        u = next_unit("f", weight, col)
        yield from known(("unit", u))
        k = yield from turn("dense", end["unit", u])
        wh, wl, o = his[u % NSPL], los[u % NSPL], B("dense", k)[:, 0:n]
        for d in range(KT):
            hi, lo, name = ins[d]
            yield from known(name)
            if d % 2 == 0:
                yield T, end["unit", u], end[name]
            mmq(o, wh[:, W(d)], hi, d == 0, False, gone("dense", k), end["unit", u], end[name])
            mmq(o, wh[:, W(d)], lo, False, False)
            (mmq if d < KT - 1 else mm)(o, wl[:, W(d)], hi, False, d == KT - 1)
        end["dense", k] = left["unit", u] = (T.sem, T.n)
        return k

    def fm_half(weight, col, ins):
        u = next_unit("h", weight, col)
        wh, wl, ks = his[u % NSPL], los[u % NSPL], []
        yield from known(("unit", u))
        for c in range(2):
            k = yield from turn("dense", end["unit", u])
            o = B("dense", k)[:]
            for d in range(4):
                hi, lo, name = ins[d]
                yield from known(name)
                if d % 2 == 0:
                    yield T, end["unit", u], end[name]
                w = slice(256 * d + P * c, 256 * d + P * c + P)
                mmq(o, wh[:, w], hi, d == 0, False, gone("dense", k), end["unit", u], end[name])
                mmq(o, wh[:, w], lo, False, False)
                (mmq if d < 3 else mm)(o, wl[:, w], hi, False, d == 3)
            end["dense", k] = (T.sem, T.n)
            ks.append(k)
        left["unit", u] = end["dense", k]
        return ks

    def tm(weight, col, ins, nt=4):
        ks = []
        for g in range(4):
            u = next_unit("t", weight, col)
            wh, wl = his[u % NSPL], los[u % NSPL]
            yield from known(("unit", u), ins[2 * g + 1][2])
            for i in range(nt):
                if g == 0:
                    ks.append((yield from turn("dense", end["unit", u], end[ins[1][2]])))
                else:
                    yield T, end["unit", u], end[ins[2 * g + 1][2]]
                k = ks[i]
                o = B("dense", k)[:]
                for kk in range(2):
                    d = 2 * g + kk
                    hi, lo, name = ins[d]
                    mmq(o, hi[:, W(i)], wh[:, W(kk, S)], d == 0, False, gone("dense", k), end["unit", u], end[name])
                    mmq(o, lo[:, W(i)], wh[:, W(kk, S)], False, False)
                    end["dense", k] = mm(o, hi[:, W(i)], wl[:, W(kk, S)], False, d == KT - 1)
            left["unit", u] = end["dense", k]
        return ks

    def pair(name, places, n=S):
        return (R[places[0]][:, 0:n], R[places[1]][:, 0:n], name)

    def split(dst, src, gain, *waits):
        h, l, name = dst
        yield A, waits
        if gain is None:
            a = act(h, src, ACT.Copy, waits)
            yield V, a
            b = tt(l, src, h.bitcast(F32), ALU.subtract, a, waits)
        else:
            a = act(h, src, ACT.Identity, waits, scale=gain)
            yield V, a
            b = stt(l, src, gain, h.bitcast(F32), ALU.mult, ALU.subtract, a, waits)
        end[name] = (a, b)

    def add_square(tag, acc, i, src, *waits, scale=None, free=()):
        n = src.shape[1]
        if i == 0:
            yield from freed(*free)
            w = [left[x] for x in free]
            yield A, w, waits
            end["acc", tag] = end["sq", tag, 0] = act(F[acc][:, 0:n], src, ACT.Square, w, waits, scale=scale)
            counted[tag] = 1
            return
        k = yield from turn("sq", waits, lane=A)
        sq = RT("sq", k)[:, 0:n]
        a = end["sq", tag, i] = act(sq, src, ACT.Square, gone("sq", k), waits, scale=scale)
        while counted.get(tag, 0) != i:
            yield False
        yield G, a, end["acc", tag]
        end["acc", tag] = left["sq", k] = tt(F[acc][:, 0:n], F[acc][:, 0:n], sq, ALU.add, a, end["acc", tag], on=G)
        counted[tag] = i + 1

    counted = {}
    def summed(*tags):
        while any(counted.get(t, 0) < KT for t in tags):
            yield False

    def refine(y, v, n, w, *waits):
        t = stt(w, v, n * EPS, y, ALU.add, ALU.mult, *waits)
        t = stt(w, w, -0.5 / n, y, ALU.mult, ALU.mult, t)
        return stt(y, w, 1.5, y, ALU.add, ALU.mult, t)

    def rstd_row(name, tile, tag, acc, n=S):
        yield from summed(tag)
        k = yield from turn("mix", end["acc", tag])
        end["mix", k] = left["acc", tag] = mm(B("mix", k)[:, 0:n], ones, F[acc][:, 0:n], True, True, gone("mix", k), end["acc", tag], end["cst"])
        yield EXP, end["mix", k], left.get(("rstd", tile))
        a = left["mix", k] = act(F[tile][:, 0:n], B("mix", k)[:, 0:n], ACT.Ln, end["mix", k], left.get(("rstd", tile)),
                                 scale=1.0 / 1024, bias=eps)
        end[name] = act(F[tile][:, 0:n], F[tile][:, 0:n], ACT.Exp, a, scale=-0.5)

    def rstd_column(name, out, tag, acc):
        yield from summed(tag)
        k = yield from turn("mix", end["acc", tag])
        n = out.shape[1]
        for i in range(n):
            t = mm(B("mix", k)[:, i:i + 1], F[acc][:, W(i)], one, True, True, gone("mix", k), end["acc", tag], end["cst"])
        end["mix", k] = left["acc", tag] = t
        yield EXP, t
        a = left["mix", k] = act(out, B("mix", k)[:, 0:n], ACT.Ln, t, scale=1.0 / 1024, bias=eps)
        end[name] = act(out, out, ACT.Exp, a, scale=-0.5)

    use_table(EXP)
    end["vec"] = load("vec", vec[:], io["vecs"])
    xt = io["xT"]
    for i in range(KT):
        end["x", i] = load(f"x{i}", F[i][:], xt[W(i)])
        if i in (0, 4, 7):
            load_unit((0, 4, 7).index(i))
    end["cst"] = load("cst", cst[:], io["consts"])
    def bias_rows(name, tile, start):
        src = bass.AP(io["b_in"].tensor, io["b_in"].offset + start, [[0, P], [1, S]])
        end[name] = load(name, F[tile][:], src)
    bias_rows("b_hi", 46, 1536)
    bias_rows("b_mv", 67, 3584)

    xs = [pair(("xs", i), XIN[i]) for i in range(KT)]
    spawn(split_units(), 1)
    for i in range(KT):
        spawn(split(xs[i], F[i][:], vcol("norm_mix", i), end["x", i], end["vec"]))
    for i in range(KT):
        spawn(add_square("x", 66, i, F[i][:], end["x", i]), 4)

    nb, e0, lb, oml = sm[:, 0:8], sm[:, 8:16], sm[:, 16:24], sm[:, 24:32]
    def bounds():
        lbv = vec[:, vat["lb"]:vat["lb"] + 8]
        yield V, end["x", 7]
        end["nb"] = ts(nb, vec[:, vat["b_ff"]:vat["b_ff"] + 8], -1.0, None, ALU.mult, None, end["vec"])
        t = tt(e0, lbv, lbv, ALU.subtract, end["vec"])
        t = act(e0, e0, ACT.Exp, t)
        yield V, t
        t = copy(lb, e0, t)
        t = recip(lb, t)
        t = tt(e0, e0, lb, ALU.mult, t)
        t = tt(lb, e0, e0, ALU.subtract, t)
        end["lb"] = ts(oml, lb, -1.0, 1.0, ALU.mult, ALU.add, t)
    spawn(bounds())

    rcol = sm[:, 32:36]
    spawn(rstd_row("rstd", RSTD, "x", 66))
    spawn(rstd_column("rcol", rcol, "x", 66))
    rbc = F[RSTD]

    def z_of(kd, rstd="rstd"):
        yield from known(rstd)
        k = yield from turn("z", end["dense", kd], end[rstd], lane=V)
        end["z", k] = left["dense", kd] = left["rstd", RSTD] = tt(RT("z", k)[:], B("dense", kd)[:], rbc[:], ALU.mult, end["dense", kd], gone("z", k), end[rstd])
        return k

    def silu_of(name, kd, bias, tile, *free):
        yield from freed(*free)
        w = [left[x] for x in free]
        k = yield from z_of(kd)
        yield SIG, end["z", k], w
        a = act(F[tile][:], RT("z", k)[:], ACT.Sigmoid, end["z", k], w, bias=bias)
        yield V, a
        end[name] = left["z", k] = stt(F[tile][:], RT("z", k)[:], bias, F[tile][:], ALU.add, ALU.mult, a)

    def forget_of(d, h, kd):
        f, kf, bias, tf, tk = (("f", "kf", "b_ff", 1, 3), ("g", "kb", "b_fb", 2, 4))[d]
        tf, tk, j = TILES["hin"][h % 2][tf], TILES["hin"][h % 2][tk], 4 * d + h
        yield from freed(*[("hin", x) for x in (h - 2,) if x >= 0])
        k = yield from z_of(kd)
        yield SIG, end["z", k], left.get(("hin", h - 2))
        a = act(F[tf][:], RT("z", k)[:], ACT.Sigmoid, end["z", k], left.get(("hin", h - 2)), bias=vcol(bias, h))
        b = left["z", k] = act(F[tk][:], RT("z", k)[:], ACT.Sigmoid, end["nb"], bias=nb[:, j:j + 1], scale=-1.0)
        yield V, a
        end[f, h] = ts(F[tf][:], F[tf][:], oml[:, j:j + 1], lb[:, j:j + 1], ALU.mult, ALU.add, a, end["lb"])
        yield V, b
        end[kf, h] = ts(F[tk][:], F[tk][:], oml[:, j:j + 1], None, ALU.mult, None, b)

    def hgrn_in(h):
        kd = yield from fm("w_in", 128 * h, xs)
        spawn(silu_of(("q", h), kd, vcol("b_q", h), TILES["hin"][h % 2][0], *[("hin", x) for x in (h - 2,) if x >= 0]))
        for d in range(2):
            kd = yield from fm("w_in", 512 * (d + 1) + 128 * h, xs)
            spawn(forget_of(d, h, kd))

    def v_of(ks):
        yield from known("rcol")
        for i, k in enumerate(ks):
            yield V, end["dense", k], end["b_hi"], end["rcol"]
            end["v_h", i] = left["dense", k] = stt(F[TILES["v_h"][i]][:], B("dense", k)[:], rcol[:, i:i + 1], F[46][:],
                                                   ALU.mult, ALU.add, end["dense", k], end["b_hi"], end["rcol"])
        left["b_hi"] = end["v_h", 3]

    vw = wide[:].rearrange("p (i h e) -> p i h e", i=4, h=4)
    end["vw ones"] = put(vw[:, :, :, 128:129], 1.0)
    def vm_of(ks):
        for i, k in enumerate(ks):
            yield V, end["dense", k], end["b_mv"], end["rcol"]
            end["v_m", i] = left["dense", k] = stt(
                vw[:, i, :, 0:128], B("dense", k)[:].rearrange("p (h e) -> p h e", h=4), rcol[:, i:i + 1],
                F[67][:].rearrange("p (h e) -> p h e", h=4), ALU.mult, ALU.add, end["dense", k], end["b_mv"], end["vw ones"])
        left["b_mv"] = end["v_m", 3]

    def blocks(ap, size):
        v = ap.rearrange("p (b two l) -> p b two l", two=2, l=size)
        return v[:, :, 0, :], v[:, :, 1, :]

    def scores(k, K, Q, *waits):
        for c in range(4):
            end["mix", k] = mm(B("mix", k)[:, W(c)], K[:, W(c)], Q[:, W(c)], True, True, gone("mix", k), waits)

    def keep_level(h, lv, k):
        yield from known(("diag", h, lv - 1))
        yield V, end["mix", k], end["diag", h, lv - 1]
        end["diag", h, lv] = left["mix", k] = put_where(F[TILES["diag"]][:], C(f"lev{lv}"), B("mix", k)[:], end["mix", k], end["diag", h, lv - 1])

    def hgrn_head(h):
        tq, tf, tg, tkf, tkb = TILES["hin"][h % 2]
        q, f, g, kf, kb = (F[i] for i in (tq, tf, tg, tkf, tkb))
        qf, kc, qc, dg = (F[TILES[n]] for n in ("qf", "kc", "qc", "diag"))
        qb = q
        free_work = left.get(("hgrn work", h - 1))
        yield V, end["kf", h], end["kb", h], free_work
        t = tt(kc[:], kf[:], kb[:], ALU.add, end["kf", h], end["kb", h], free_work)
        k = yield from turn("mix", t, end["q", h])
        scores(k, kc, q, t, end["q", h])
        read = end["mix", k]
        yield V, end["f", h]
        s_qf = tt(qf[:], q[:], f[:], ALU.mult, end["q", h], end["f", h], free_work)
        yield A, read
        end["diag", h, -1] = left["mix", k] = copy(dg[:], B("mix", k)[:], end["mix", k], free_work, on=A)
        yield V, read, end["g", h]
        s_qb = tt(q[:], q[:], g[:], ALU.mult, end["g", h], s_qf, read)
        s_kf, s_kb = end["kf", h], end["kb", h]
        df, db, s_df, s_db = f[:], g[:], end["f", h], end["g", h]
        size = 1
        while size < P:
            (qfe, qfo), (qbe, qbo), (kfe, kfo), (kbe, kbo) = (blocks(x[:], size) for x in (qf, qb, kf, kb))
            (qce, qco), (kce, kco) = (blocks(x[:], size) for x in (qc, kc))
            yield A, s_qf, read
            c_qf = act(qco, qfo, ACT.Copy, s_qf, read, free_work)
            c_kf = act(kce, kfe, ACT.Copy, s_kf)
            c_qb = act(qce, qbe, ACT.Copy, s_qb)
            c_kb = act(kco, kbo, ACT.Copy, s_kb)
            n = S // (2 * size)
            lv = size.bit_length() - 1
            t2 = F[TILES["t2"][lv % 2]]
            (dfe, dfo), (dbe, dbo) = blocks(df, 1), blocks(db, 1)
            line = lambda x: x.rearrange("p b l -> p (b l)")
            over = lambda x: x.to_broadcast([P, n, size])
            yield V, c_qf, s_kb
            n_df = tt(t2[:, 0:n], line(dfe), line(dfo), ALU.mult, s_df, s_kb, free_work)
            n_db = tt(t2[:, 256:256 + n], line(dbe), line(dbo), ALU.mult, s_db)
            s_qf = tt(qfo, qfo, over(dfe), ALU.mult, s_qf, s_df, c_qf)
            s_kf = tt(kfe, kfe, over(dfo), ALU.mult, s_kf, c_kf)
            s_qb = tt(qbe, qbe, over(dbo), ALU.mult, s_qb, s_db, c_qb)
            s_kb = tt(kbo, kbo, over(dbe), ALU.mult, s_kb, c_kb)
            k = yield from turn("mix", c_kb)
            scores(k, kc, qc, c_kb)
            read = end["mix", k]
            spawn(keep_level(h, lv, k))
            df, db, s_df, s_db = t2[:, 0:n], t2[:, 256:256 + n], n_df, n_db
            size *= 2
        place = {}
        near = ((0, 1, kf, qf), (2, 3, kf, qf), (1, 0, kb, qb), (3, 2, kb, qb))
        k = yield from turn("mix", s_qf, s_kb)
        for n, (ks, qt, K, Q) in enumerate(near):
            end["mix", k] = mm(B("mix", k)[:, W(n)], K[:, W(ks)], Q[:, W(qt)], True, True, s_qf, s_qb, s_kf, s_kb, gone("mix", k))
            place[ks, qt] = (F[TILES["t2"][1]], n)
        near_read = end["mix", k]
        yield A, near_read
        end["near"] = left["mix", k] = copy(F[TILES["t2"][1]][:], B("mix", k)[:], near_read, s_qf, s_kf, s_qb, s_kb, on=A)
        yield V, near_read
        u = [tt(qf[:, W(3)], qf[:, W(3)], df[:, 2:3].to_broadcast([P, P]), ALU.mult, near_read, s_df),
             tt(kf[:, W(0)], kf[:, W(0)], df[:, 1:2].to_broadcast([P, P]), ALU.mult),
             tt(qb[:, W(0)], qb[:, W(0)], db[:, 1:2].to_broadcast([P, P]), ALU.mult, s_db),
             tt(kb[:, W(3)], kb[:, W(3)], db[:, 2:3].to_broadcast([P, P]), ALU.mult)]
        for m, (K, Q, s0, t0, dst) in enumerate(((kf, qf, 0, 2, kc), (kb, qb, 2, 0, qc))):
            k = yield from turn("mix", u)
            for j in range(2):
                end["mix", k] = mm(B("mix", k)[:, W(j, 256)], K[:, W(s0 + j)], Q[:, P * t0:P * t0 + 256], True, True, u, gone("mix", k))
                for i in range(2):
                    place[s0 + j, t0 + i] = (dst, 2 * j + i)
            far_read = end["mix", k]
            yield A, far_read
            end["far", m] = left["mix", k] = copy(dst[:], B("mix", k)[:], far_read, read, on=A)
        left["hin", h] = far_read
        for i in range(4):
            place[i, i] = (dg, i)
        yield from known(("v_h", 3), ("diag", h, 6))
        o = yield from turn("out", end["far", 1], end["diag", h, 6])
        for i in range(4):
            if i:
                yield T,
            for j in range(4):
                src, n = place[j, i]
                end["out", o] = mm(B("out", o)[:, W(i)], F[TILES["v_h"][j]][:, W(h)], src[:, W(n)], j == 0, j == 3,
                                   end["v_h", j], end["diag", h, 6], end["near"], end["far", 0], end["far", 1], gone("out", o))
        left["hgrn work", h] = left["v_h", h] = end["out", o]
        spawn(head_out(h, o))

    def head_out(h, o):
        k = yield from turn("sq", end["out", o], lane=A)
        rb = RT("sq", k)
        a = act(rb[:], B("out", o)[:], ACT.Square, end["out", o], gone("sq", k))
        m = yield from turn("mix", a)
        t = end["mix", m] = mm(B("mix", m)[:], ones, rb[:], True, True, a, gone("mix", m))
        yield EXP, t
        t = act(rb[:], B("mix", m)[:], ACT.Ln, t, scale=1.0 / P, bias=eps)
        t = act(rb[:], rb[:], ACT.Exp, t, scale=-0.5)
        y = F[TILES["yh"]]
        yield from known(("hg", h), *[("y_h", x) for x in (h - 1,) if x >= 0])
        yield V, t
        t = left["mix", m] = refine(rb[:], B("mix", m)[:], P, y[:], t, end.get(("y_h", h - 1)))
        t = left["out", o] = left["sq", k] = stt(y[:], B("out", o)[:], vcol("hgrn_norm", h), rb[:], ALU.mult, ALU.mult, t)
        t = left["hg", h] = tt(y[:], y[:], F[TILES["hg"][h]][:], ALU.mult, t, end["hg", h])
        yield from split(y_h[h], y[:], None, t)
        left["yh", h] = end["y_h", h]

    y_h = [pair(("y_h", h), TILES["y_h"][h]) for h in range(4)]
    y_m = [pair(("y_m", h), TILES["y_m"][h]) for h in range(4)]

    def gates():
        kd = yield from fm("w_in", 4608, xs)
        spawn(gates_of(kd), 2)

    def gates_of(kd):
        g0, g1, g2, g3, g4 = (F[i] for i in TILES["gates"])
        k = yield from z_of(kd)
        yield A, end["z", k]
        z_ok = left["z", k] = act(g0[:], RT("z", k)[:], ACT.Identity, end["z", k], bias=vcol("b_gt"))
        a = act(g1[:], g0[:], ACT.Abs, z_ok)
        a = act(g1[:], g1[:], ACT.Exp, a, scale=-1.0)
        a = act(g1[:], g1[:], ACT.Ln, a, bias=one, table=LN)
        yield V, a
        t = stt(g1[:], g0[:], 0.0, g1[:], ALU.min, ALU.subtract, a)
        yield from freed("b_hi")
        k = yield from turn("mix", t)
        for i in range(4):
            end["mix", k] = tr(B("mix", k)[:, W(i)], g1[:, W(i)], t, gone("mix", k))
        turned = end["mix", k]
        yield A, turned
        t = left["mix", k] = copy(g2[:], B("mix", k)[:], turned, left["b_hi"], on=A)
        k = yield from turn("mix", t)
        b = B("mix", k)
        for i in range(4):
            for j in range(i + 1):
                mmq(b[0:64, W(i)], g2[:, P * j + 32:P * j + 96], C("le") if j == i else ones, j == 0, j == i, t, gone("mix", k))
            for j in range(i, 4):
                end["mix", k] = mm(b[64:96, W(i)], g2[:, P * j + 96:P * j + 128], C("ge") if j == i else ones, j == i, j == 3)
        summed_up = end["mix", k]
        yield A, summed_up
        f_ok = left["mix", k] = copy(g4[0:96, :], b[0:96, :], summed_up, on=A)
        yield V, f_ok
        x0 = put(g1[96:128, :], 0.0, turned)
        x1 = tt(g1[0:96, :], g0[0:96, :], g4[0:96, :], ALU.subtract, f_ok, z_ok, turned)
        m_f = m_b = ts(g3[0:96, :], g1[0:96, :], 0.0, None, ALU.max, None, x1)
        for lv in range(9):
            size = 1 << lv
            e, o = blocks(g3[:], size)
            n = S // (2 * size)
            yield V, m_f
            m_f = tt(o[0:4], o[0:4], e[0:4, :, size - 1:size].to_broadcast([4, n, size]), ALU.max, m_f)
            m_b = tt(e[64:68], e[64:68], o[64:68, :, 0:1].to_broadcast([4, n, size]), ALU.max, m_b)
        end["M"] = (m_f, m_b)
        yield V, m_b
        t = tt(g0[0:96, :], g3[0:96, :], g4[0:96, :], ALU.add, m_f, m_b, x1)
        left["F"] = t
        t = ts(g0[0:96, :], g0[0:96, :], -88.0, None, ALU.max, None, t)
        yield EXP, t
        a = act(g1[32:36, :], g0[0:4, :], ACT.Exp, t, x1, scale=-1.0)
        a = act(g1[96:100, :], g0[64:68, :], ACT.Exp, x0, scale=-1.0)
        k = yield from turn("mix", a)
        for i in range(4):
            end["mix", k] = tr(B("mix", k)[:, W(i)], g1[:, W(i)], a, gone("mix", k))
        left["gate temps"] = end["mix", k]
        yield A, end["mix", k]
        end["gate columns"] = left["mix", k] = copy(g2[:], B("mix", k)[:], end["mix", k], summed_up, on=A)

    def conv_of(name, h, ct, n, scale, kd):
        tile = TILES[name][h]
        free = ("hin", 2 if tile < 53 else 3)
        yield from freed(free, ("acc", "x"), "b_mv", *[("conv", x) for x in (n - 2,) if x >= 0])
        kz = yield from z_of(kd)
        x = RT("z", kz)
        yield A, end["z", kz]
        x_ok = act(x[:], x[:], ACT.Identity, end["z", kz], bias=vcol("b_m" + name, h))
        w = lambda j: vcol("conv_w", 8 * j + ct)
        y, g = F[tile], F[TILES["conv"][n % 2]]
        yield A, x_ok, left[free]
        t = act(y[:], x[:], ACT.Identity, x_ok, left[free], scale=w(2), bias=vcol("conv_b", ct))
        for j in (0, 1, 3, 4):
            o, i = (slice(2 - j, S), slice(0, S - 2 + j)) if j < 2 else (slice(0, S + 2 - j), slice(j - 2, S))
            yield V, t
            t = stt(y[:, o], x[:, i], w(j), y[:, o], ALU.mult, ALU.add, t, x_ok)
        left["z", kz] = t
        w = (left["acc", "x"], left["b_mv"], left.get(("conv", n - 2)))
        yield SIG, t, w
        a = act(g[:], y[:], ACT.Sigmoid, t, w)
        yield V, a
        end[name, h] = left["conv", n] = stt(y[:], y[:], scale, g[:], ALU.mult, ALU.mult, a)

    def conv_in(h):
        spawn(conv_of("q", h, h, 2 * h, 1.0, (yield from fm("w_in", 2560 + 128 * h, xs))))
        spawn(conv_of("k", h, 4 + h, 2 * h + 1, P ** -0.5, (yield from fm("w_in", 3072 + 128 * h, xs))))

    def over_rows(h, d, r0, mask):
        mb, md = F[TILES["mb"][d]], F[TILES["md"][d]]
        k = yield from turn("mix", end["M"])
        end["mix", k] = mm(B("mix", k)[:], ident[r0:r0 + 4, r0 + h:r0 + h + 1].to_broadcast([4, P]), F[TILES["gates"][3]][r0:r0 + 4, :], True, True,
                           end["M"], gone("mix", k))
        free = (left["v_h", 3], left.get(("mlstm exp", h - 1)))
        yield A, end["mix", k], free
        end["mb", h, d] = left["mix", k] = copy(mb[:], B("mix", k)[:], end["mix", k], free, on=A)
        yield V, end["mb", h, d]
        end["md", h, d] = tt(md[:].rearrange("p (c t) -> p c t", c=4), mb[:].rearrange("p (c t) -> p c t", c=4),
                             C(mask).unsqueeze(1).to_broadcast([P, 4, P]), ALU.add, end["mb", h, d])

    def weights_of(h, j):
        q, kk = F[TILES["q"][h]], F[TILES["k"][h]]
        mb, md, col = [F[i] for i in TILES["mb"]], [F[i] for i in TILES["md"]], F[TILES["gates"][2]]
        e, g = (F[TILES["pt"][i]] for i in (j, j + 1))
        yield from known(("md", h, 0), ("md", h, 1), "gate columns")
        k = yield from turn("mix", end["q", h], end["k", h])
        b = B("mix", k)
        s = end["mix", k] = left["qk", h, j] = mm(b[:], kk[:, W(j)], q[:], True, True, end["q", h], end["k", h], gone("mix", k))
        c0, c1 = col[:, P * j + h:P * j + h + 1], col[:, P * j + 64 + h:P * j + 64 + h + 1]
        free = (left["hg", 3], left.get(("pt", h - 1)), left["hgrn work", 3])
        yield EXP, end["md", h, 0], free
        a = act(e[:, W(j)], md[0][:, W(j)], ACT.Exp, end["md", h, 0], end["gate columns"], free, scale=-1.0, bias=c0)
        if j < 3:
            a = act(e[:, P * j + P:], mb[0][:, P * j + P:], ACT.Exp, end["mb", h, 0], scale=-1.0, bias=c0)
        yield V, a, s
        end["p fwd", h, j] = tt(e[:, P * j:], e[:, P * j:], b[:, P * j:], ALU.mult, a, s)
        yield EXP, end["md", h, 1]
        a = act(g[:, W(j)], md[1][:, W(j)], ACT.Exp, end["md", h, 1], scale=-1.0, bias=c1)
        if j > 0:
            a = act(g[:, 0:P * j], mb[1][:, 0:P * j], ACT.Exp, end["mb", h, 1], scale=-1.0, bias=c1)
        end["weight exps", h, j] = a
        yield V, a
        end["p bwd", h, j] = left["mix", k] = tt(g[:, 0:P * j + P], g[:, 0:P * j + P], b[:, 0:P * j + P], ALU.mult, a, s)

    def mlstm_row(h, i):
        pt, hn, col = [F[x] for x in TILES["pt"]], F[TILES["hn"]], F[TILES["gates"][2]]
        o0 = 40 + 16 * h
        o = yield from turn("out", end["p bwd", h, 3], [end["v_m", j] for j in range(4)])
        b = B("out", o)
        for j in range(i + 1):
            mmq(b[:, 0:129], pt[j][:, W(i)], vw[:, j, h, :], j == 0, j == i, end["p fwd", h, j], end["v_m", j], gone("out", o))
        for j in range(i, 4):
            end["out", o] = mm(b[:, 129:258], pt[j + 1][:, W(i)], vw[:, j, h, :], j == i, j == 3, end["p bwd", h, j])
        left["pt", h, i] = end["out", o]
        den = sm[:, o0 + 2 * i:o0 + 2 * i + 2]
        c = P * i + 32 + h
        yield A, end["out", o]
        t = act(den, b[:, 128:258:129], ACT.Abs, end["out", o])
        yield V, t
        t = tt(den, den, col[:, c:c + 65:64], ALU.max, t, end["gate columns"])
        t = recip(den, t)
        free = (left.get(("hn", h - 1)), left["hgrn work", 3])
        yield A, t, free
        a = act(hn[:, W(i)], b[:, 0:128], ACT.Identity, t, free, scale=den[:, 0:1])
        yield V, a
        t = left["out", o] = stt(hn[:, W(i)], b[:, 129:257], den[:, 1:2], hn[:, W(i)], ALU.mult, ALU.add, a)
        yield A, t
        end["hn", h, i] = act(F[TILES["junk"]][:, W(i)], hn[:, W(i)], ACT.Square, t, acc=sm[:, o0 + 8 + i:o0 + 9 + i])

    def mlstm_out(h):
        hn, y = F[TILES["hn"]], F[TILES["ym"]]
        ss, rs, wk = (sm[:, x:x + 4] for x in (48 + 16 * h, 52 + 16 * h, 512 + 4 * h))
        yield from known(*[("hn", h, i) for i in range(4)])
        w = [end["hn", h, i] for i in range(4)]
        yield EXP, w
        a = act(rs, ss, ACT.Ln, w, scale=1.0 / P, bias=eps)
        a = act(rs, rs, ACT.Exp, a, scale=-0.5)
        yield V, a
        a = refine(rs, ss, P, wk, a)
        for i in range(4):
            t = ts(hn[:, W(i)], hn[:, W(i)], rs[:, i:i + 1], None, ALU.mult, None, a)
        k = yield from turn("mix", t)
        for i in range(4):
            end["mix", k] = tr(B("mix", k)[:, W(i)], hn[:, W(i)], t, gone("mix", k))
        left["hn", h] = end["mix", k]
        if h:
            yield from freed(("ym", h - 1))
        yield V, end["mix", k], end["mo", h]
        t = left["mix", k] = left["mo", h] = stt(y[:], B("mix", k)[:], vcol("mlstm_norm", h), F[TILES["mo"][h]][:], ALU.mult, ALU.mult,
                                                 end["mix", k], end["mo", h], left.get(("ym", h - 1)))
        yield from split(y_m[h], y[:], None, t, [left["qk", h, j] for j in range(4)])
        left["ym", h] = end["y_m", h]

    def mlstm_head(h):
        yield from freed(("v_h", 3), ("hgrn work", 3), ("hg", 3))
        yield from known("M", ("q", h), ("k", h), ("v_m", 3))
        for d, (r0, mask) in enumerate(((0, "hi"), (64, "lo"))):
            spawn(over_rows(h, d, r0, mask), 2)
        for j in range(4):
            spawn(weights_of(h, j), 2)
        yield from known(*[("p bwd", h, j) for j in range(4)])
        left["mlstm exp", h] = [end["weight exps", h, j] for j in range(4)] + [end["md", h, 1]]
        if h:
            yield from freed(("hn", h - 1))
        for i in range(4):
            spawn(mlstm_row(h, i), 2)
        yield from freed(*[("pt", h, i) for i in range(4)])
        left["pt", h] = [left["pt", h, i] for i in range(4)]
        spawn(mlstm_out(h), 2)

    def hg_in(h):
        spawn(silu_of(("hg", h), (yield from fm("w_in", 2048 + 128 * h, xs)), vcol("b_hg", h), TILES["hg"][h]))

    def mo_of(h, kd):
        k = yield from z_of(kd)
        yield SIG, end["z", k]
        end["mo", h] = left["z", k] = act(F[TILES["mo"][h]][:], RT("z", k)[:], ACT.Sigmoid, end["z", k], bias=vcol("b_mo", h))

    def mo_in(h):
        spawn(mo_of(h, (yield from fm("w_in", 4096 + 128 * h, xs))))

    def mix_dense():
        yield from hgrn_in(0)
        spawn(v_of((yield from tm("w_in", 1536, xs))))
        yield from hgrn_in(1)
        yield from hg_in(0)
        yield from gates()
        yield from hg_in(1)
        yield from hgrn_in(2)
        yield from hg_in(2)
        yield from mo_in(0)
        yield from mo_in(1)
        yield from hgrn_in(3)
        yield from hg_in(3)
        yield from mo_in(2)
        yield from mo_in(3)
        spawn(vm_of((yield from tm("w_in", 3584, xs))))
        for h in range(4):
            yield from conv_in(h)
        left["xs"] = end["dense", uses["dense"] - 1]
        yield from xkv()

    def hgrn_all():
        for h in range(4):
            yield from known(*[(n, h) for n in ("q", "f", "g", "kf", "kb")])
            yield from hgrn_head(h)

    def mlstm_all():
        for h in range(4):
            yield from mlstm_head(h)

    memn = []
    for i in range(KT):
        th, tl = TILES["memn"][2 * (i // 2):2 * (i // 2) + 2]
        memn.append((R[th][:, W(i % 2, 256)], R[tl][:, W(i % 2, 256)], ("memn", i)))

    def mem_in(i):
        x = F[TILES["mem"][i]]
        yield from freed(("hgrn work", 3), ("yh", 3), "F")
        end["mem", i] = load(f"x{i}", x[:].rearrange("p (k t) -> p k t", k=2),
                             io["memT"][W(i, 256)].rearrange("(k p) t -> p k t", k=2), left["hgrn work", 3], left["yh", 3], left["F"])
        yield from freed("xs", ("conv", 6))
        for j in range(2):
            c, d = W(j, 256), 2 * i + j
            spawn(split(memn[d], x[:, c], vcol("norm_mem", d), end["mem", i], left["xs"]))
            spawn(add_square("mem", 66, d, x[:, c], end["mem", i], free=[("conv", 6)]), 4)

    def kx_of(i, k):
        yield from known("rstd mem")
        free = (left["gate temps"], left["hin", 3])
        yield V, end["dense", k], end["rstd mem"], free
        end["kx", i] = left["dense", k] = left["rstd", RSTD1] = tt(F[TILES["kx"][i // 2]][:, W(i % 2, 256)], B("dense", k)[:, 0:256],
                                                                   F[RSTD1][:, 0:256], ALU.mult, end["dense", k], end["rstd mem"], free)

    rc = sm[:, 36:38]
    def vx_of(g, ks):
        yield from known("rcol mem")
        free = ([end["sq", "mem", i] for i in range(KT)], [end["memn", i] for i in range(KT)])
        for i, k in enumerate(ks):
            yield A, end["dense", k], end["rcol mem"], free
            end["vx", 2 * g + i] = left["dense", k] = act(F[TILES["vx"][2 * g + i]][:], B("dense", k)[:], ACT.Identity,
                                                          end["dense", k], end["rcol mem"], free, scale=rc[:, i:i + 1])

    def xkv():
        for i in range(4):
            spawn(mem_in(i))
        spawn(rstd_row("rstd mem", RSTD1, "mem", 66, 256))
        spawn(rstd_column("rcol mem", rc, "mem", 66))
        for i in range(8):
            spawn(kx_of(i, (yield from fm("w_xkv", 128 * i, memn, 256))))
        for g, c in enumerate((1024, 1536)):
            spawn(vx_of(g, (yield from tm("w_xkv", c, memn, 2))))
        left["memn"] = end["dense", uses["dense"] - 1]

    def add_to(i, ring, k, *waits):
        w = (end["x", i], left.get(("x", i)), waits)
        yield V, end[ring, k], w
        end["x", i] = left[ring, k] = tt(F[i][:], F[i][:], B(ring, k)[:], ALU.add, end[ring, k], w)

    def stream(i, k, nxt, gain, tag, *waits):
        yield from add_to(i, "dense", k)
        spawn(add_square(tag, 66, i, F[i][:], end["x", i], free=[("acc", "x")]), 4)
        yield from split(nxt[i], F[i][:], vcol(gain, i), end["x", i], waits)
        yield from known(("sq", tag, i))
        left["x", i] = (end[nxt[i][2]], end["sq", tag, i])

    def sublayer(weight, ins, nxt, gain, tag, free):
        for i in range(KT):
            k = yield from fm(weight, 128 * i, ins)
            yield from freed(free)
            spawn(stream(i, k, nxt, gain, tag, left[free]))
        left[weight] = end["dense", uses["dense"] - 1]

    xs1 = [pair(("xs1", i), XIN[i]) for i in range(KT)]
    xs2 = [pair(("xs2", i), XIN[i]) for i in range(KT)]
    xs3 = [pair(("xs3", i), XIN[i]) for i in range(KT)]

    def xattn_probs(h, g):
        kx, p = F[TILES["kx"][h]], F[TILES["pp"][2 * (h % 2) + g]]
        q = [F[TILES["qx"][2 * h]], F[TILES["qx"][2 * h + 1]]]
        o = 104 + 16 * h
        nm, su = sm[:, o:o + 4], sm[:, o + 4:o + 8]
        k = yield from turn("mix", end["qx", 2 * h + 1], end["qx", 2 * h])
        b = B("mix", k)
        for i in (2 * g, 2 * g + 1):
            for d in range(2):
                end["mix", k] = mm(b[:, W(i % 2, 256)], q[d][:, W(i)], kx[:, W(d, 256)], d == 0, d == 1,
                                   end["qx", 2 * h + d], end["kx", 2 * h + d], gone("mix", k))
        yield V, end["mix", k]
        t = reduce(nm[:, W(g, 2)], b[:].rearrange("p (i s) -> p i s", i=2), ALU.max, end["mix", k])
        t = ts(nm[:, W(g, 2)], nm[:, W(g, 2)], -1.0 / 16, None, ALU.mult, None, t)
        free = (left["mo", 3], left.get(("pp", h - 2)))
        yield EXP, t, free
        for i in range(2):
            c = 2 * g + i
            a = act(p[:, W(i, 256)], b[:, W(i, 256)], ACT.Exp, t, free, scale=1.0 / 16, bias=nm[:, c:c + 1], acc=su[:, c:c + 1])
        left["mix", k] = a
        yield V, a
        t = recip(su[:, W(g, 2)], a)
        for i in range(2):
            c = 2 * g + i
            end["pp", h, g] = ts(p[:, W(i, 256)], p[:, W(i, 256)], su[:, c:c + 1], None, ALU.mult, None, t)

    def xattn_out(h, d):
        pts = [F[i] for i in TILES["pts"][2 * (h % 2):2 * (h % 2) + 2]]
        k = yield from turn("out", end["pts", h, 0], end["pts", h, 1], end["vx", 2 * (h // 2) + 1])
        for j in range(2):
            v = F[TILES["vx"][2 * (h // 2) + j]]
            c = 256 * (h % 2) + P * d
            end["out", k] = left["pts", h, d] = mm(B("out", k)[:], v[:, c:c + P], pts[j][:], j == 0, j == 1, end["vx", 2 * (h // 2) + j],
                                                   end["pts", h, j], gone("out", k))
        yield from split(xo[2 * h + d], B("out", k)[:], None, end["out", k], left["w_out"])
        left["out", k] = end["xo", 2 * h + d]

    def xattn_head(h):
        yield from known(("qx", 2 * h), ("qx", 2 * h + 1), ("kx", 2 * h + 1), ("vx", 2 * (h // 2) + 1))
        for g in range(2):
            spawn(xattn_probs(h, g), 2)
        yield from known(("pp", h, 0), ("pp", h, 1))
        two, pts = TILES["pp"][2 * (h % 2):2 * (h % 2) + 2], TILES["pts"][2 * (h % 2):2 * (h % 2) + 2]
        if h >= 2:
            yield from freed(("pts", h - 2, 0), ("pts", h - 2, 1))
        free = (left.get(("pts", h - 2, 0)), left.get(("pts", h - 2, 1)), left["hn", 3], left["pt", 3], left["ym", 3])
        for j in range(2):
            k = yield from turn("mix", end["pp", h, 0], end["pp", h, 1])
            for i in range(4):
                c = 256 * (i % 2) + P * j
                end["mix", k] = tr(B("mix", k)[:, W(i)], F[two[i // 2]][:, c:c + P], end["pp", h, i // 2], gone("mix", k))
            yield (V if j else A), end["mix", k], free
            end["pts", h, j] = left["mix", k] = copy(F[pts[j]][:], B("mix", k)[:], end["mix", k], free, on=V if j else A)
        left["pp", h] = end["mix", k]
        for d in range(2):
            spawn(xattn_out(h, d), 2)

    xo = [pair(("xo", i), TILES["xo"][i]) for i in range(KT)]
    def qx_of(i, k):
        yield from known("rstd 1")
        free = (left["pt", 3], left["mlstm exp", 3])
        yield V, end["dense", k], end["rstd 1"], free
        end["qx", i] = left["dense", k] = left["rstd", RSTD] = tt(F[TILES["qx"][i]][:], B("dense", k)[:], F[RSTD][:], ALU.mult,
                                                                  end["dense", k], end["rstd 1"], free)

    def xattn_all():
        yield from freed(("ym", 3))
        for h in range(4):
            yield from xattn_head(h)

    def x_dense():
        for i in range(KT):
            left["x", i] = (end["xs", i], end["sq", "x", i])
        yield from sublayer("w_out", y_h + y_m, xs1, "norm_xattn", "x1", "memn")
        spawn(rstd_row("rstd 1", RSTD, "x1", 66))
        for i in range(KT):
            spawn(qx_of(i, (yield from fm("w_xq", 128 * i, xs1))))
        left["w_xq"] = end["dense", uses["dense"] - 1]
        yield from sublayer("w_xo", xo, xs2, "norm_mlp", "x2", "w_xq")
        spawn(rstd_row("rstd 2", RSTD, "x2", 66))
        yield from mlp()

    gg = sm[:, 168:176]
    end["gg"] = tt(gg, vec[:, vat["norm_final"]:vat["norm_final"] + 8], vec[:, vat["norm_mix_2"]:vat["norm_mix_2"] + 8], ALU.mult, end["vec"])
    hid = [[pair(("hid", r, c), TILES["hid"][c]) for c in range(8)] for r in range(4)]
    def hid_of(r, c, kd, free):
        k = yield from z_of(kd, "rstd 2")
        z = RT("z", k)
        yield V, end["z", k]
        t = stt(z[:], z[:], 0.0, z[:], ALU.max, ALU.mult, end["z", k])
        yield from split(hid[r][c], z[:], None, t, free)
        left["z", k] = end["hid", r, c]

    def last_stream(i, k):
        yield from add_to(i, "dense", k)
        spawn(add_square("x3", 66, i, F[i][:], end["x", i]), 4)
        spawn(add_square("x3n", 67, i, F[i][:], end["x", i], scale=vcol("norm_final", i)), 4)
        yield from split(xs3[i], F[i][:], gg[:, i:i + 1], end["x", i], end["gg"], left["w_up"])
        yield from known(("sq", "x3", i), ("sq", "x3n", i))
        left["x3", i] = (end["xs3", i], end["sq", "x3", i], end["sq", "x3n", i])

    def mlp():
        free = left["w_xo"]
        for r in range(4):
            for c in range(8):
                kd = yield from fm("w_up", 128 * (8 * r + c), xs2)
                spawn(hid_of(r, c, kd, free))
            left["w_up"] = end["dense", kd]
            for i in range(KT):
                k = yield from fm("w_down", 128 * i, hid[r])
                spawn(add_to(i, "dense", k) if r < 3 else last_stream(i, k))
            free = left["w_down"] = end["dense", k]

    def both(name, n, t1, t2, *waits):
        yield from summed("x3", "x3n")
        ks = yield from turn("mix", end["acc", "x3"], end["acc", "x3n"], n=2)
        for k, tag, acc in zip(ks, ("x3", "x3n"), (66, 67)):
            if n == S:
                t = mm(B("mix", k)[:], ones, F[acc][:], True, True, gone("mix", k), end["acc", tag])
            else:
                for i in range(n):
                    t = mm(B("mix", k)[:, i:i + 1], F[acc][:, W(i)], one, True, True, gone("mix", k), end["acc", tag])
            end["mix", k] = left["acc", tag] = t
        k1, k2 = ks
        yield EXP, end["mix", k1], waits
        t = act(t1, B("mix", k1)[:, 0:n], ACT.Ln, end["mix", k1], waits, scale=1.0 / 1024, bias=eps)
        t = act(t1, t1, ACT.Exp, t, scale=-0.5)
        yield V, t, waits
        t = end[name + " final"] = left["mix", k1] = refine(t1, B("mix", k1)[:, 0:n], 1024, t2, t, waits)
        q = tt(t2, t1, t1, ALU.mult, t, waits)
        q = left["mix", k2] = tt(t2, t2, B("mix", k2)[:, 0:n], ALU.mult, q, end["mix", k2])
        yield EXP, q
        q = act(t2, t2, ACT.Ln, q, scale=1.0 / 1024, bias=eps)
        q = act(t2, t2, ACT.Exp, q, scale=-0.5)
        yield V, q
        end[name] = tt(t2, t2, t1, ALU.mult, q)

    rcol2 = sm[:, 180:184]
    def between():
        yield from both("rstd 3", S, F[RSTD1][:], F[RSTD][:], left["rstd", RSTD], left["rstd", RSTD1])
        spawn(rescale(), 4)
        yield from both("rcol 3", 4, sm[:, 176:180], rcol2)

    def rescale():
        for i in range(KT):
            yield from freed(("x3", i))
            yield V, end["rstd 3 final"], left["x3", i]
            end["x", i] = left["rstd", RSTD1] = stt(F[i][:], F[i][:], vcol("norm_final", i), F[RSTD1][:], ALU.mult, ALU.mult, end["rstd 3 final"], left["x3", i])

        end["h0"] = end["x", 7]

    def decay_of(d, i, k):
        b, x, y = B("mix", k), F[TILES["la"][d][i]], F[TILES["dt"][2 * i + d]]
        free = (left["pp", 3], left["w_xo"])
        yield A, end["mix", k]
        a = act(y[:], b[:], ACT.Abs, end["mix", k], free, left["pt", 3])
        yield V, a
        end["min", d, i] = left["mix", k] = ts(x[:], b[:], 0.0, None, ALU.min, None, a, free)
        yield EXP, a
        end["exp", d, i] = act(y[:], y[:], ACT.Exp, a, scale=-1.0)

    def logs():
        order = [(d, i) for i in range(4) for d in range(2)]
        yield from known(*[("exp", *x) for x in order])
        for d, i in order:
            y = F[TILES["dt"][2 * i + d]]
            yield LN, end["exp", d, i]
            a = act(y[:], y[:], ACT.Ln, end["exp", d, i], bias=one, table=LN)
            spawn(log_of(d, i, y, a))

    def log_of(d, i, y, a):
        x = F[TILES["la"][d][i]]
        yield V, a
        end["la", d, i] = tt(x[:], x[:], y[:], ALU.subtract, a, end["min", d, i])

    def decays(kd):
        free = (left["pts", 3, 0], left["pts", 3, 1])
        end["pos"] = load("pos", F[TILES["pos"]][:].bitcast(I32), bass.AP(io["pos"].tensor, io["pos"].offset, [[0, P], [1, S]]), free)
        end["upa"] = load("upa", F[TILES["upa"]][:], io["gla_up"], free)
        z, upa = F[TILES["zt"]], F[TILES["upa"]]
        t = put(z[0:64, :], 1.0, free)
        yield from known("rstd 3")
        yield V, end["rstd 3"], end["dense", kd]
        for o in (0, 32):
            t = tt(z[o:o + 16, :], B("dense", kd)[o:o + 16, :], F[RSTD][o:o + 16, :], ALU.mult, end["dense", kd], end["rstd 3"], t)
        left["dense", kd] = t
        for i in range(4):
            for d, o in ((0, 0), (1, 32)):
                k = yield from turn("mix", t, end["upa"])
                end["mix", k] = left["zt"] = mm(B("mix", k)[:], z[o:o + 17, W(i)], upa[o:o + 17, :], True, True, t, end["upa"], gone("mix", k))
                spawn(decay_of(d, i, k))
        yield from logs()

    def gqk_of(name, h, sc, k):
        yield from known("rstd 3")
        yield V, end["dense", k], end["rstd 3"]
        end[name, h] = left["dense", k] = left["rstd", RSTD] = stt(F[TILES[name][h]][:], B("dense", k)[:], sc, F[RSTD][:], ALU.mult, ALU.mult,
                                                                   end["dense", k], end["rstd 3"], left["w_down"])

    def gqk_in(h):
        for name, col, sc in (("gq", 768, P ** -0.5), ("gk", 1280, 1.0)):
            spawn(gqk_of(name, h, sc, (yield from fm("w_in_2", col + 128 * h, xs3))))

    def gv_of(g, ks):
        yield from known("rcol 3")
        for i, k in enumerate(ks):
            n = 4 * g + i
            yield A, end["dense", k], end["rcol 3"]
            end["gv", n] = left["dense", k] = act(F[TILES["gv"][n]][:], B("dense", k)[:], ACT.Identity, end["dense", k], end["rcol 3"],
                                                  left["w_xo"], scale=rcol2[:, i:i + 1])

    def gv_in(g):
        spawn(gv_of(g, (yield from tm("w_in_2", 1792 + 512 * g, xs3))))

    def gr_of(i, kd):
        k = yield from z_of(kd, "rstd 3")
        x = F[TILES["gr"][i]]
        yield SIG, end["z", k]
        a = act(x[:], RT("z", k)[:], ACT.Sigmoid, end["z", k], left["w_down"])
        yield V, a
        end["gr", i] = left["z", k] = tt(x[:], RT("z", k)[:], x[:], ALU.mult, a)

    def gr_in(h):
        for i in (2 * h, 2 * h + 1):
            spawn(gr_of(i, (yield from fm("w_in_2", 2816 + 128 * i, xs3))))

    gplace = [{}, {}]
    def gla_way(h, d):
        q, kk = F[TILES["gq"][h]], F[TILES["gk"][h]]
        dg, nr = F[TILES["gdiag"]], F[TILES["near"]]
        cm, mid, last = (("cf", 63, 127), ("cb", 64, 0))[d]
        e1, e2, ks, qs, fr = (F[TILES[n][d]] for n in ("e1", "e2", "ks", "qs", "far"))
        place = gplace[h % 2]
        busy = (left.get(("gla e", h - 1, d)), [end["la", x, i] for i in range(4) for x in range(2)], left["acc", "x3"], left["acc", "x3n"], left["sq last"])
        k = yield from turn("mix", [end["la", d, i] for i in range(4)])
        for i in range(4):
            end["mix", k] = left["la", h, d] = mm(B("mix", k)[:, W(i)], F[TILES["la"][d][i]][:, W(h)], C(cm), True, True, end["la", d, i], gone("mix", k))
        yield EXP, end["mix", k], busy
        a1 = act(e1[:], B("mix", k)[:], ACT.Exp, end["mix", k], busy)
        a2 = left["mix", k] = act(e2[:], B("mix", k)[:], ACT.Exp, busy, scale=-1.0)
        o = 192 + 40 * h + 20 * d
        h0, h1, w, aa, cc = sm[:, o:o + 4], sm[:, o + 4:o + 8], sm[:, o + 8:o + 10], sm[:, o + 10:o + 11], sm[:, o + 11:o + 12]
        yield V, a1
        t1 = copy(h0, e1[:, mid::P], a1)
        t2 = copy(h1, e1[:, last::P], a1)
        f1 = put(e1[:, mid::P], 1.0, t1)
        tq = tt(e1[:], e1[:], q[:], ALU.mult, f1, t2, end["gq", h])
        yield V, a2
        f2 = put(e2[:, mid::P], 1.0, a2)
        tk = tt(e2[:], e2[:], kk[:], ALU.mult, f2, end["gk", h])
        k = yield from turn("mix", tq, tk)
        scores(k, e2, e1, tk, tq)
        if d == 0:
            t = tt(w, h1[:, 0:4:2], h0[:, 1:4:2], ALU.mult, t1, t2)
            ta = tt(aa, w[:, 0:1], h1[:, 1:2], ALU.mult, t)
            tc = tt(cc, w[:, 1:2], h0[:, 2:3], ALU.mult, t)
            near, far_k, far_q = ((0, 1, w[:, 0:1]), (2, 3, w[:, 1:2])), ((0, aa), (1, h1[:, 1:2])), ((2, h0[:, 2:3]), (3, cc))
        else:
            t = tt(w, h1[:, 1:4:2], h0[:, 0:4:2], ALU.mult, t1, t2)
            ta = tt(aa, w[:, 1:2], h1[:, 2:3], ALU.mult, t)
            tc = tt(cc, w[:, 0:1], h0[:, 1:2], ALU.mult, t)
            near, far_k, far_q = ((1, 0, w[:, 0:1]), (3, 2, w[:, 1:2])), ((2, h1[:, 2:3]), (3, aa)), ((0, cc), (1, h0[:, 1:2]))
        for n, (i, _, c) in enumerate(near):
            t = ts(ks[:, W(n)], e2[:, W(i)], c, None, ALU.mult, None, tk, ta, tc, busy)
        for n, (i, c) in enumerate(far_k):
            t = ts(ks[:, W(2 + n)], e2[:, W(i)], c, None, ALU.mult, None)
        for n, (i, c) in enumerate(far_q):
            t = ts(qs[:, W(n)], e1[:, W(i)], c, None, ALU.mult, None, tq)
        left["gqk", h, d] = (tq, tk)
        if h:
            yield from freed(("gla pairs", h - 1))
        free = left.get(("gla pairs", h - 1)) or busy
        if d == 0:
            yield A, end["mix", k], free
            end["gdiag", h, 0] = left["mix", k] = copy(dg[:], B("mix", k)[:], end["mix", k], free, on=A)
        else:
            yield from known(("gdiag", h, 0))
            yield V, end["mix", k], end["gdiag", h, 0]
            end["gdiag", h, 1] = left["mix", k] = put_where(dg[:], C("hi"), B("mix", k)[:], end["mix", k], end["gdiag", h, 0])
        k = yield from turn("mix", t)
        for n, (i, j, _) in enumerate(near):
            end["mix", k] = mm(B("mix", k)[:, W(n)], ks[:, W(n)], e1[:, W(j)], True, True, t, gone("mix", k))
            place[i, j] = (nr, 2 * d + n)
        yield V, end["mix", k], free
        end["gnear", h, d] = left["mix", k] = copy(nr[:, W(d, 256)], B("mix", k)[:, 0:256], end["mix", k], free)
        k = yield from turn("mix", t)
        for n, (i, _) in enumerate(far_k):
            end["mix", k] = mm(B("mix", k)[:, W(n, 256)], ks[:, W(2 + n)], qs[:, 0:256], True, True, t, gone("mix", k))
            for m, (j, _) in enumerate(far_q):
                place[i, j] = (fr, 2 * n + m)
        left["gla e", h, d] = end["mix", k]
        yield A, end["mix", k], free
        end["gfar", h, d] = left["mix", k] = copy(fr[:], B("mix", k)[:], end["mix", k], free, on=A)

    def gla_out(h):
        place = gplace[h % 2]
        yield from known(("gdiag", h, 1), ("gnear", h, 0), ("gnear", h, 1), ("gfar", h, 0), ("gfar", h, 1), ("gv", 4 * (h // 2) + 3))
        for i in range(4):
            place[i, i] = (F[TILES["gdiag"]], i)
        pairs = [end[n, h, d] for n in ("gnear", "gfar") for d in range(2)] + [end["gdiag", h, 1]]
        two = []
        for v in range(2):
            o = yield from turn("out", pairs)
            two.append(o)
            for i in range(4):
                if i:
                    yield T,
                for j in range(4):
                    src, n = place[j, i]
                    m = 4 * (h // 2) + j
                    c = 256 * (h % 2) + P * v
                    end["out", o] = mm(B("out", o)[:, W(i)], F[TILES["gv"][m]][:, c:c + P], src[:, W(n)], j == 0, j == 3, end["gv", m],
                                       pairs, gone("out", o))
        left["gla pairs", h] = left["gv", h] = end["out", o]
        zs = []
        for v, o in enumerate(two):
            z = yield from turn("z", end["out", o], lane=A)
            zs.append(z)
            end["z", z] = act(RT("z", z)[:], B("out", o)[:], ACT.Square, end["out", o], gone("z", z))
        m = yield from turn("mix", end["z", zs[0]], end["z", zs[1]])
        for v, z in enumerate(zs):
            end["mix", m] = left["z", z] = mm(B("mix", m)[:], ones, RT("z", z)[:], v == 0, v == 1, end["z", z], gone("mix", m))
        rb = F[RSTD1]
        yield EXP, end["mix", m], left["rstd", RSTD1]
        t = left["mix", m] = act(rb[:], B("mix", m)[:], ACT.Ln, end["mix", m], left["rstd", RSTD1], scale=1.0 / 256, bias=eps)
        t3 = act(rb[:], rb[:], ACT.Exp, t, scale=-0.5)
        yield from known(("gr", 2 * h), ("gr", 2 * h + 1))
        for v, o in enumerate(two):
            i = 2 * h + v
            y, g = F[TILES["yg"]], F[TILES["gr"][i]]
            yield V, t3, left["yg"]
            t = left["out", o] = left["rstd", RSTD1] = stt(y[:], B("out", o)[:], vcol("gla_norm_2", i), rb[:], ALU.mult, ALU.mult, t3, left["yg"])
            t = tt(y[:], y[:], g[:], ALU.mult, t, end["gr", i])
            yield from split(y_gla[i], y[:], None, t, left["gqk", h, 0], left["gqk", h, 1])
            left["yg"] = end["y_gla", i]
        left["gla work", h] = left["yg"]

    y_gla = [pair(("y_gla", i), (TILES[("gq", "gk")[i % 2]][i // 2], TILES["gr"][i])) for i in range(8)]
    def gla_ways(d):
        yield from known(*[("la", x, i) for i in range(4) for x in range(2)])
        while uses["sq"] and ("sq", uses["sq"] - 1) not in left:
            yield False
        left["sq last"] = left["sq", uses["sq"] - 1]
        yield from freed(("acc", "x3"), ("acc", "x3n"))
        for h in range(4):
            yield from known(("gq", h), ("gk", h))
            yield from gla_way(h, d)

    def gla_outs():
        yield from known(("la", 1, 3), "h0")
        left["yg"] = left["zt"]
        for h in range(4):
            yield from gla_out(h)

    sin, cos = F[TILES["sin"]], F[TILES["cos"]]
    def rope_tables():
        ang, n = F[TILES["pos"]], sin
        magic = 12582912.0
        dead = (left["la", 3, 0], left["la", 3, 1])
        yield V, dead
        t = copy(n[:], ang[:].bitcast(I32), end["pos"], dead)
        t = ts(ang[:], n[:], vcol("freq"), None, ALU.mult, None, t)
        yield V, t
        t = ts(n[:], ang[:], float(np.float32(0.5 / np.pi)), magic, ALU.mult, ALU.add, t)
        t = ts(n[:], n[:], -magic, None, ALU.add, None, t)
        for c in TWO_PI:
            yield V, t
            t = stt(ang[:], n[:], -c, ang[:], ALU.mult, ALU.add, t)
        t = ts(ang[:], ang[:], 3.1415925, -3.1415925, ALU.min, ALU.max, t)
        yield A, t
        b = act(cos[:], ang[:], ACT.Abs, t, dead)
        end["sin"] = act(sin[:], ang[:], ACT.Sin, t)
        end["cos"] = act(cos[:], cos[:], ACT.Sin, b, scale=-1.0, bias=vcol("halfpi"))
        left["pos"] = end["sin"]

    def rotated(name, kd, tile, n):
        x, y = F[tile], F[TILES["rot"][n % 2]]
        dead = (left["la", 3, 0], left["la", 3, 1], left["gv", 1])
        yield V, end["dense", kd], dead
        t = left["dense", kd] = left["rstd", RSTD] = tt(x[:], B("dense", kd)[:], F[RSTD][:], ALU.mult, end["dense", kd], end["rstd 3"], dead)
        k = yield from turn("mix", t)
        end["mix", k] = mm(B("mix", k)[:], C("rot"), x[:], True, True, t, gone("mix", k))
        yield from known("sin", "cos")
        if n >= 2:
            yield from freed(("rot", n - 2))
        yield V, end["mix", k], end["sin"], left.get(("rot", n - 2))
        u = left["mix", k] = tt(y[:], B("mix", k)[:], sin[:], ALU.mult, end["mix", k], end["sin"], left.get(("rot", n - 2)))
        yield G, end["mix", k], end["cos"]
        t = tt(x[:], x[:], cos[:], ALU.mult, end["mix", k], end["cos"], on=G)
        end[name] = left["rot", n] = tt(x[:], x[:], y[:], ALU.add, t, u, on=G)

    def av_of(kd):
        kz = yield from z_of(kd, "rstd 3")
        k = yield from turn("mix", end["z", kz])
        for i in range(4):
            end["mix", k] = left["z", kz] = tr(B("mix", k)[:, W(i)], RT("z", kz)[:, W(i)], end["z", kz], gone("mix", k))
        yield A, end["mix", k]
        end["av"] = left["mix", k] = copy(F[TILES["av"]][:], B("mix", k)[:], end["mix", k], left["gv", 1], on=A)

    def att_in():
        spawn(rope_tables(), 2)
        spawn(rotated("ak", (yield from fm("w_in_2", 512, xs3)), TILES["ak"], 0))
        for j in range(4):
            spawn(rotated(("aq", j), (yield from fm("w_in_2", 64 * j, xs3)), TILES["aq"][j], j + 1))
        spawn(av_of((yield from fm("w_in_2", 640, xs3))))

    def gate_of(name, i, kd, *free):
        yield from freed(*free)
        w = [left[x] for x in free]
        k = yield from z_of(kd, "rstd 3")
        yield SIG, end["z", k], w
        end[name, i] = left["z", k] = act(F[TILES[name][i]][:], RT("z", k)[:], ACT.Sigmoid, end["z", k], w)

    def gate2_in(name, col, tiles, *free):
        for i in tiles:
            spawn(gate_of(name, i, (yield from fm("w_in_2", col + 128 * i, xs3)), *free))

    def att_probs(n, j, k0, nk):
        ak, aq = F[TILES["ak"]], F[TILES["aq"][j]]
        m0 = cat["hi"] + P * (k0 - n + 1)
        mx = sm[:, 352 + 32 * n:360 + 32 * n]
        ks = yield from turn("mix", end["aq", j], end["ak"], n=2)
        for g in range(2):
            r = W(g, 64)
            end["mix", ks[g]] = mm(B("mix", ks[g])[:, 0:P * nk], aq[r, W(n)], ak[r, P * k0:P * k0 + P * nk], True, True,
                                   end["aq", j], end["ak"], gone("mix", ks[g]))
        for g, k in enumerate(ks):
            hd = 4 * g + j
            x = F[TILES["sc"][hd]]
            free = (left.get(("sc", n - 1)), left["gla work", 3], left["gla pairs", 3])
            yield V, end["mix", k], free
            t = left["mix", k] = stt(x[:, 0:P * nk], B("mix", k)[:, 0:P * nk], 0.125, cst[:, m0:m0 + P * nk], ALU.mult, ALU.subtract, end["mix", k], free)
            end["max", n, hd] = reduce(mx[:, hd:hd + 1], x[:, 0:P * nk], ALU.max, t)

    def attention():
        sinks = vec[:, vat["sink"]:vat["sink"] + 8]
        av = F[TILES["av"]]
        for n in range(4):
            k0, k1 = max(0, n - 1), min(3, n + 1)
            nk = k1 - k0 + 1
            o = 352 + 32 * n
            mx, nm, es, su = (sm[:, o + 8 * i:o + 8 * i + 8] for i in range(4))
            for j in range(4):
                spawn(att_probs(n, j, k0, nk), 2)
            yield from known(*[("max", n, hd) for hd in range(8)])
            w = [end["max", n, hd] for hd in range(8)]
            yield V, w
            t = tt(mx, mx, sinks, ALU.max, w)
            t1 = ts(nm, mx, -1.0, None, ALU.mult, None, t)
            t2 = tt(es, sinks, mx, ALU.subtract, t)
            yield EXP, t1
            a = []
            for hd in range(8):
                x = F[TILES["sc"][hd]]
                a.append(act(x[:, 0:P * nk], x[:, 0:P * nk], ACT.Exp, t1, bias=nm[:, hd:hd + 1], acc=su[:, hd:hd + 1]))
            t = act(es, es, ACT.Exp, t2)
            yield V, t
            t = tt(su, su, es, ALU.add, t, a)
            t = recip(su, t)
            for hd in range(8):
                x = F[TILES["sc"][hd]]
                end["probs", hd] = ts(x[:, 0:P * nk], x[:, 0:P * nk], su[:, hd:hd + 1], None, ALU.mult, None, t)
            ob = yield from turn("out", end["probs", 3])
            for kk in range(nk):
                for g in range(2):
                    k = yield from turn("mix", end["probs", 4 * g + 3])
                    for j in range(4):
                        end["mix", k] = tr(B("mix", k)[:, W(j)], F[TILES["sc"][4 * g + j]][:, W(kk)], end["probs", 4 * g + j], gone("mix", k))
                    y = F[TILES["apt"][g]]
                    free = (left.get(("apt", g)), left["gla work", 3])
                    yield (A if g else V), end["mix", k], free
                    end["apt", g] = left["mix", k] = copy(y[:], B("mix", k)[:], end["mix", k], free, on=A if g else V)
                for g in range(2):
                    c = P * (k0 + kk) + 64 * g
                    yield T, end["apt", g]
                    end["out", ob] = left["apt", g] = mm(B("out", ob)[W(g, 64), :], av[:, c:c + 64], F[TILES["apt"][g]][:], kk == 0, kk == nk - 1,
                                                         end["apt", g], end["av"], gone("out", ob))
            left["sc", n] = end["mix", k]
            hi, lo = (x[:].rearrange("p (j t) -> p j t", j=4)[:, :, W(n)] for x in y_att_places)
            b = B("out", ob)[:].rearrange("p (j t) -> p j t", j=4)
            yield A, end["out", ob]
            a = act(hi, b, ACT.Copy, end["out", ob], left["gla pairs", 3])
            yield V, a
            end["y_att", n] = left["out", ob] = tt(lo, b, hi.bitcast(F32), ALU.subtract, a, left["rot", 4])
        left["ak"] = (end["mix", k], end["out", ob])
        end["y_att"] = [end["y_att", n] for n in range(4)]

    y_att_places = [nc.alloc_sbuf_tensor_at(f"y_att{i}", [P, 4 * S], F32R, offset=tile_at[i]) for i in TILES["y_att"]]
    y_att = [(*(x[:, W(j, S)] for x in y_att_places), "y_att") for j in range(4)]

    pieces = []
    for p in range(8):
        pieces += [(w, e, d) for w in ("w_gate", "w_upx", "w_dn")[:3 if p < 7 else 2] for d in range(KT) for e in (2 * p, 2 * p + 1)]
    pieces += [("w_dn", e, (q, v)) for q in range(4) for v in range(2) for e in (14, 15)]
    def address(x):
        return cst_at + 4 * cat["lev0"] if x == "cst" else raw_at + 4096 * x[1] if isinstance(x, tuple) else tile_at[x]
    names = EX_FIRST + EX_NEW
    at = [address(x) for x in names]
    NEX = len(EX_FIRST)
    ex = [nc.alloc_sbuf_tensor_at(f"ex{i}", [P, 1024], F32, offset=a) for i, a in enumerate(at)]
    turns = lambda xs, n: [names.index(xs[i % len(xs)]) for i in range(n)]
    where = turns(EX_FIRST, EX_SWITCH) + turns(EX_LAST, EX_END - EX_SWITCH) + turns(EX_FINAL, len(pieces) - EX_END)
    before = [max([m for m in range(n) if where[m] == where[n]] + [-1]) for n in range(len(pieces))]
    sent = [0]
    def send_piece(*waits):
        n = sent[0]
        w, e, d = pieces[n]
        if before[n] < 0 and n >= EX_END:
            waits = left["pick", 7]
        dst, src = ex[where[n]][:], io[w][e]
        if isinstance(d, tuple):
            dst, src = dst.rearrange("p (d c) -> p d c", d=4), src.rearrange("(d p) c -> p d c", p=P)[:, 4 * d[1]:4 * d[1] + 4, W(d[0], 256)]
        else:
            src = src[W(d), :]
        end["piece", n] = load(f"ex{where[n]}", dst, src, left.get(("piece", before[n])), waits)
        sent[0] += 1

    def send_pieces():
        while sent[0] < len(pieces) and before[sent[0]] < taken[0]:
            if sent[0] >= EX_END and ("pick", 7) not in left:
                return
            if sent[0] == EX_SWITCH + 12 and ("p", 0) not in end:
                if taken[0] < EX_SWITCH:
                    return
                last_loads()
            send_piece()

    merged = [pair(("merged", i), XIN[i]) for i in range(KT)]
    small = nc.alloc_sbuf_tensor_at("small", [P, 320], F32, offset=cst_at + 4 * cat["lev0"] + 4096)
    wr, aff, rank_t = small[:, 0:128], small[:, 128:192], small[:, 192:320]
    def gla_branch_of(i, k):
        x = F[TILES["g_gla"][i]]
        yield from known(("g_gla", i))
        yield V, end["dense", k], end["g_gla", i]
        end["gla branch", i] = left["dense", k] = tt(x[:], x[:], B("dense", k)[:], ALU.mult, end["dense", k], end["g_gla", i])

    def merge(i, k):
        x, y = F[TILES["g_att"][i]], F[TILES["g_gla"][i]]
        yield from known(("g_att", i), ("gla branch", i))
        yield V, end["dense", k], end["g_att", i]
        t = left["dense", k] = tt(x[:], x[:], B("dense", k)[:], ALU.mult, end["dense", k], end["g_att", i])
        t = left["g_gla", i] = tt(x[:], x[:], y[:], ALU.add, t, end["gla branch", i])
        yield from split(merged[i], x[:], None, t, left["xs3"])

    def h1_of(i, k):
        yield from add_to(i, "dense", k)
        end["h1", i] = end["x", i]
        yield from known(*[("merged", j) for j in range(8)])
        yield from add_square("h1", 66, i, F[i][:], end["x", i], [left["g_gla", j] for j in range(8)])

    def dense_2():
        yield from known(*[x[2] for x in xs3])
        kd = yield from fm("w_in_2", 3840, xs3)
        spawn(decays(kd), 2)
        yield from gqk_in(0)
        yield from gv_in(0)
        yield from gr_in(0)
        yield from gqk_in(1)
        yield from gr_in(1)
        yield from gv_in(1)
        yield from gqk_in(2)
        yield from gr_in(2)
        yield from gqk_in(3)
        yield from gr_in(3)
        yield from gate2_in("g_gla", 4896, range(0, 4), ("pt", 3))
        while ("la", 3, 0) not in left or ("la", 3, 1) not in left:
            yield False
        yield from att_in()
        yield from gate2_in("g_gla", 4896, range(4, 8), "pos", ("gla work", 3), ("gla e", 3, 0), ("gla e", 3, 1))
        for i in range(8):
            spawn(gla_branch_of(i, (yield from fm("w_branch_gla_2", 128 * i, y_gla))))
        left["y_gla"] = end["dense", uses["dense"] - 1]
        for _ in range(4):
            send_piece(left["y_gla"])
        yield from gate2_in("g_att", 3872, range(8), "y_gla")
        left["xs3"] = end["dense", uses["dense"] - 1]
        for c in range(4):
            for v, k in enumerate((yield from fm_half("w_branch_attn_2", 256 * c, y_att))):
                spawn(merge(2 * c + v, k))
        left["y_att"] = end["dense", uses["dense"] - 1]
        end["wr"] = load("wr", wr[:, 0:P], io["w_router"], left["y_att"])
        spawn(gain_router())
        spawn(logits(), 2)
        spawn(rstd_column("rcol 4", rcol4, "h1", 66), 1)
        for i in range(KT):
            k = yield from fm("w_out_2", 128 * i, merged)
            spawn(h1_of(i, k))
            for _ in range((3, 3, 3, 3, 3, 2, 1, 0)[i]):
                send_piece(left["y_att"], end["merged", 7], [left["g_gla", j] for j in range(8)])
        left["merged"] = end["dense", k]

    def attend():
        yield from known("av", "ak", *[("aq", j) for j in range(4)])
        yield from freed(("gla work", 3))
        yield from attention()

    rank = F[TILES["rank"]]
    number = rank_t[:, 64:128]
    rcol4 = sm[:, 184:188]
    def gain_router():
        yield V, end["wr"]
        for d in range(KT):
            t = end["wr"] = ts(wr[:, W(d, 16)], wr[:, W(d, 16)], vcol("norm_ffn_2", d), None, ALU.mult, None, end["wr"])

    def logits():
        yield from known(*[("merged", j) for j in range(8)])
        k = yield from turn("out")
        for i in range(KT):
            yield from known(("h1", i))
            yield T, end["h1", i], end["wr"]
            for t in range(4):
                end["out", k] = left["logits", i] = mm(B("out", k)[:, W(t, 16)], F[i][:, W(t)], wr[:, W(i, 16)], i == 0 and t == 0, i == KT - 1 and t == 3,
                                                       end["h1", i], end["wr"], gone("out", k))
        end["logits"] = k

    def turned(i, v, *waits):
        yield from known(*[("h1", 4 * v + d) for d in range(4)])
        o = yield from turn("out", [end["h1", 4 * v + d] for d in range(4)], waits)
        for d in range(4):
            end["out", o] = tr(B("out", o)[:, W(d)], F[4 * v + d][:, W(i)], [end["h1", 4 * v + x] for x in range(4)], gone("out", o), waits)
        left["turned", i, v] = end["out", o]
        yield from known("rcol 4")
        yield A, end["out", o], end["rcol 4"]
        end["hn_t", i, v] = left["out", o] = act(F[TILES["hn_t"][i][v]][:], B("out", o)[:], ACT.Identity, end["out", o], end["rcol 4"], left["merged"],
                                                 scale=rcol4[:, i:i + 1])

    def router():
        yield from known("logits", "rcol 4")
        k = end["logits"]
        a3, b3 = (x[:, 0:64].rearrange("p (i e) -> p i e", i=4) for x in (aff, B("out", k)))
        m4, s4 = sm[:, 480:484], sm[:, 484:488]
        yield V, end["rcol 4"], end["out", k]
        over = lambda x: x.unsqueeze(2).to_broadcast([P, 4, 16])
        t = left["out", k] = tt(a3, b3, over(rcol4), ALU.mult, end["rcol 4"], end["out", k], left["y_att"])
        t = reduce(m4, a3, ALU.max, t)
        t = tt(a3, a3, over(m4), ALU.subtract, t)
        yield EXP, t
        t = act(aff[:, 0:64], aff[:, 0:64], ACT.Exp, t)
        yield V, t
        t = reduce(s4, a3, ALU.add, t)
        t = recip(s4, t)
        end["aff"] = tt(a3, a3, over(s4), ALU.mult, t)
        k = yield from turn("mix", end["aff"])
        for i in range(4):
            end["mix", k] = tr(B("mix", k)[0:16, W(i)], aff[:, W(i, 16)], end["aff"], gone("mix", k))
        yield V, end["mix", k]
        t = left["mix", k] = copy(rank[0:16, :], B("mix", k)[0:16, :], end["mix", k], left["y_att"])
        t8 = sm[0:16, 488:496]
        for r in range(8):
            yield V, t
            t = V.do(lambda e: e.max(t8, rank[0:16, :]), t, cost=600)
            t = V.do(lambda e: e.match_replace(rank[0:16, :], t8, rank[0:16, :], -1.0), t, cost=600)
            spawn(turned(r % 4, r // 4, t), 3)
        yield V, t
        t = ts(rank[0:16, :], rank[0:16, :], -0.5, None, ALU.is_lt, None, t)
        k = yield from turn("mix", t)
        for i in range(4):
            end["mix", k] = tr(B("mix", k)[:, W(i, 16)], rank[0:16, W(i)], t, gone("mix", k))
        yield V, end["mix", k]
        t2 = left["mix", k] = copy(rank_t[:, 0:64], B("mix", k)[:, 0:64], end["mix", k], left["y_att"])
        k = yield from turn("mix", t2)
        mm(B("mix", k)[:, 0:64], C("le"), rank_t[:, 0:64], True, False, t2, gone("mix", k))
        for i in range(1, 4):
            end["mix", k] = mm(B("mix", k)[:, 16 * i:64], ones, rank_t[:, 0:64 - 16 * i], False, i == 3)
        yield V, end["mix", k]
        end["rank_t"] = left["mix", k] = tt(number[:, 0:64], rank_t[:, 0:64], B("mix", k)[:, 0:64], ALU.mult, end["mix", k])
        spawn(ranks(k, t2), 5)

    def ranks(k, t2):
        yield from known(("xg", 0, 3))
        k2 = yield from turn("mix", t2)
        for i in range(4):
            if i:
                yield T,
            for j in range(i + 1):
                end["mix", k2] = mm(B("mix", k2)[0:16, W(i)], rank_t[:, W(j, 16)], C("le") if j == i else ones, j == 0, j == i, t2, gone("mix", k2))
        yield V, end["mix", k2]
        end["rank"] = left["mix", k2] = tt(rank[0:16, :], rank[0:16, :], B("mix", k2)[0:16, :], ALU.mult, end["mix", k2])
        first["down"] = (left["mix", k], left["mix", k2])

    def choose(p, rank):
        pick = F[TILES["pick"]]
        out = pick[:].rearrange("p (i e s) -> p i e s", i=4, e=2)
        no = C("slots", 64).unsqueeze(1).unsqueeze(1).to_broadcast([P, 4, 2, 64])
        rk = number.rearrange("p (i e) -> p i e", i=4)[:, :, 2 * p:2 * p + 2].unsqueeze(3).to_broadcast([P, 4, 2, 64])
        yield from known("rank_t", "aff")
        if p:
            yield from freed(("pick", p - 1), *[("xg", x) for x in (p - 2,) if x >= 0])
        free = (left.get(("pick", p - 1)), left["y_att"])
        yield V, end["rank_t"], free
        end["pick", p] = tt(out, no, rk, ALU.is_equal, end["rank_t"], free)
        for v in range(2):
            spawn(chosen(p, v), rank[v])
        spawn(affinities(p), rank[1])

    def chosen(p, v):
        pick = F[TILES["pick"]]
        yield from known(*[("hn_t", i, v) for i in range(4)])
        o = yield from turn("out", end["pick", p], [end["hn_t", i, v] for i in range(4)])
        for d in range(4):
            if d:
                yield T,
            for i in range(4):
                end["out", o] = mm(B("out", o)[:, W(d)], F[TILES["hn_t"][i][v]][:, W(d)], pick[:, W(i)], i == 0, i == 3,
                                   end["hn_t", i, v], end["pick", p], gone("out", o))
        left["pick", p, v] = end["out", o]
        free = (left["merged"], left.get(("xg", p - 2)))
        on = A if v else V
        yield on, end["out", o], free
        for d in range(4):
            x, b, g = F[TILES["xg"][p % 2][v]][:, W(d)], B("out", o)[:, W(d)], vcol("norm_ffn_2", 4 * v + d)
            end["xg", p, 4 * v + d] = (act(x, b, ACT.Identity, end["out", o], free, scale=g) if on is A
                                       else ts(x, b, g, None, ALU.mult, None, end["out", o], free))
        left["out", o] = end["xg", p, 4 * v + 3]

    def affinities(p):
        pick = F[TILES["pick"]]
        yield from freed(("pick", p, 0), ("pick", p, 1))
        o = yield from turn("out", end["aff"], end["pick", p])
        for i in range(4):
            end["out", o] = mm(B("out", o)[:, 0:2], pick[:, W(i)], aff[:, 16 * i + 2 * p:16 * i + 2 * p + 2], i == 0, i == 3, end["aff"], end["pick", p], gone("out", o))
        left["pick", p] = end["out", o]
        ac = sm[:, 496 + p:497 + p]
        yield V, end["out", o]
        t = copy(ac[0:64], B("out", o)[0:64, 0:1], end["out", o])
        end["ac", p] = left["out", o] = copy(ac[64:128], B("out", o)[64:128, 1:2], t)
        yield from back(p)

    def back(p):
        yield from known("rank")
        if p:
            yield from freed(("put", p - 1))
        o = yield from turn("out", end["rank"])
        for v in range(2):
            end["out", o] = mm(B("out", o)[W(v, 64), :], ident[0:16, 2 * p + v:2 * p + v + 1].to_broadcast([16, 64]), rank[0:16, :],
                               True, True, end["rank"], gone("out", o))
        yield V, end["out", o], left.get(("put", p - 1)), left["y_att"]
        end["put", p] = left["out", o] = ts(F[TILES["put"]][:], B("out", o)[:], vcol("slot"), None, ALU.is_equal, None, end["out", o],
                                            left.get(("put", p - 1)), left["y_att"])

    def expert_mms(ring, p, w, lhs):
        ks = yield from turn(ring, n=2)
        for d in range(KT):
            x, names = lhs(d)
            yield from known(*names)
            for e in (2 * p, 2 * p + 1):
                n = taken[0]
                assert pieces[n] == (w, e, d)
                taken[0] += 1
                half = W(e % 2, 64)
                yield T, end["piece", n], [end[x] for x in names]
                for f, k in enumerate(ks):
                    end[ring, k] = left["piece", n] = mm(B(ring, k)[half, :], x[:, half], ex[where[n]][:, W(f, S)], d == 0, d == KT - 1,
                                                         end["piece", n], gone(ring, k), [end[x] for x in names])
                send_pieces()
        return ks
    taken = [0]

    def last_down(q):
        k = yield from turn("down")
        for v in range(2):
            n = taken[0]
            assert pieces[n] == ("w_dn", 14, (q, v)) and pieces[n + 1] == ("w_dn", 15, (q, v))
            taken[0] += 2
            yield from known(("ht", 7, v))
            yield T, end["piece", n], end["piece", n + 1], end["ht", 7, v]
            for d in range(4):
                for e in range(2):
                    end["down", k] = left["piece", n + e] = mm(B("down", k)[W(e, 64), 0:256], F[TILES["ht"][v]][:, W(d)][:, W(e, 64)],
                                                               ex[where[n + e]][:, W(d, 256)], v == 0 and d == 0, v == 1 and d == 3,
                                                               end["piece", n + e], gone("down", k), end["ht", 7, v])
            send_pieces()
        return k

    def last_out(q, k):
        yield from known(("ac", 7), ("put", 7))
        yield from freed(("ey", 6))
        ey = F[TILES["ey"][q // 2]][:, W(q % 2, 256)]
        yield A, end["down", k], end["ac", 7], left["ey", 6]
        end["ey", 7, q] = left["down", k] = act(ey, B("down", k)[:, 0:256], ACT.Identity, end["down", k], end["ac", 7], left["ey", 6],
                                                scale=sm[:, 503:504])
        for d in range(2):
            o = yield from turn("out", end["ey", 7, q], end["put", 7])
            end["out", o] = mm(B("out", o)[:], ey[:, W(d)], F[TILES["put"]][:], True, True, end["ey", 7, q], end["put", 7], gone("out", o))
            spawn(h2_of(2 * q + d, o))

    def expert_gate(p, f, k):
        x = F[TILES["eh"][f]]
        if p:
            yield from freed(("eh", p - 1))
        yield SIG, end["gate", k], left.get(("eh", p - 1))
        a = act(x[:], B("gate", k)[:], ACT.Sigmoid, end["gate", k], left.get(("eh", p - 1)), left["merged"])
        yield V, a
        end["silu", p, f] = left["gate", k] = tt(x[:], x[:], B("gate", k)[:], ALU.mult, a)

    def expert_hidden(p, f, k):
        x = F[TILES["eh"][f]]
        yield from known(("silu", p, f))
        yield V, end["up", k], end["silu", p, f]
        t = left["up", k] = tt(x[:], x[:], B("up", k)[:], ALU.mult, end["silu", p, f], end["up", k])
        if p:
            yield from freed(("ht", p - 1))
        o = yield from turn("out", t)
        for c in range(4):
            end["out", o] = tr(B("out", o)[:, W(c)], x[:, W(c)], t, gone("out", o))
        left["eh", p, f] = end["out", o]
        free = (left["merged"], left.get(("ht", p - 1)))
        on = A if f else V
        yield on, end["out", o], free
        end["ht", p, f] = left["out", o] = copy(F[TILES["ht"][f]][:], B("out", o)[:], end["out", o], free, on=on)

    def expert_out(p, kd):
        yield from known(("ac", p), ("put", p))
        if p == 0:
            for i in range(KT):
                left["x", i] = [left["logits", i]] + [left["turned", j, i // 4] for j in range(4)]
        if p:
            yield from freed(("ey", p - 1))
        for f in range(2):
            free = (left.get(("ey", p - 1)), left["y_att"])
            yield A, end["down", kd[f]], end["ac", p], free
            end["ey", p, f] = left["down", kd[f]] = act(F[TILES["ey"][f]][:], B("down", kd[f])[:], ACT.Identity, end["down", kd[f]], end["ac", p],
                                                        free, scale=sm[:, 496 + p:497 + p])
        for d in range(KT):
            o = yield from turn("out", end["ey", p, d // 4], end["put", p])
            end["out", o] = mm(B("out", o)[:], F[TILES["ey"][d // 4]][:, W(d % 4)], F[TILES["put"]][:], True, True,
                               end["ey", p, d // 4], end["put", p], gone("out", o))
            spawn(add_to(d, "out", o))
        left["put", p] = left["ey", p] = end["out", o]

    def experts():
        yield from known("rank_t")
        first["gate"] = first["up"] = [left["dense", uses["dense"] - n] for n in range(1, 5)]
        for p in range(8):
            if p < 7:
                spawn(choose(p + 1, (3, 3)), 3)
            xg = lambda d: (F[TILES["xg"][p % 2][d // 4]][:, W(d % 4)], [("xg", p, d)])
            ht = lambda d: (F[TILES["ht"][d // 4]][:, W(d % 4)], [("ht", p, d // 4)])
            ks = yield from expert_mms("gate", p, "w_gate", xg)
            for f in range(2):
                spawn(expert_gate(p, f, ks[f]))
            ks = yield from expert_mms("up", p, "w_upx", xg)
            left["xg", p] = end["up", ks[1]]
            for f in range(2):
                spawn(expert_hidden(p, f, ks[f]))
            yield from freed(("eh", p, 0), ("eh", p, 1))
            left["eh", p] = left["eh", p, 1]
            yield from known("rank")
            if p < 7:
                ks = yield from expert_mms("down", p, "w_dn", ht)
                left["ht", p] = end["down", ks[1]]
                spawn(expert_out(p, ks), 3)
        for q in range(4):
            spawn(last_out(q, (yield from last_down(q))))
        end["experts"] = True

    def piece_left(address):
        i = at.index(address)
        return ("piece", max(n for n in range(len(pieces)) if where[n] == i))
    def tile_left(*tiles):
        return [piece_left(tile_at[i - i % 2]) for i in tiles]
    ps = [pair(("ps", i), TILES["ps"][i]) for i in range(2)]
    xs4 = [pair(("xs4", i), TILES["xs4"][i]) for i in range(KT)]

    def last_loads():
        for i in range(2):
            end["p", i] = load(f"x{i}", F[TILES["p"][i]][:], io["pT"][W(i)], [left[x] for x in tile_left(TILES["p"][i])])
        for u in range(nunit, nunit + NRAW):
            load_unit(u, left[piece_left(raw_at + 4096 * (u % NRAW))])

    def p_in(i):
        yield from known(("p", i))
        yield from split(ps[i], F[TILES["p"][i]][:], None, end["p", i], [left[x] for x in tile_left(*TILES["ps"][i])])

    def last_units():
        yield from known(("raw", nunit))
        for u in range(nunit, len(plan)):
            free = []
            if u < nunit + NSPL:
                free = [piece_left(raw_at + 4096 * (NRAW + o + u % NSPL)) for o in (0, NSPL)]
                yield from freed(*free)
            else:
                yield from freed(("unit", u - NSPL))
            yield from split_unit(u, [left[x] for x in free])

    def pw_of(i, k):
        free = tile_left(TILES["pw"][i])
        yield from freed(*free)
        yield A, end["out", k], left[free[0]]
        end["pw", i] = left["out", k] = copy(F[TILES["pw"][i]][:], B("out", k)[:], end["out", k], left[free[0]], on=A)

    def ple():
        for g in range(2):
            u = next_unit("w", "w_ple_2", S * g)
            yield from known(("unit", u), ("ps", 0), ("ps", 1))
            for c in range(4):
                k = yield from turn("out", end["unit", u], end["ps", 0], end["ps", 1])
                o = B("out", k)[:]
                for d, (hi, lo, name) in enumerate(ps):
                    w = slice(S * d + P * c, S * d + P * c + P)
                    mmq(o, his[u % NSPL][:, w], hi, d == 0, False, end["unit", u], end[name], gone("out", k))
                    mmq(o, his[u % NSPL][:, w], lo, False, False)
                    (mmq if d == 0 else mm)(o, los[u % NSPL][:, w], hi, False, d == 1)
                end["out", k] = (T.sem, T.n)
                spawn(pw_of(4 * g + c, k))
            left["unit", u] = end["out", k]
        left["ps"] = end["out", k]

    def h2_of(i, o):
        yield from add_to(i, "out", o)
        yield from freed(*tile_left(66, 68, *TILES["xs4"][i]))
        free = [left[x] for x in tile_left(66, 68)]
        spawn(add_square("h2", 66, i, F[i][:], end["x", i], free), 4)
        yield from freed("ps")
        yield from split(xs4[i], F[i][:], vcol("norm_ple_2", i), end["x", i], [left[x] for x in tile_left(*TILES["xs4"][i])], left["ps"])
        yield from known(("sq", "h2", i))
        left["x", i] = (end["xs4", i], end["sq", "h2", i])

    def gated(i, kd):
        yield from known("rstd 5")
        k = yield from turn("z", end["dense", kd], end["rstd 5"], lane=V)
        z = RT("z", k)
        free = [left[x] for x in tile_left(70, 72)]
        q = left["dense", kd] = tt(z[:], B("dense", kd)[:], F[RSTD][:], ALU.mult, end["dense", kd], end["rstd 5"], gone("z", k), free)
        yield SIG, q
        a = act(z[:], z[:], ACT.Sigmoid, q)
        yield V, a
        q = tt(z[:], z[:], F[TILES["pw"][i]][:], ALU.mult, a, end["pw", i])
        end["h3", i] = left["z", k] = tt(F[i][:], F[i][:], z[:], ALU.add, q, end["x", i], left["x", i])
        yield from add_square("h3", 67, i, F[i][:], end["h3", i])

    def tail():
        yield from known(("silu", 7, 0), ("silu", 7, 1))
        yield from freed(*[("up", uses["up"] - n) for n in (1, 2)])
        for n in range(1, 5):
            left["dense", uses["dense"] - n] = [left[r, uses[r] - m] for r in ("gate", "up") for m in (1, 2)]
        spawn(after_down())
        spawn(rstd_row("rstd 5", RSTD, "h2", 66))
        ks = []
        for g in range(4):
            u = next_unit("t", "w_ple_gate_2", 0)
            wh, wl = his[u % NSPL], los[u % NSPL]
            for c in range(4):
                yield from known(("unit", u))
                for x in range(2):
                    hi, lo, name = xs4[2 * g + x]
                    yield from known(name)
                    if g == 0 and x == 0:
                        ks.append((yield from turn("dense", end["unit", u], end[name])))
                    else:
                        yield T, end["unit", u], end[name]
                    k = ks[c]
                    o, w = B("dense", k)[:], slice(S * x + P * c, S * x + P * c + P)
                    mmq(o, wh[:, w], hi, g == 0 and x == 0, False, gone("dense", k), end["unit", u], end[name])
                    mmq(o, wh[:, w], lo, False, False)
                    t = mm(o, wl[:, w], hi, False, g == 3 and x == 1)
                if g == 3:
                    end["dense", k] = t
                    spawn(gated(c, k))
            left["unit", u] = t
        for i in range(4, KT):
            spawn(gated(i, (yield from fm("w_ple_gate_2", 128 * i, xs4))))
        yield from rstd_row("rstd 6", RSTD1, "h3", 67)
        for i in range(KT):
            y, on = F[TILES["out"][i]], V
            yield on, end["rstd 6"]
            q = stt(y[:], F[i][:], vcol("norm_final_2", i), F[RSTD1][:], ALU.mult, ALU.mult, end["rstd 6"], end["h3", i], [left[x] for x in tile_left(TILES["out"][i])])
            left["sent", i] = D.dma(channel(f"sent{i}"), lambda e, y=y, i=i: e.dma_start(outs[W(i)], y[:]), q, cost=700)

    def after_down():
        yield from known("experts")
        yield from known(*[("ey", 7, q) for q in range(4)])
        for n in range(1, 3):
            left["mix", uses["mix"] - n] = [end["ey", 7, q] for q in range(4)]

    jobs.run(hgrn_all(), mix_dense(), mlstm_all())
    jobs.run(xattn_all(), x_dense())
    jobs.run(between(), gla_ways(0), gla_ways(1), gla_outs(), attend(), dense_2())
    for i in range(NRAW):
        send_piece(left["raw", nunit - NRAW + (i - nunit) % NRAW])
    for i in range(2 * NSPL):
        send_piece(left["merged"])
    jobs.run()
    for _ in range(NEX - sent[0]):
        send_piece(left["acc", "h1"], left["z", uses["z"] - 1], left["sq", uses["sq"] - 1],
                   left["rstd", RSTD1])
    spawn(choose(0, (2, 4)), 2)
    jobs.run(router(), experts(), last_units(), p_in(0), p_in(1), ple(), tail())
    jobs.run()
    D.wait(*[left["sent", i] for i in range(KT)])
    with nc.Block() as block:
        block.sync(lambda e: D.play(e))
        block.vector(lambda e: V.play(e))
        block.scalar(lambda e: A.play(e))
        block.gpsimd(lambda e: G.play(e))
        block.tensor(lambda e: T.play(e))



def pack(inputs):
    g = {k: np.asarray(v) for k, v in inputs.items()}
    f32 = np.float32
    w = {n: g[n][0] for n in ("w_in", "w_xkv", "w_out", "w_xq", "w_xo", "w_up", "w_down", "w_in_2", "w_branch_attn_2",
                                "w_branch_gla_2", "w_out_2", "w_ple_2", "w_ple_gate_2")}
    rows = np.concatenate([np.r_[64 * j:64 * j + 64, 256 + 64 * j:320 + 64 * j] for j in range(4)])
    w["w_branch_attn_2"] = w["w_branch_attn_2"][rows]
    plan = unit_plan()
    units = np.zeros((len(plan), P, 1024), f32)
    for u, (kind, name, k0, cols) in enumerate(plan):
        m = w[name]
        nk, nc_ = {"f": (8, 128), "t": (2, 512), "h": (4, 256), "w": (2, 512)}[kind]
        dst = units[u].reshape(P, nk, nc_)
        src = m[128 * k0:128 * (k0 + nk)].reshape(nk, P, m.shape[1])
        cols = np.asarray(cols)
        have = cols >= 0
        dst[:, :, have] = src[:, :, cols[have]].transpose(1, 0, 2)
    vat, nvc = vec_index()
    vec = np.zeros((P, nvc), f32)
    def put(name, a, off=0):
        a = np.asarray(a, dtype=f32).reshape(-1, P).T
        vec[:, vat[name] + off:vat[name] + off + a.shape[1]] = a
    for n in ("norm_mix", "norm_xattn", "norm_mem", "norm_mlp"):
        put(n, g[n][0])
    put("norm_final", g["norm_final"])
    b = g["b_in"][0]
    for n, o in (("b_q", 0), ("b_ff", 512), ("b_fb", 1024), ("b_hg", 2048), ("b_mq", 2560), ("b_mk", 3072), ("b_mo", 4096)):
        put(n, b[o:o + 512])
    for i in range(4):
        for r, o in ((i, 4608), (64 + i, 4612), (32 + i, 4616), (96 + i, 4620)):
            vec[r, vat["b_gt"]] = b[o + i]
    put("lb", g["hgrn_lb_logits"][0, 0])
    put("lb", g["hgrn_lb_logits"][1, 0], 4)
    put("hgrn_norm", g["hgrn_norm"][0])
    for j in range(5):
        put("conv_w", g["mlstm_conv_w"][0, j], 8 * j)
    put("conv_b", g["mlstm_conv_b"][0])
    put("mlstm_norm", g["mlstm_norm"][0])
    vec[:, vat["eps"]] = EPS
    for n in ("norm_mix_2", "gla_norm_2", "norm_ffn_2", "norm_ple_2"):
        put(n, g[n][0])
    put("norm_final_2", g["norm_final_2"])
    vec[:, vat["sink"]:vat["sink"] + 8] = g["attn_sink_2"][0]
    i = np.arange(P) % 64
    freq = f32(500000.0) ** (-(2 * (i % 8)).astype(f32) / f32(16))
    vec[:, vat["freq"]] = np.where(i < 16, freq, 0)
    vec[:, vat["halfpi"]] = np.pi / 2
    vec[:, vat["slot"]] = np.arange(P) % 64 + 1
    up = np.zeros((P, S), f32)
    for o, d in ((0, "fwd"), (32, "bwd")):
        up[o:o + 16] = g[f"gla_gate_up_{d}_2"][0]
        up[o + 16] = g[f"gla_gate_bias_{d}_2"][0]
    return {
        "units": units, "consts": np.concatenate(list(const_columns().values()), axis=1), "vecs": vec,
        "w_gate": g["w_exp_gate_2"][0], "w_upx": g["w_exp_up_2"][0], "w_dn": g["w_exp_down_2"][0],
        "w_router": np.ascontiguousarray(g["w_router_2"][0].reshape(8, P, 16).transpose(1, 0, 2).reshape(P, 128)),
        "pT": np.ascontiguousarray(g["p_2"][0, 0].T),
        "gla_up": up, "pos": g["positions_2"],
        "xT": np.ascontiguousarray(g["x"][0].T), "memT": np.ascontiguousarray(g["mem"][0].T), "b_in": b,
    }


def kernel(**inputs):
    import concourse.bacc as bacc
    from concourse.bass_utils import run_bass_kernel_spmd

    nc = bacc.Bacc("TRN2", target_bir_lowering=False, num_devices=1)
    arrays = pack(inputs)
    io = {k: nc.dram_tensor(k, a.shape, mybir.dt.from_np(a.dtype), kind="ExternalInput").ap() for k, a in arrays.items()}
    out = nc.dram_tensor("outT", (1024, S), F32, kind="ExternalOutput").ap()
    encoder_decoder_kernel(nc, io, out)
    r = run_bass_kernel_spmd(nc, [arrays], core_ids=[0])
    return np.ascontiguousarray(r.results[0]["outT"].T)[None]
```
